# Optimizing a Trainium2 kernel written in Bass

```python
import math
import jax
import jax.numpy as jnp
from jax import lax
import numpy as np

D_MODEL = 2048
BATCH = 1
SEQ = 1024
DEPTH = 1
DEC_BATCH = 8
DEC_SEQ = 1
PAST_LEN = 4096
PAGE_SIZE = 128

HEAD_DIM = 128
N_HEADS_TOTAL = D_MODEL // HEAD_DIM
D_MIX = N_HEADS_TOTAL * HEAD_DIM
H_A = N_HEADS_TOTAL // 2
DH_A = HEAD_DIM // 2
D_A = H_A * HEAD_DIM
H_B = N_HEADS_TOTAL - H_A
HKV_B = max(1, H_B // 4)
D_B = H_B * HEAD_DIM
D_BKV = HKV_B * HEAD_DIM
H_IDX = 4
D_IDX = 64
D_PLE = 256
TOPK_MAX = 256
ROPE_THETA = 500000.0
ROPE_FRAC = 4
RMS_EPS = 1e-6
Q_BLOCK = 128
SPLIT_SIZES = (D_A, D_A, D_A, D_A, D_B, D_BKV, D_BKV, D_B, H_IDX * D_IDX, D_IDX, H_IDX)
N_IN = sum(SPLIT_SIZES)

kernel_name = "hymba_diff_dsa_decoder_step"

def _rmsnorm(x, w):
    xf = x.astype(jnp.float32)
    y = xf * lax.rsqrt(jnp.mean(xf * xf, axis=-1, keepdims=True) + RMS_EPS)
    return (y * w.astype(jnp.float32)).astype(x.dtype)

def _rope(x, pos):
    d = x.shape[-1]
    r = d // ROPE_FRAC
    half = r // 2
    inv = ROPE_THETA ** (-(2.0 / r) * jnp.arange(half, dtype=jnp.float32))
    ang = pos.astype(jnp.float32)[:, None] * inv[None, :]
    ang = ang.reshape((pos.shape[0],) + (1,) * (x.ndim - 3) + (half,))
    cos, sin = jnp.cos(ang), jnp.sin(ang)
    xf = x.astype(jnp.float32)
    x1, x2, rest = xf[..., :half], xf[..., half:r], xf[..., r:]
    out = jnp.concatenate([x1 * cos - x2 * sin, x2 * cos + x1 * sin, rest], axis=-1)
    return out.astype(x.dtype)

def _split_cols(z):
    offs = [int(o) for o in np.cumsum(SPLIT_SIZES)[:-1]]
    return jnp.split(z, offs, axis=-1)

def _q_block(t):
    return Q_BLOCK if t % Q_BLOCK == 0 else t

def _to_blocks(a, nb, qb):
    b = a.shape[0]
    return a.reshape((b, nb, qb) + a.shape[2:]).swapaxes(0, 1)

def _from_blocks(o):
    nb, b, qb = o.shape[:3]
    return o.swapaxes(0, 1).reshape((b, nb * qb) + o.shape[3:])

def _diff_attention(q1, q2, k1, k2, v, lam, q_pos, k_pos):
    b, t = q1.shape[:2]
    qb = _q_block(t)
    nb = t // qb
    scale = 1.0 / math.sqrt(q1.shape[-1])

    def block(args):
        a1, a2, qp = args
        vis = (k_pos[None, :] <= qp[:, None])[None, None]
        s1 = jnp.einsum('bqhd,bshd->bhqs', a1, k1).astype(jnp.float32) * scale
        s2 = jnp.einsum('bqhd,bshd->bhqs', a2, k2).astype(jnp.float32) * scale
        s1 = jnp.where(vis, s1, -jnp.inf)
        s2 = jnp.where(vis, s2, -jnp.inf)
        pr = jax.nn.softmax(s1, axis=-1) - lam * jax.nn.softmax(s2, axis=-1)
        return jnp.einsum('bhqs,bshd->bqhd', pr.astype(v.dtype), v)

    out = lax.map(block, (_to_blocks(q1, nb, qb), _to_blocks(q2, nb, qb), q_pos.reshape(nb, qb)))
    return _from_blocks(out)

def _dsa_attention(q, k, v, qi, ki, wi, q_pos, k_pos, topk):
    b, t, h, d = q.shape
    hkv = k.shape[2]
    g = h // hkv
    qb = _q_block(t)
    nb = t // qb
    scale = 1.0 / math.sqrt(d)

    def block(args):
        qq, qqi, ww, qp = args
        rel = jax.nn.relu(jnp.einsum('bqhd,bsd->bqhs', qqi, ki).astype(jnp.float32))
        score = jnp.einsum('bqhs,bqh->bqs', rel, ww.astype(jnp.float32))
        vis = k_pos[None, :] <= qp[:, None]
        score = jnp.where(vis[None], score, -jnp.inf)
        _, idx = lax.top_k(score, topk)
        kg = jax.vmap(lambda kb_, ib: kb_[ib])(k, idx)
        vg = jax.vmap(lambda vb_, ib: vb_[ib])(v, idx)
        ok = k_pos[idx] <= qp[None, :, None]
        s = jnp.einsum('bqngd,bqknd->bqngk', qq.reshape(b, qb, hkv, g, d), kg).astype(jnp.float32) * scale
        s = jnp.where(ok[:, :, None, None, :], s, -jnp.inf)
        pr = jax.nn.softmax(s, axis=-1)
        o = jnp.einsum('bqngk,bqknd->bqngd', pr.astype(v.dtype), vg)
        return o.reshape(b, qb, h, d)

    out = lax.map(block, (_to_blocks(q, nb, qb), _to_blocks(qi, nb, qb),
                          _to_blocks(wi, nb, qb), q_pos.reshape(nb, qb)))
    return _from_blocks(out)

def _layer(x, p, q_pos, k_pos, past, topk, lam_init,
           pre_w, post_w, w_in, lq1, lk1, lq2, lk2, sub_w, w_out, w_pg, b_pg, w_pe):
    b, t, _ = x.shape
    h = _rmsnorm(x, pre_w)
    z = h @ w_in
    qa, ka, va, ga, qs, ks, vs, gs, qi, ki, wi = _split_cols(z)

    qa = _rope(qa.reshape(b, t, H_A, 2, DH_A), q_pos)
    ka = _rope(ka.reshape(b, t, H_A, 2, DH_A), q_pos).reshape(b, t, H_A, HEAD_DIM)
    va = va.reshape(b, t, H_A, HEAD_DIM)
    qs = _rope(qs.reshape(b, t, H_B, HEAD_DIM), q_pos)
    ks = _rope(ks.reshape(b, t, HKV_B, HEAD_DIM), q_pos)
    vs = vs.reshape(b, t, HKV_B, HEAD_DIM)
    qi = _rope(qi.reshape(b, t, H_IDX, D_IDX), q_pos)
    ki = _rope(ki, q_pos)
    new_rows = (ka, va, ks, vs, ki)

    if past is None:
        ka_all, va_all, ks_all, vs_all, ki_all = new_rows
    else:
        ka_all, va_all, ks_all, vs_all, ki_all = [
            jnp.concatenate([pr_, nr_], axis=1) for pr_, nr_ in zip(past, new_rows)]
    s_len = ka_all.shape[1]

    lam = (jnp.exp(jnp.sum(lq1.astype(jnp.float32) * lk1.astype(jnp.float32)))
           - jnp.exp(jnp.sum(lq2.astype(jnp.float32) * lk2.astype(jnp.float32))) + lam_init)
    k_split = ka_all.reshape(b, s_len, H_A, 2, DH_A)
    oa = _diff_attention(qa[..., 0, :], qa[..., 1, :], k_split[..., 0, :], k_split[..., 1, :],
                         va_all, lam, q_pos, k_pos)
    oa = _rmsnorm(oa, sub_w) * (1.0 - lam_init)
    oa = oa.reshape(b, t, D_A) * jax.nn.silu(ga)

    ob = _dsa_attention(qs, ks_all, vs_all, qi, ki_all, wi, q_pos, k_pos, topk)
    ob = ob.reshape(b, t, D_B) * jax.nn.silu(gs)

    o = jnp.concatenate([oa, ob], axis=-1) @ w_out
    x = x + _rmsnorm(o, post_w)
    x = x + jax.nn.sigmoid(x @ w_pg + b_pg) * (p @ w_pe)
    return x, new_rows

def setup_inputs(seed: int = 0) -> dict:
    key = jax.random.key(seed)
    ks = jax.random.split(key, 24)
    n_pages = PAST_LEN // PAGE_SIZE
    n_used = DEC_BATCH * n_pages
    n_pool = n_used + max(1, n_used // 4)

    def nrm(k, shape, s=1.0):
        return s * jax.random.normal(k, shape, jnp.float32)

    page_table = jax.random.permutation(ks[10], n_pool)[:n_used].reshape(DEC_BATCH, n_pages).astype(jnp.int32)
    return {
        'x_prompt': nrm(ks[0], (BATCH, SEQ, D_MODEL)),
        'x_sample': nrm(ks[1], (DEC_BATCH, DEC_SEQ, D_MODEL)),
        'p_prompt': nrm(ks[2], (DEPTH, BATCH, SEQ, D_PLE)),
        'p_sample': nrm(ks[3], (DEPTH, DEC_BATCH, DEC_SEQ, D_PLE)),
        'cache_diff_k': nrm(ks[4], (DEPTH, n_pool, PAGE_SIZE, H_A, HEAD_DIM)),
        'cache_diff_v': nrm(ks[5], (DEPTH, n_pool, PAGE_SIZE, H_A, HEAD_DIM)),
        'cache_dsa_k': nrm(ks[6], (DEPTH, n_pool, PAGE_SIZE, HKV_B, HEAD_DIM)),
        'cache_dsa_v': nrm(ks[7], (DEPTH, n_pool, PAGE_SIZE, HKV_B, HEAD_DIM)),
        'cache_idx_k': nrm(ks[8], (DEPTH, n_pool, PAGE_SIZE, D_IDX)),
        'page_table': page_table,
        'pre_norm_w': 1.0 + nrm(ks[11], (DEPTH, D_MODEL), 0.05),
        'post_norm_w': 1.0 + nrm(ks[12], (DEPTH, D_MODEL), 0.05),
        'w_in': nrm(ks[13], (DEPTH, D_MODEL, N_IN), D_MODEL ** -0.5),
        'lam_q1': nrm(ks[14], (DEPTH, DH_A), 0.1),
        'lam_k1': nrm(ks[15], (DEPTH, DH_A), 0.1),
        'lam_q2': nrm(ks[16], (DEPTH, DH_A), 0.1),
        'lam_k2': nrm(ks[17], (DEPTH, DH_A), 0.1),
        'diff_norm_w': 1.0 + nrm(ks[18], (DEPTH, HEAD_DIM), 0.05),
        'w_out': nrm(ks[19], (DEPTH, D_MIX, D_MODEL), D_MIX ** -0.5),
        'w_ple_gate': nrm(ks[20], (DEPTH, D_MODEL, D_MODEL), D_MODEL ** -0.5),
        'b_ple_gate': nrm(ks[21], (DEPTH, D_MODEL), 0.01),
        'w_ple_proj': nrm(ks[22], (DEPTH, D_PLE, D_MODEL), D_PLE ** -0.5),
    }

def reference(x_prompt, x_sample, p_prompt, p_sample, cache_diff_k, cache_diff_v, cache_dsa_k,
              cache_dsa_v, cache_idx_k, page_table, pre_norm_w, post_norm_w, w_in, lam_q1, lam_k1,
              lam_q2, lam_k2, diff_norm_w, w_out, w_ple_gate, b_ple_gate, w_ple_proj):
    t_p = x_prompt.shape[1]
    t_s = x_sample.shape[1]
    db, n_pages = page_table.shape
    past_len = n_pages * cache_diff_k.shape[2]
    pos_p = jnp.arange(t_p, dtype=jnp.int32)
    pos_s_q = past_len + jnp.arange(t_s, dtype=jnp.int32)
    pos_s_k = jnp.arange(past_len + t_s, dtype=jnp.int32)
    topk_p = min(TOPK_MAX, t_p // 4)
    topk_s = min(TOPK_MAX, (past_len + t_s) // 4)

    hp, hs = x_prompt, x_sample
    rows_p, rows_s = [], []
    for i in range(DEPTH):
        lam_init = 0.8 - 0.6 * math.exp(-0.3 * i)
        weights = (pre_norm_w[i], post_norm_w[i], w_in[i], lam_q1[i], lam_k1[i], lam_q2[i],
                   lam_k2[i], diff_norm_w[i], w_out[i], w_ple_gate[i], b_ple_gate[i], w_ple_proj[i])
        hp, new_p = _layer(hp, p_prompt[i], pos_p, pos_p, None, topk_p, lam_init, *weights)

        def gather(c):
            g = c[i, page_table]
            return g.reshape((db, past_len) + g.shape[3:])

        past = (gather(cache_diff_k), gather(cache_diff_v), gather(cache_dsa_k),
                gather(cache_dsa_v), gather(cache_idx_k))
        hs, new_s = _layer(hs, p_sample[i], pos_s_q, pos_s_k, past, topk_s, lam_init, *weights)
        rows_p.append(new_p)
        rows_s.append(new_s)

    def stack(rows, j):
        return jnp.stack([r[j] for r in rows], axis=0)

    return (hp, hs,
            stack(rows_p, 0), stack(rows_p, 1), stack(rows_p, 2), stack(rows_p, 3), stack(rows_p, 4),
            stack(rows_s, 0), stack(rows_s, 1), stack(rows_s, 2), stack(rows_s, 3), stack(rows_s, 4))


_drawn_inputs = setup_inputs


def setup_inputs(seed=0):
    import zlib

    import numpy as np

    out = dict(_drawn_inputs(seed))
    spreads = {}
    factors = {'lam_q1': 200.0, 'b_ple_gate': 43.942}
    for name, (base, spread) in spreads.items():
        noise = np.random.default_rng([zlib.crc32(name.encode()), seed]).standard_normal(out[name].shape)
        drawn = base * np.exp(spread * noise) if base else spread * noise
        out[name] = jnp.asarray(drawn.astype(out[name].dtype))
    for name, factor in factors.items():
        out[name] = (out[name] * factor).astype(out[name].dtype)
    return out
```

```python
import math
import numpy as np
import concourse.bass as bass
from concourse import mybir
from contextlib import ExitStack

F32 = mybir.dt.float32
BF16 = mybir.dt.bfloat16
I32 = mybir.dt.int32
U32 = mybir.dt.uint32
ALU = mybir.AluOpType
ACT = mybir.ActivationFunctionType
AX = mybir.AxisListType
ds = bass.ds

P = 128
D = 2048
KT = D // P
T = 1024
NT = T // P
NB = 8
PAST = 4096
NPG = PAST // P
POOL = 320
HA, HB, HKV = 8, 8, 2
HD = 128
NI = 4
DI = 64
TOPK = 256
BS = T - P
CW = 256
ROWS = 32
QA, KA, VA, GA = 0, 1024, 2048, 3072
QS, KS, VS, GS = 4096, 5120, 5376, 5632
QI, KI, WI = 6656, 6912, 6976
NIN = 6980
NEG = -1.0e30
TAKEN = -3.0e38
EPS = 1e-6
LAM_INIT = 0.8 - 0.6 * math.exp(-0.3 * 0)
SC_A = 1.0 / math.sqrt(64.0)
SC_B = 1.0 / math.sqrt(128.0)


class Chain:

    def __init__(self, eng, sem, clear=False):
        self.eng, self.sem, self.n = eng, sem, 0
        if clear:
            eng.sem_clear(sem)

    def __call__(self, ins):
        self.n += 1
        ins.then_inc(self.sem, 1)
        self.eng.wait_ge(self.sem, self.n)


def rope(link, z, tab, t1, t2, r):
    h = r // 2
    nd = len(z.shape) - 1
    cut = lambda a, lo, hi: a[tuple([slice(None)] * nd + [slice(lo, hi)])]
    cos, sin = tab
    x = cut(z, 0, r)
    link(link.eng.tensor_tensor(t1, x, cos, ALU.mult))
    link(link.eng.tensor_tensor(t2, x, sin, ALU.mult))
    link(link.eng.tensor_tensor(cut(z, 0, h), cut(t1, 0, h), cut(t2, h, r), ALU.subtract))
    link(link.eng.tensor_tensor(cut(z, h, r), cut(t1, h, r), cut(t2, 0, h), ALU.add))



def spread(ap, axis, n):
    ap = ap.unsqueeze(axis)
    shape = list(ap.shape)
    shape[axis] = n
    return ap.broadcast_to(shape)


def hymba_step(nc, x_prompt, x_sample, p_prompt, p_sample, cache_dk, cache_dv, cache_sk, cache_sv, cache_ik,
               page_table, pre_w, post_w, w_in, lam_q1, lam_k1, lam_q2, lam_k2, sub_w, w_out, w_pg, b_pg, w_pe,
               rope_a, rope_b, rope_new,
               y_prompt, y_sample, dk_p, dv_p, sk_p, sv_p, ik_p, dk_s, dv_s, sk_s, sv_s, ik_s):
    def dram(name, shape, dt=F32):
        return nc.dram_tensor(name, shape, dt, kind="Internal").ap()

    zs_d = dram("zs_d", [NB, NIN])
    snew_a_d = dram("snew_a_d", [NB, 16])
    mask_d = dram("mask_d", [NT, P, T])
    qiT_d = dram("qiT_d", [2, P, T])
    oT_d = dram("oT_d", [HA + HB, P, T])

    xp = x_prompt.rearrange("b (t p) d -> p (b t) d", p=P)
    xs = x_sample.rearrange("b s d -> (b s) d")
    win = w_in.rearrange("l (k p) n -> p (l k) n", p=P)

    ctx = ExitStack()
    with ctx:
        def sb(name, shape, dt=F32):
            return ctx.enter_context(nc.sbuf_tensor(name, shape, dt))

        held = []

        def sem(name):
            held.append(nc.alloc_semaphore(name=name))
            return held[-1]

        def end_stage():
            nc.clear_and_free_semaphores(held)
            held.clear()
            nc.all_engine_barrier()

        hT = sb("hT", [P, KT, T])
        W = sb("W", [P, 2, KT, CW])
        big = sb("big", [P, 7 * 1024])
        qk = sb("qk", [P, NT, 2 * HD])
        vg = sb("vg", [P, 2, NT, HD])
        qkT = sb("qkT", [P, 2, T])
        e12 = sb("e12", [P, 2, T])
        pT = sb("pT", [P, NT, P])
        kiT = sb("kiT", [P, T])
        bias = sb("bias", [P, (NT - 1) * BS + T], BF16)
        qb = sb("qb", [P, 1024])
        ident = sb("ident", [P, P])
        ones = sb("ones", [P, P])
        identb = sb("identb", [P, P], BF16)
        causal = sb("causal", [P, P], BF16)
        ropa = sb("ropa", [P, NT, 2, 16])
        gsT = sb("gsT", [P, 26, NB])
        si = sb("si", [P, NB, NPG + 1])
        wall = sb("wall", [P, NT, NI])
        odec = sb("odec", [P, 16, ROWS])
        lam = sb("lam", [P, 4])
        coefm = sb("coefm", [P, HA])
        small = sb("small", [P, 320])
        ptab = sb("ptab", [1, NB * NPG], I32)

        Z = [ctx.enter_context(nc.psum_tensor(f"Z{i}", [P, 512], F32)) for i in range(2)]
        S = [ctx.enter_context(nc.psum_tensor(f"S{i}", [P, T], F32)) for i in range(2)]
        TB = ctx.enter_context(nc.psum_tensor("TB", [P, 512], F32))
        DB = ctx.enter_context(nc.psum_tensor("DB", [P, 512], F32))

        hTs = pT[:, 0:4, :].rearrange("p a b -> p (a b)").rearrange("p (k r) -> p k r", r=ROWS)
        zs = big[0:NB, 0:NIN]
        xbuf = [big[:, 0:2048], big[:, 2048:4096]]
        junk = big[:, 4096:6144]
        prew = qk[:, :, :].rearrange("p a b -> p (a b)")
        lamin = kiT[:, 0:256].rearrange("p (a d) -> p a d", a=4)
        maskt = qb
        ss, rs = small[:, 0:9], small[:, 16:25]
        sel = small[:, 32:40]
        eps = small[:, 48:49]
        tmp = e12[:, 0, 0:512].rearrange("p (s n) -> p s n", s=2)
        NCH = (NIN + CW - 1) // CW
        width = lambda c: min(CW, NIN - c * CW)
        rows = lambda t: P if t < NT else NB

        s_const = sem("u_const")
        s_mask = sem("u_mask")
        s_maskout = sem("u_maskout")
        s_in = sem("u_in")
        s_x = [sem(f"u_x{i}") for i in range(2)]
        s_ss = sem("u_ss")
        s_rs = sem("u_rs")
        s_h = sem("u_h")
        s_ht = sem("u_ht")
        s_hc = sem("u_hc")
        s_pool = sem("u_pool")
        s_act = sem("u_act")
        s_lam = sem("u_lam")
        s_w = [sem(f"u_w{i}") for i in range(2)]
        s_pz = sem("u_pz")
        s_evz = sem("u_evz")
        s_ps = sem("u_ps")
        s_evs = sem("u_evs")
        s_dve = sem("u_dve")

        with nc.Block() as block:
            @block.sync
            def _(sp):
                sp.dma_start(prew, pre_w.partition_broadcast(P).rearrange("q l d -> q (l d)")).then_inc(s_in, 16)
                for t in range(NT + 1):
                    if t >= 2:
                        sp.wait_ge(s_ht, 2 * (t - 1))
                        sp.wait_ge(s_ss, t - 1)
                    src = xp[:, t, :] if t < NT else xs
                    sp.dma_start(xbuf[t % 2][0:rows(t), :], src).then_inc(s_x[t % 2], 16)
                for c in range(2):
                    sp.dma_start(W[:, c, :, :], win[:, :, c * CW:(c + 1) * CW]).then_inc(s_w[c], 16)
                with sp.Fori(1, 13) as i:
                    for s in range(2):
                        sp.wait_ge(s_pz, 2 * i + s - 1)
                        sp.dma_start(W[:, s, :, :], win[:, :, ds(2 * i * CW + s * CW, CW)]).then_inc(s_w[s], 16)
                for c in range(26, NCH):
                    sp.wait_ge(s_pz, c - 1)
                    sp.dma_start(W[:, c % 2, :, 0:width(c)], win[:, :, c * CW:c * CW + width(c)]).then_inc(s_w[c % 2], 16)

            @block.gpsimd
            def _(pool):
                link = Chain(pool, s_pool)
                pool.memset(odec[:, :, :], 0.0)
                pool.memset(hTs, 0.0)
                pool.memset(ones[:, :], 1.0)
                for a, v in ((ident, 0.0), (identb, 0.0), (causal, 0.0)):
                    pool.memset(a[:, :], v)
                pool.memset(coefm[:, :], 0.0)
                pool.memset(small[:, 40:48], 0.0)
                pool.memset(eps, EPS)
                link(pool.memset(sel, 0.0))
                for a in (ident, identb):
                    pool.affine_select(out=a[:, :], in_=a[:, :], compare_op=ALU.not_equal, fill=1.0, base=0,
                                       pattern=[[-1, P]], channel_multiplier=1)
                pool.affine_select(out=causal[:, :], in_=causal[:, :], compare_op=ALU.is_ge, fill=NEG, base=0,
                                   pattern=[[-1, P]], channel_multiplier=1)
                for g in range(4):
                    link(pool.affine_select(out=sel, in_=sel, compare_op=ALU.not_equal, fill=1.0, base=-32 * g,
                                            pattern=[[-1, NB]], channel_multiplier=1))
                for s, a in ((0, coefm[:, :]), (1, small[:, 40:48])):
                    v = a.rearrange("p (g j) -> p g j", j=2)
                    link(pool.affine_select(out=v, in_=v, compare_op=ALU.not_equal, fill=1.0, base=-s,
                                            pattern=[[-32, 4], [-2, 2]], channel_multiplier=1))
                pool.nop().then_inc(s_const, 1)
                for t in range(NT):
                    if t:
                        pool.wait_ge(s_maskout, 16 * t)
                    link(pool.memset(maskt[:, :], 0.0))
                    pool.affine_select(out=maskt[:, :], in_=maskt[:, :], compare_op=ALU.is_ge, fill=NEG, base=P * t,
                                       pattern=[[-1, T]], channel_multiplier=1).then_inc(s_mask, 1)
                    pool.wait_ge(s_mask, t + 1)
                    pool.dma_start(mask_d[t, :, :], maskt[:, :]).then_inc(s_maskout, 16)
                pool.wait_ge(s_maskout, 16 * NT)

            @block.scalar
            def _(act):
                for i, v in enumerate((lam_q1, lam_k1, lam_q2, lam_k2)):
                    act.dma_start(lamin[:, i, :], v.partition_broadcast(P).rearrange("q l d -> q (l d)")).then_inc(s_in, 16)
                act.dma_start(ptab[:, :], page_table.rearrange("b n -> (b n)").unsqueeze(0)).then_inc(s_in, 16)
                act.dma_start(ropa[:, :, :, :], rope_a.rearrange("(t p) a r -> p t a r", p=P)).then_inc(s_in, 16)
                for t in range(NT + 1):
                    act.wait_ge(s_x[t % 2], 16 * (t // 2 + 1))
                    r = rows(t)
                    if t:
                        act.wait_ge(s_ss, t)
                    act.activation(junk[0:r, :], xbuf[t % 2][0:r, :], ACT.Square, accum_out=ss[0:r, t:t + 1]).then_inc(s_ss, 1)
                    act.wait_ge(s_ss, t + 1)
                    act.wait_ge(s_const, 1)
                    act.activation(rs[0:r, t:t + 1], ss[0:r, t:t + 1], ACT.Sqrt, scale=1.0 / D, bias=eps[0:r, :]).then_inc(s_rs, 1)
                    for j in range(2):
                        act.wait_ge(s_ht, 2 * t + j + 1)
                        if t < NT:
                            act.activation(hT[:, 8 * j:8 * j + 8, t * P:(t + 1) * P],
                                           S[j][:, :].rearrange("p (k n) -> p k n", n=P), ACT.Copy).then_inc(s_hc, 1)
                        else:
                            act.activation(hTs[:, 8 * j:8 * j + 8, 0:NB],
                                           S[j][:, :].rearrange("p (k n) -> p k n", n=P)[:, :, 0:NB], ACT.Copy).then_inc(s_hc, 1)
                act.wait_ge(s_lam, 1)
                act.activation(lam[:, 2:4], lam[:, 2:4], ACT.Exp).then_inc(s_act, 1)

                def copy_partial(c, cc, w):
                    act.wait_ge(s_pz, cc + 1)
                    if c >= 2:
                        act.wait_ge(s_ps, cc - 1)
                    act.activation(tmp[:, c % 2, 0:w], Z[c % 2][:, 0:w], ACT.Copy).then_inc(s_evz, 1)
                copy_partial(0, 0, CW)
                copy_partial(1, 1, CW)
                with act.Fori(1, 13) as i:
                    for s in range(2):
                        copy_partial(2 + s, 2 * i + s, CW)
                for c in range(26, NCH):
                    copy_partial(c, c, width(c))

            @block.vector
            def _(dve):
                link = Chain(dve, s_dve)
                dve.wait_ge(s_in, 16 * 7)
                link(dve.tensor_tensor(lamin[:, 0:4:2, :], lamin[:, 0:4:2, :], lamin[:, 1:4:2, :], ALU.mult))
                link(dve.tensor_reduce(lam[:, 2:4], lamin[:, 0:4:2, :], AX.X, ALU.add))
                dve.nop().then_inc(s_lam, 1)
                for t in range(NT + 1):
                    dve.wait_ge(s_rs, t + 1)
                    r = rows(t)
                    link(dve.reciprocal(rs[0:r, t:t + 1], rs[0:r, t:t + 1]))
                    dve.scalar_tensor_tensor(out=xbuf[t % 2][0:r, :], in0=xbuf[t % 2][0:r, :], scalar=rs[0:r, t:t + 1],
                                             in1=prew[0:r, :], op0=ALU.mult, op1=ALU.mult).then_inc(s_h, 1)
                dve.wait_ge(s_act, 1)
                link(dve.tensor_tensor(lam[:, 1:2], lam[:, 3:4], lam[:, 2:3], ALU.subtract))
                link(dve.tensor_scalar(lam[:, 0:1], lam[:, 1:2], -LAM_INIT, None, ALU.add))
                dve.wait_ge(s_const, 1)
                link(dve.scalar_tensor_tensor(out=coefm[:, :], in0=small[:, 40:48], scalar=lam[:, 0:1], in1=coefm[:, :],
                                              op0=ALU.mult, op1=ALU.add))

                def take(c, cc, w):
                    dve.wait_ge(s_ps, cc + 1)
                    src = (TB, DB)[c % 2]
                    dst = zs[:, cc * CW:cc * CW + w] if isinstance(cc, int) else big[0:NB, ds(cc * CW, w)]
                    dve.tensor_copy(dst, src[0:NB, 0:w]).then_inc(s_evs, 1)
                take(0, 0, CW)
                take(1, 1, CW)
                with dve.Fori(1, 13) as i:
                    for s in range(2):
                        take(2 + s, 2 * i + s, CW)
                for c in range(26, NCH):
                    take(c, c, width(c))

            @block.tensor
            def _(pe):
                pe.wait_ge(s_const, 1)
                for t in range(NT + 1):
                    pe.wait_ge(s_h, t + 1)
                    r = rows(t)
                    for j in range(2):
                        if t:
                            pe.wait_ge(s_hc, 2 * (t - 1) + j + 1)
                        for k in range(8):
                            kk = 8 * j + k
                            mm = pe.transpose(S[j][:, k * P:k * P + r], xbuf[t % 2][0:r, kk * P:(kk + 1) * P], ident[0:r, 0:r])
                        mm.then_inc(s_ht, 1)
                pe.wait_ge(s_hc, 2 * (NT + 1))

                def add(c, cc, w):
                    pe.wait_ge(s_evz, cc + 1)
                    if c >= 2:
                        pe.wait_ge(s_evs, cc - 1)
                    pe.matmul((TB, DB)[c % 2][0:NB, 0:w], sel, tmp[:, c % 2, 0:w], start=True, stop=True).then_inc(s_ps, 1)

                def project(c, cc, w):
                    pe.wait_ge(s_w[c % 2], cc * 8 - (c % 2) * 8 + 16)
                    if c >= 2:
                        pe.wait_ge(s_evz, cc - 1)
                    for k in range(KT):
                        g = k % 4
                        mm = pe.matmul(Z[c % 2][32 * g:32 * g + 32, 0:w], hTs[:, k, :], W[:, c % 2, k, 0:w],
                                       start=(k < 4), stop=(k >= KT - 4))
                    mm.then_inc(s_pz, 1)
                project(0, 0, CW)
                project(1, 1, CW)
                add(0, 0, CW)
                project(2, 2, CW)
                add(1, 1, CW)
                project(3, 3, CW)
                add(2, 2, CW)
                with pe.Fori(2, 13) as i:
                    for s in range(2):
                        project(2 + s, 2 * i + s, CW)
                        add(3 + s, 2 * i + s - 1, CW)
                for c in range(26, NCH):
                    project(c, c, width(c))
                    add(c - 1, c - 1, CW)
                add(NCH - 1, NCH - 1, width(NCH - 1))

        end_stage()

        zg = lambda lo, n, d: zs[:, lo:lo + n * d].rearrange("p (g d) -> p g d", d=d)
        rnew = small[0:NB, 64:160].rearrange("p (a r) -> p a r", a=2)
        sna, snb, sni, rel4 = small[0:NB, 160:176], small[0:NB, 176:184], small[0:NB, 184:185], small[0:NB, 188:192]
        snew_i_d = dram("snew_i_d", [NB, 1])
        flat8 = lambda a: a[0:NB, :, :].rearrange("p a b -> p (a b)")
        gates = flat8(e12)
        prod8 = flat8(pT)
        kid = vg[:, 0, :, :]
        qi4 = qk[:, :, :].rearrange("p t (g d) -> p t g d", d=DI)

        v_in = sem("v_in")
        v_dve = sem("v_dve")
        v_rot = sem("v_rot")
        v_out = sem("v_out")
        v_eg = sem("v_eg")
        v_tr = sem("v_tr")
        v_w = [sem("v_w0"), sem("v_w1")]
        v_z = [sem("v_z0"), sem("v_z1")]
        v_zf = [sem("v_zf0"), sem("v_zf1")]
        v_ki = sem("v_ki")
        v_qt = sem("v_qt")
        v_qc = sem("v_qc")
        v_st = sem("v_st")

        with nc.Block() as block:
            @block.sync
            def _(sp):
                sp.dma_start(rnew, rope_new.unsqueeze(0).broadcast_to([NB, 2, 48])).then_inc(v_in, 16)
                sp.dma_start(W[:, 0, :, :], win[:, :, QI:KI]).then_inc(v_w[0], 16)
                sp.dma_start(W[:, 1, :, 0:NIN - KI], win[:, :, KI:NIN]).then_inc(v_w[1], 16)
                sp.wait_ge(v_rot, 1)
                sp.dma_start(zs_d, zs).then_inc(v_out, 16)
                for dst, lo, n in ((dk_s, KA, 1024), (dv_s, VA, 1024), (sk_s, KS, 256), (sv_s, VS, 256)):
                    sp.dma_start(dst.rearrange("l b s h d -> (l b s) (h d)"), zs[:, lo:lo + n]).then_inc(v_out, 16)
                sp.dma_start(ik_s.rearrange("l b s d -> (l b s) d"), zs[:, KI:KI + DI]).then_inc(v_out, 16)
                sp.wait_ge(v_rot, 2)
                sp.dma_start(snew_a_d, sna).then_inc(v_out, 16)
                sp.wait_ge(v_rot, 3)
                sp.dma_start(snew_i_d, sni).then_inc(v_out, 16)
                sp.wait_ge(v_qc, 2)
                sp.dma_start(qiT_d.rearrange("j p t -> p j t"), qkT[:, :, :]).then_inc(v_st, 16)
                sp.wait_ge(v_ki, 2)
                sp.dma_start(ik_p.rearrange("l b (t p) d -> p (l b t) d", p=P), kid[:, :, 0:DI]).then_inc(v_st, 16)
                sp.wait_ge(v_out, 16 * 8)
                sp.dma_start(si[0:1, :, NPG:NPG + 1], snew_i_d.unsqueeze(0),
                             allow_slow_non_contiguous=True).then_inc(v_st, 16)
                sp.wait_ge(v_st, 48)

            @block.vector
            def _(dve):
                link = Chain(dve, v_dve)
                dve.wait_ge(v_in, 16)
                tab = lambda n, lo, r: tuple(spread(rnew[:, a, lo:lo + r], 1, n) for a in (0, 1))
                for lo, n, d, c0 in ((QA, 32, DI, 0), (QS, 10, HD, 16), (QI, 5, DI, 0)):
                    r = d // 4
                    tt = [prod8[:, a * 512:a * 512 + n * r].rearrange("p (g r) -> p g r", r=r) for a in (0, 1)]
                    rope(link, zg(lo, n, d), tab(n, c0, r), tt[0], tt[1], r)
                link(dve.memset(si[:, :, NPG:NPG + 1], NEG))
                dve.nop().then_inc(v_rot, 1)
                pr = prod8[:, 0:1024]
                link(dve.tensor_tensor(pr, zs[:, QA:QA + 1024], zs[:, KA:KA + 1024], ALU.mult))
                link(dve.tensor_reduce(sna, pr.rearrange("p (g d) -> p g d", d=64), AX.X, ALU.add))
                dve.nop().then_inc(v_rot, 1)
                link(dve.tensor_tensor(pr.rearrange("p (n j d) -> p n j d", n=2, d=HD),
                                       zs[:, QS:QS + 1024].rearrange("p (n j d) -> p n j d", n=2, d=HD),
                                       spread(zg(KS, 2, HD), 2, 4), ALU.mult))
                link(dve.tensor_reduce(snb, pr.rearrange("p (g d) -> p g d", d=HD), AX.X, ALU.add))
                link(dve.tensor_tensor(pr[:, 0:256].rearrange("p (g d) -> p g d", d=DI), zg(QI, 4, DI),
                                       spread(zs[:, KI:KI + DI], 1, NI), ALU.mult))
                link(dve.tensor_reduce(rel4, pr[:, 0:256].rearrange("p (g d) -> p g d", d=DI), AX.X, ALU.add))
                link(dve.scalar_tensor_tensor(out=rel4, in0=rel4, scalar=0.0, in1=zs[:, WI:WI + NI], op0=ALU.max, op1=ALU.mult))
                link(dve.tensor_reduce(sni, rel4, AX.X, ALU.add))
                dve.nop().then_inc(v_rot, 1)
                dve.wait_ge(v_eg, 1)
                link(dve.tensor_scalar(gates, gates, 1.0, None, ALU.add))
                link(dve.reciprocal(gates, gates))
                link(dve.tensor_tensor(gates[:, 0:1024], gates[:, 0:1024], zs[:, GA:GA + 1024], ALU.mult))
                link(dve.tensor_tensor(gates[:, 1024:2048], gates[:, 1024:2048], zs[:, GS:GS + 1024], ALU.mult))
                dve.nop().then_inc(v_rot, 1)
                dve.wait_ge(v_tr, 1)
                link(dve.tensor_copy(gsT[:, :, :].rearrange("p a b -> p (a b)"), TB[:, 0:26 * NB]))
                dve.wait_ge(v_zf[0], 4)
                dve.wait_ge(v_zf[1], 4)
                t4 = lambda a, g: prompt_tmp[:, a * 512:a * 512 + NT * g * 16].rearrange("p (t g r) -> p t g r", g=g, r=16)
                prompt_tmp = pT[:, :, :].rearrange("p a b -> p (a b)")
                ptab4 = lambda g: tuple(spread(ropa[:, :, a, :], 2, g) for a in (0, 1))
                rope(link, qi4, ptab4(4), t4(0, 4), t4(1, 4), 16)
                dve.nop().then_inc(v_ki, 1)
                dve.wait_ge(v_zf[0], 8)
                dve.wait_ge(v_zf[1], 8)
                rope(link, kid[:, :, 0:DI], tuple(ropa[:, :, a, :] for a in (0, 1)),
                     prompt_tmp[:, 0:128].rearrange("p (t r) -> p t r", r=16),
                     prompt_tmp[:, 512:640].rearrange("p (t r) -> p t r", r=16), 16)
                link(dve.tensor_copy(kid[:, :, DI:2 * DI], kid[:, :, 0:DI]))
                dve.nop().then_inc(v_ki, 1)

            @block.scalar
            def _(act):
                act.activation(gates[:, 0:1024], zs[:, GA:GA + 1024], ACT.Exp, scale=-1.0)
                act.activation(gates[:, 1024:2048], zs[:, GS:GS + 1024], ACT.Exp, scale=-1.0).then_inc(v_eg, 1)
                for c in range(2 * NT):
                    s, t = c // NT, c % NT
                    act.wait_ge(v_z[c % 2], c // 2 + 1)
                    if s == 0:
                        act.activation(qk[:, t, :], Z[c % 2][:, 0:CW], ACT.Copy).then_inc(v_zf[c % 2], 1)
                    else:
                        act.activation(kid[:, t, 0:DI], Z[c % 2][:, 0:DI], ACT.Copy)
                        act.activation(wall[:, t, :], Z[c % 2][:, DI:DI + NI], ACT.Copy).then_inc(v_zf[c % 2], 1)
                for j in range(2):
                    act.wait_ge(v_qt, j + 1)
                    act.activation(qkT[:, j, :], S[j][:, :], ACT.Copy).then_inc(v_qc, 1)
                act.wait_ge(v_qt, 3)
                act.activation(kiT[:, :], S[0][:, :], ACT.Copy).then_inc(v_qc, 1)

            @block.tensor
            def _(pe):
                for c in range(2 * NT):
                    s, t = c // NT, c % NT
                    if t == 0:
                        pe.wait_ge(v_w[s], 16)
                    if c >= 2:
                        pe.wait_ge(v_zf[c % 2], c // 2)
                    w = CW if s == 0 else NIN - KI
                    for k in range(KT):
                        mm = pe.matmul(Z[c % 2][:, 0:w], hT[:, k, t * P:(t + 1) * P], W[:, s, k, 0:w],
                                       start=(k == 0), stop=(k == KT - 1))
                    mm.then_inc(v_z[c % 2], 1)
                    if c == 0:
                        pe.wait_ge(v_rot, 4)
                        for j in range(26):
                            src = gates[:, j * P:(j + 1) * P] if j < 16 else (
                                zs[:, QS + (j - 16) * P:QS + (j - 15) * P] if j < 24 else zs[:, VS + (j - 24) * P:VS + (j - 23) * P])
                            mm = pe.transpose(TB[:, j * NB:(j + 1) * NB], src, ident[0:NB, 0:NB])
                        mm.then_inc(v_tr, 1)
                pe.wait_ge(v_ki, 1)
                for j in range(2):
                    for t in range(NT):
                        mm = pe.transpose(S[j][:, t * P:(t + 1) * P], qk[:, t, j * P:(j + 1) * P], ident[:, :])
                    mm.then_inc(v_qt, 1)
                pe.wait_ge(v_ki, 2)
                pe.wait_ge(v_qc, 1)
                for t in range(NT):
                    mm = pe.transpose(S[0][:, t * P:(t + 1) * P], kid[:, t, :], ident[:, :])
                mm.then_inc(v_qt, 1)

        end_stage()

        ring_k = [big[:, s * 1024:(s + 1) * 1024] for s in range(4)]
        ring_v = [big[:, (4 + s) * 1024:(5 + s) * 1024] for s in range(2)] + ring_k[2:4]
        work = big[:, 6 * 1024:7 * 1024]
        pTf = pT[:, :, :].rearrange("p a b -> p (a b)")
        prods = [work, pTf]
        kib = sb("kib", [P, 2, 4, DI])
        kprod = sb("kprod", [P, 2, 4, DI])
        qib = sb("qib", [P, NI, DI])
        sc = sb("sc", [P, NPG + 1, 16])
        ex = sb("ex", [P, NPG + 1, 16])
        vnew = sb("vnew", [P, 1024])
        qit = sb("qit", [P, 2, P])
        subw = sb("subw", [P, HD])
        srel = sb("srel", [P, NPG, NI])
        mx, nmx = small[:, 192:208].rearrange("p (t j) -> p t j", j=2), small[:, 208:224].rearrange("p (t j) -> p t j", j=2)
        rsum, rrec = small[:, 224:240].rearrange("p (t j) -> p t j", j=2), small[:, 240:256].rearrange("p (t j) -> p t j", j=2)
        cc, ss8, top8, m16, es16 = small[:, 256:264], small[:, 264:272], small[:, 272:280], small[:, 288:304], small[:, 304:320]
        mm1, den, coef, dg16 = small[0:16, 64:65], small[:, 65:66], small[:, 72:80], small[0:16, 80:96]
        zero = small[:, 104:105]
        wib, wic = small[:, 96:100], small[:, 100:104]
        od = e12[:, 1, 0:256]
        z4 = qk[:, :, :].rearrange("p t (g d) -> p t g d", d=DI)
        onat = qk[:, :, 0:HD]
        v_sb, g_sb = vg[:, 0, :, :], vg[:, 1, :, :]
        sqs = kprod[:, 0, 0:2, :].rearrange("p a d -> p (a d)")
        sig = qk[:, :, HD:2 * HD]
        INDEX_AT = (12, 12, 13, 13)
        ROUNDS = (8, 3, 3, 3, 3, 3, 3, 3, 3)
        SOFTMAX_AT = (13, 14, 16)
        TURN_AT = 11
        ROPE_AT = 24
        assert sum(ROUNDS) == TOPK // 8
        F = lambda t: t if t < 4 else 2 * t - 4
        NF = F(NT)
        key_spans = lambda t: [(lo, min(lo + 512, t * P)) for lo in range(0, t * P, 512)] + [(t * P, t * P + P)]
        dkv = lambda a: a.rearrange("l n p h d -> (l n) p (h d)")
        ck, cv, ci = dkv(cache_dk), dkv(cache_dv), cache_ik.rearrange("l n p d -> (l n) p d")

        w_rdy = [sem("a_w0"), sem("a_w1")]
        w_used = [sem("a_wu0"), sem("a_wu1")]
        k_rdy = [sem(f"a_k{s}") for s in range(4)]
        k_used = [sem(f"a_ku{s}") for s in range(4)]
        v_rdy = [sem(f"a_v{s}") for s in range(4)]
        v_used = [sem(f"a_vu{s}") for s in range(4)]
        i_rdy = [sem("a_i0"), sem("a_i1")]
        i_used = [sem("a_iu0"), sem("a_iu1")]
        q_rdy = [sem("a_q0"), sem("a_q1")]
        q_free = [sem("a_qf0"), sem("a_qf1")]
        b_in = sem("a_bin")
        vn_in = sem("a_vnin")
        c_in = sem("a_cin")
        t_in = sem("a_tin")
        qt_in = sem("a_qtin")
        g_si = sem("a_gsi")
        g_ch = sem("a_gch")
        z_full = [sem("a_z0"), sem("a_z1")]
        z_free = [sem("a_zf0"), sem("a_zf1")]
        s_full = [sem("a_s0"), sem("a_s1")]
        s_free = [sem("a_sf0"), sem("a_sf1")]
        t_full, t_free = sem("a_t"), sem("a_tf")
        d_ch, a_ch = sem("a_dch"), sem("a_ach")
        d_ps = sem("a_dps")
        d_red = sem("a_dred")
        d_rot = sem("a_drot")
        d_m = sem("a_dm")
        p_m = sem("a_pm")
        d_sub = sem("a_dsub")
        a_e = sem("a_ae")
        d_es = sem("a_des")
        d_od = sem("a_dod")
        a_eg = sem("a_aeg")
        d_nm = sem("a_dnm")
        a_x = sem("a_ax")
        d_p = sem("a_dp")
        a_ss = sem("a_ass")
        a_sq = sem("a_asq")
        d_og = sem("a_dog")
        a_rl = sem("a_arl")
        p_idx = sem("a_pidx")
        d_top = sem("a_dtop")
        st_k, st_v, st_o = sem("a_stk"), sem("a_stv"), sem("a_sto")
        x_in = sem("a_xin")

        with nc.Block() as block:
            @block.sync
            def _(sp):
                for s in (*w_used, *k_used, *v_used, *i_used, *q_free, *z_free, *s_free, d_sub, p_m, g_si, p_idx, t_free, t_full,
                          st_k, st_v, st_o, d_og, a_sq):
                    sp.sem_inc(s, 1)
                sp.dma_start(subw[:, :], sub_w.partition_broadcast(P).rearrange("q l d -> q (l d)")).then_inc(x_in, 16)
                with sp.Fori(0, HA) as i:
                    sp.wait_ge(w_used[0], 1 + i)
                    for j, lo in enumerate((QA, KA)):
                        sp.dma_start(W[:, 0, :, j * HD:(j + 1) * HD], win[:, :, ds(i * HD + lo, HD)]).then_inc(w_rdy[0], 16)
                    sp.wait_ge(k_used[3], 1 + 8 * i)
                    sp.dma_start(qb[:, :], zs_d[ds(i, 1), QA:QA + 1024].broadcast_to([P, 1024])).then_inc(b_in, 16)
                    sp.wait_ge(d_sub, 1 + i)
                    if True:
                        sp.wait_ge(x_in, 17)
                    sp.dma_start(sc[0:1, NPG, :], snew_a_d[ds(i, 1), :]).then_inc(b_in, 16)
                    sp.wait_ge(g_si, 1 + i)
                    sp.dma_start(qib[:, :, :].rearrange("p h d -> p (h d)"),
                                 zs_d[ds(i, 1), QI:QI + 256].broadcast_to([P, 256])).then_inc(c_in, 16)
                    sp.dma_start(wib, zs_d[ds(i, 1), WI:WI + NI].broadcast_to([P, NI])).then_inc(c_in, 16)
                    for j in range(8):
                        if j == 4:
                            sp.wait_ge(w_used[1], 1 + i)
                            for q, lo in enumerate((VA, GA)):
                                sp.dma_start(W[:, 1, :, q * HD:(q + 1) * HD], win[:, :, ds(i * HD + lo, HD)]).then_inc(w_rdy[1], 16)
                        sp.wait_ge(i_used[j % 2], 1 + 4 * i + j // 2)
                        for s in range(4):
                            page = sp.value_load(ptab[0:1, ds(i * NPG + 4 * j + s, 1)], min_val=0, max_val=POOL - 1)
                            sp.dma_start(kib[:, j % 2, s, :], ci[ds(page, 1), :, :].rearrange("o p d -> (o p) d")).then_inc(i_rdy[j % 2], 16)
                            sp.wait_ge(k_used[s], 1 + 8 * i + j)
                            if j == 0 and s >= 2:
                                sp.wait_ge(v_used[s], 1 + 8 * i)
                            sp.dma_start(ring_k[s], ck[ds(page, 1), :, :].rearrange("o p d -> (o p) d")).then_inc(k_rdy[s], 16)
                    sp.wait_ge(p_m, 1 + 5 * i)
                    sp.dma_start(vnew[0:1, :], zs_d[ds(i, 1), VA:VA + 1024]).then_inc(vn_in, 16)
                    sp.wait_ge(p_idx, 1 + i)
                    sp.dma_start(qit[:, :, :], qiT_d[:, :, ds(i * P, P)].rearrange("j p t -> p j t")).then_inc(qt_in, 16)
                    sp.wait_ge(d_ps, (NPG - 1) * (i + 1))
                    sp.dma_start(work, mask_d[ds(i, 1), :, :].rearrange("o p t -> (o p) t")).then_inc(t_in, 16)
                    sp.wait_ge(d_rot, i + 1)
                    sp.dma_start(dk_p.rearrange("l b (t p) h d -> p (l b t) h d", p=P)[:, :, ds(i, 1), :].rearrange("p t o d -> p t (o d)"),
                                 qk[:, :, HD:2 * HD]).then_inc(st_k, 16)
                    for b in range(2):
                        sp.wait_ge(z_free[b], 1 + 12 * i + 8)
                    sp.dma_start(dv_p.rearrange("l b (t p) h d -> p (l b t) h d", p=P)[:, :, ds(i, 1), :].rearrange("p t o d -> p t (o d)"),
                                 v_sb).then_inc(st_v, 16)
                for s, lo in enumerate((KS, VS)):
                    sp.wait_ge(w_used[s], 1 + HA)
                    sp.dma_start(W[:, s, :, :], win[:, :, lo:lo + CW]).then_inc(w_rdy[s], 16)
                    sp.wait_ge(w_rdy[s], 32 * HA + 16)
                sp.wait_ge(st_k, 1 + 16 * HA)
                sp.wait_ge(st_v, 1 + 16 * HA)

            @block.gpsimd
            def _(pool):
                pool.memset(sc[:, NPG, :], NEG)
                pool.memset(den, 1.0)
                pool.memset(zero, 0.0)
                pool.memset(vnew[:, :], 0.0).then_inc(x_in, 1)
                with pool.Fori(0, HA) as i:
                    link = Chain(pool, g_ch, clear=True)
                    pool.wait_ge(c_in, 32 * i + 32)
                    pool.wait_ge(a_sq, 1 + i)
                    for u in range(8 * NI):
                        j, h = u // NI, u % NI
                        if h == 0:
                            pool.wait_ge(i_rdy[j % 2], 64 * (4 * i + j // 2 + 1))
                        pool.wait_ge(q_free[u % 2], 1 + 16 * i + u // 2)
                        mul = pool.tensor_tensor(kprod[:, u % 2, :, :], kib[:, j % 2, :, :], spread(qib[:, h, :], 1, 4), ALU.mult)
                        mul.then_inc(q_rdy[u % 2], 1)
                        if h == NI - 1:
                            pool.wait_ge(q_rdy[u % 2], 16 * i + u // 2 + 1)
                            pool.nop().then_inc(i_used[j % 2], 1)
                    for b in range(2):
                        pool.wait_ge(q_free[b], 1 + 16 * i + 16)
                    link(pool.tensor_tensor(zero, zero, zero, ALU.mult))
                    link(pool.tensor_scalar(srel[:, :, :], srel[:, :, :], 0.0, None, ALU.max))
                    link(pool.tensor_tensor(srel[:, :, :], srel[:, :, :], spread(wib, 1, NPG), ALU.mult))
                    for h in range(1, NI):
                        link(pool.tensor_tensor(srel[:, :, 0], srel[:, :, 0], srel[:, :, h], ALU.add))
                    pool.tensor_copy(si[:, ds(i, 1), 0:NPG].rearrange("p o n -> p (o n)"), srel[:, :, 0]).then_inc(g_si, 1)
                    pool.wait_ge(g_si, 1 + i + 1)
                    for v in range(NPG):
                        page = pool.value_load(ptab[0:1, ds(i * NPG + v, 1)], min_val=0, max_val=POOL - 1)
                        pool.wait_ge(v_used[v % 4], 1 + 8 * i + v // 4)
                        if v in (2, 3):
                            pool.wait_ge(k_used[v], 1 + 8 * i + 8)
                        pool.dma_start(ring_v[v % 4], cv[ds(page, 1), :, :].rearrange("o p d -> (o p) d")).then_inc(v_rdy[v % 4], 16)

            @block.scalar
            def _(act):
                with act.Fori(0, HA) as i:
                    act.wait_ge(st_k, 1 + 16 * i)
                    act.wait_ge(d_og, 1 + i)
                    for c in range(2 * NT):
                        t = c % NT
                        act.wait_ge(z_full[c % 2], 12 * i + c // 2 + 1)
                        if c == NT:
                            act.wait_ge(st_v, 1 + 16 * i)
                        if c < NT:
                            act.activation(qk[:, t, :], Z[c % 2][:, 0:CW], ACT.Copy).then_inc(z_free[c % 2], 1)
                        else:
                            act.activation(vg[:, :, t, :], Z[c % 2][:, 0:CW].rearrange("p (a d) -> p a d", d=HD), ACT.Copy).then_inc(z_free[c % 2], 1)
                        if c + 1 == TURN_AT:
                            act.wait_ge(st_o, 1 + 16 * i)
                            for j in range(2):
                                act.wait_ge(s_full[j], (12, 11)[j] * i + 1)
                                act.activation(qkT[:, j, :], S[j][:, :], ACT.Copy).then_inc(s_free[j], 1)
                        if c + 1 == SOFTMAX_AT[2]:
                            act.wait_ge(d_sub, 1 + i + 1)
                            act.activation(ex[:, :, :], ex[:, :, :], ACT.Exp, scale=SC_A).then_inc(a_e, 1)
                        for h in range(NI):
                            if INDEX_AT[h] == c + 1:
                                act.wait_ge(s_full[h % 2], (12, 11)[h % 2] * i + h // 2 + 2)
                                act.activation(S[h % 2][:, :], S[h % 2][:, :], ACT.Relu).then_inc(a_rl, 1)

                    def squares(t):
                        act.wait_ge(z_free[t % 2], 1 + 12 * i + 8 + t // 2 + 1)
                        if t:
                            act.wait_ge(a_ss, NT * i + t)
                        act.activation(sqs, onat[:, t, :], ACT.Square, accum_out=ss8[:, t:t + 1]).then_inc(a_ss, 1)

                    for t in range(NT):
                        n = (t + 1) * P
                        act.wait_ge(d_nm, NT * i + t + 1)
                        act.wait_ge(t_full, 1 + NF * i + F(t))
                        for j in range(2):
                            x = act.activation(e12[:, j, 0:n], S[j][:, 0:n], ACT.Exp, scale=SC_A, bias=nmx[:, t, j:j + 1],
                                               accum_out=rsum[:, t, j:j + 1])
                            x.then_inc(s_free[j], 1)
                        act.wait_ge(s_free[1], 1 + 11 * i + 4 + t)
                        act.nop().then_inc(a_x, 1)
                        if t == 0:
                            for b in range(2):
                                act.wait_ge(z_free[b], 1 + 12 * i + 8)
                            act.wait_ge(st_k, 1 + 16 * i + 16)
                            act.activation(sig, g_sb, ACT.Sigmoid).then_inc(a_eg, 1)
                        for f in range(F(t + 1) - F(t)):
                            act.wait_ge(t_full, 1 + NF * i + F(t) + f + 1)
                            if f == 0:
                                if t:
                                    act.wait_ge(z_full[(t - 1) % 2], 12 * i + 8 + (t - 1) // 2 + 1)
                            nb = min(4, t + 1 - 4 * f)
                            act.activation(pTf[:, 512 * f:512 * f + nb * P], TB[:, 0:nb * P], ACT.Copy).then_inc(t_free, 1)
                        if t:
                            squares(t - 1)
                    squares(NT - 1)
                    act.wait_ge(a_ss, NT * i + NT)
                    act.activation(ss8, ss8, ACT.Sqrt, scale=1.0 / HD, bias=eps).then_inc(a_sq, 1)
                    act.wait_ge(s_full[0], 12 * i + 12)
                    act.activation(qkT[:, 0, :], S[0][:, :], ACT.Copy).then_inc(s_free[0], 1)
                    act.wait_ge(s_free[0], 1 + 12 * i + 12)
                    act.dma_start(oT_d[ds(i, 1), :, :].rearrange("o p t -> (o p) t"), qkT[:, 0, :]).then_inc(st_o, 16)
                act.wait_ge(st_o, 1 + 16 * HA)

            @block.vector
            def _(dve):
                dve.wait_ge(x_in, 17)
                dve.tensor_scalar(subw[:, :], subw[:, :], 1.0 - LAM_INIT, None, ALU.mult).then_inc(x_in, 1)
                dve.wait_ge(x_in, 18)
                with dve.Fori(0, HA) as i:
                    link = Chain(dve, d_ch, clear=True)
                    dve.wait_ge(b_in, 32 * i + 32)
                    dve.wait_ge(g_si, 1 + i)

                    def page_sum(p):
                        dve.wait_ge(k_used[p % 4], 1 + 8 * i + p // 4 + 1)
                        return dve.tensor_reduce(sc[:, p, :], prods[p % 2].rearrange("p (g d) -> p g d", d=64), AX.X, ALU.add)

                    def index_sum(u):
                        j, h = u // NI, u % NI
                        dve.wait_ge(q_rdy[u % 2], 16 * i + u // 2 + 1)
                        dve.tensor_reduce(srel[:, 4 * j:4 * j + 4, h], kprod[:, u % 2, :, :], AX.X, ALU.add).then_inc(q_free[u % 2], 1)

                    for p in range(NPG):
                        dve.wait_ge(k_rdy[p % 4], 16 * (8 * i + p // 4 + 1))
                        if p >= 2:
                            dve.wait_ge(d_ps, (NPG - 1) * i + p - 1)
                        dve.tensor_tensor(prods[p % 2], ring_k[p % 4], qb[:, :], ALU.mult).then_inc(k_used[p % 4], 1)
                        if p:
                            page_sum(p - 1).then_inc(d_ps, 1)
                            index_sum(p - 1)
                        if p == ROPE_AT:
                            for b in range(2):
                                dve.wait_ge(z_free[b], 1 + 12 * i + 4)
                            rope(link, z4, tuple(spread(ropa[:, :, a, :], 2, 4) for a in (0, 1)),
                                 *[e12[:, 1, a * 512:(a + 1) * 512].rearrange("p (t g r) -> p t g r", g=4, r=16) for a in (0, 1)], 16)
                            dve.nop().then_inc(d_rot, 1)
                    index_sum(NPG - 1)
                    page_sum(NPG - 1).then_inc(d_red, 1)
                    dve.wait_ge(d_red, i + 1)
                    link(dve.tensor_reduce(m16, sc[:, :, :].rearrange("p n h -> p h n"), AX.X, ALU.max))
                    dve.nop().then_inc(d_m, 1)
                    link(dve.tensor_copy(wic, wall[:, ds(i, 1), :].rearrange("p o h -> p (o h)")))
                    dve.wait_ge(t_in, 16 * i + 16)
                    for h in range(NI):
                        dve.wait_ge(a_rl, NI * i + h + 1)
                        dve.scalar_tensor_tensor(out=work, in0=S[h % 2][:, :], scalar=wic[:, h:h + 1], in1=work,
                                                 op0=ALU.mult, op1=ALU.add).then_inc(s_free[h % 2], 1)
                        dve.wait_ge(s_free[h % 2], 1 + (12, 11)[h % 2] * i + h // 2 + 2)
                    link(dve.memset(top8, 0.0))

                    def take(rounds):
                        for r in range(rounds):
                            link(dve.max(top8, work))
                            link(dve.match_replace(out=work, in_to_replace=top8, in_values=work, imm_value=TAKEN))

                    dve.wait_ge(p_m, 1 + 5 * i + 1)
                    link(dve.tensor_reduce(mm1, DB[0:16, 256:384], AX.X, ALU.max))
                    link(dve.tensor_scalar(dg16, ident[0:16, 0:16], mm1, None, ALU.mult))
                    dve.nop().then_inc(d_m, 1)
                    take(3)
                    dve.wait_ge(p_m, 1 + 5 * i + 2)
                    dve.tensor_tensor(ex[:, :, :], sc[:, :, :], spread(DB[:, 384:400], 1, NPG + 1), ALU.subtract).then_inc(d_sub, 1)
                    take(3)
                    dve.wait_ge(a_e, i + 1)
                    dve.tensor_reduce(es16, ex[:, :, :].rearrange("p n h -> p h n"), AX.X, ALU.add).then_inc(d_es, 1)
                    take(ROUNDS[0] - 6)
                    def maxima(t):
                        n = (t + 1) * P
                        for j in range(2):
                            dve.wait_ge(s_full[j], (12, 11)[j] * i + 4 + t)
                            last = dve.tensor_reduce(mx[:, t, j:j + 1], S[j][:, 0:n], AX.X, ALU.max)
                        link(last)
                        dve.tensor_scalar(nmx[:, t, :], mx[:, t, :], -SC_A, None, ALU.mult).then_inc(d_nm, 1)

                    def natural(t):
                        dve.wait_ge(z_full[t % 2], 12 * i + 8 + t // 2 + 1)
                        dve.tensor_scalar(onat[:, t, :], Z[t % 2][:, 0:HD], rrec[:, t, 0:1], None, ALU.mult).then_inc(z_free[t % 2], 1)

                    def sample_products():
                        dve.wait_ge(d_p, NT * i + NT)
                        link(dve.memset(od, 0.0))
                        dve.wait_ge(p_m, 1 + 5 * i + 4)
                        for g in range(4):
                            last = dve.tensor_copy(od[32 * g:32 * g + 4, :], DB[32 * g:32 * g + 4, 0:256])
                        last.then_inc(d_od, 1)

                    maxima(0)
                    dve.wait_ge(p_m, 1 + 5 * i + 3)
                    for g in range(4):
                        last = dve.tensor_copy(den[32 * g:32 * g + 4, :], TB[32 * g:32 * g + 4, 0:1])
                    link(last)
                    link(dve.reciprocal(cc[:, 0:1], den))
                    link(dve.tensor_scalar(coef, coefm[:, :], cc[:, 0:1], None, ALU.mult))
                    for t in range(NT):
                        n = (t + 1) * P
                        dve.wait_ge(a_x, NT * i + t + 1)
                        link(dve.reciprocal(rrec[:, t, :], rsum[:, t, :]))
                        link(dve.scalar_tensor_tensor(out=cc[:, t:t + 1], in0=rsum[:, t, 0:1], scalar=rrec[:, t, 1:2],
                                                      in1=lam[:, 0:1], op0=ALU.mult, op1=ALU.mult))
                        dve.scalar_tensor_tensor(out=e12[:, 0, 0:n], in0=e12[:, 1, 0:n], scalar=cc[:, t:t + 1],
                                                 in1=e12[:, 0, 0:n], op0=ALU.mult, op1=ALU.add).then_inc(d_p, 1)
                        if t:
                            natural(t - 1)
                        if t == 1:
                            dve.wait_ge(a_eg, i + 1)
                            link(dve.tensor_tensor(g_sb, g_sb, sig, ALU.mult))
                        if t == 2:
                            link(dve.tensor_tensor(g_sb, g_sb, spread(subw[:, :], 1, NT), ALU.mult))
                        if t + 1 < NT:
                            take(1)
                            maxima(t + 1)
                            take(ROUNDS[t + 1] - 1)
                        else:
                            sample_products()
                            take(ROUNDS[NT])
                    natural(NT - 1)
                    for b in range(2):
                        dve.wait_ge(z_free[b], 1 + 12 * i + 12)
                    link(dve.tensor_tensor(g_sb, g_sb, onat, ALU.mult))
                    dve.wait_ge(a_sq, 1 + i + 1)
                    link(dve.reciprocal(ss8, ss8))
                    dve.tensor_tensor(g_sb, g_sb, spread(ss8, 2, HD), ALU.mult).then_inc(d_og, 1)
                    dve.wait_ge(p_m, 1 + 5 * i + 5)
                    for j in range(2):
                        last = dve.tensor_copy(odec[:, j:HA:2, ds(i, 1)].rearrange("p h o -> p (h o)"), DB[:, 408 + 4 * j:412 + 4 * j])
                    link(last)
                    dve.tensor_scalar(bias[:, ds(i * BS, T)], work, TAKEN / 2, NEG,
                                      ALU.is_gt, ALU.mult).then_inc(d_top, 1)
                    dve.wait_ge(d_top, i + 1)

            @block.tensor
            def _(pe):
                with pe.Fori(0, HA) as i:
                    def project(c):
                        s, t = c // NT, c % NT
                        if t == 0:
                            pe.wait_ge(w_rdy[s], 32 * i + 32)
                        pe.wait_ge(z_free[c % 2], 1 + 12 * i + c // 2)
                        for k in range(KT):
                            mm = pe.matmul(Z[c % 2][:, 0:CW], hT[:, k, t * P:(t + 1) * P], W[:, s, k, :],
                                           start=(k == 0), stop=(k == KT - 1))
                        mm.then_inc(z_full[c % 2], 1)
                        if t == NT - 1:
                            pe.wait_ge(z_full[c % 2], 12 * i + c // 2 + 1)
                            pe.nop().then_inc(w_used[s], 1)

                    def index(h):
                        j, r = h % 2, 64 * (h % 2)
                        if h == 0:
                            pe.wait_ge(qt_in, 16 * i + 16)
                        pe.wait_ge(s_free[j], 1 + (12, 11)[j] * i + 1 + h // 2)
                        for lo in (0, 512):
                            mm = pe.matmul(S[j][:, lo:lo + 512], qit[r:r + 64, h // 2, :], kiT[r:r + 64, lo:lo + 512], start=True, stop=True)
                        mm.then_inc(s_full[j], 1)

                    for c in range(2 * NT + 1):
                        if c == TURN_AT:
                            pe.wait_ge(d_rot, i + 1)
                            for j in range(2):
                                pe.wait_ge(s_free[j], 1 + (12, 11)[j] * i)
                                for t in range(NT):
                                    mm = pe.transpose(S[j][:, t * P:(t + 1) * P], qk[:, t, j * HD:(j + 1) * HD], ident[:, :])
                                mm.then_inc(s_full[j], 1)
                        for h in range(NI):
                            if INDEX_AT[h] == c:
                                index(h)
                        if c == SOFTMAX_AT[0]:
                            pe.wait_ge(d_m, 2 * i + 1)
                            pe.transpose(DB[0:16, 256:384], m16, ident[:, :]).then_inc(p_m, 1)
                        if c == SOFTMAX_AT[1]:
                            pe.wait_ge(d_m, 2 * i + 2)
                            pe.matmul(DB[:, 384:400], ones[0:16, :], dg16, start=True, stop=True).then_inc(p_m, 1)
                        if c == SOFTMAX_AT[2]:
                            pe.wait_ge(d_es, i + 1)
                            for g in range(4):
                                mm = pe.matmul(TB[32 * g:32 * g + 4, 0:1], es16[:, 4 * g:4 * g + 4], ones[:, 0:1], start=True, stop=True)
                            mm.then_inc(p_m, 1)
                        if c < 2 * NT:
                            project(c)
                    for j in range(2):
                        pe.wait_ge(s_full[j], (12, 11)[j] * i + 3)
                    pe.nop().then_inc(p_idx, 1)

                    def values(v):
                        if v < NPG:
                            pe.wait_ge(v_rdy[v % 4], 16 * (8 * i + v // 4 + 1))
                        else:
                            pe.wait_ge(vn_in, 16 * i + 16)
                        page = ring_v[v % 4] if v < NPG else vnew[:, :]
                        for g in range(4):
                            mm = pe.matmul(DB[32 * g:32 * g + 4, 0:256], ex[:, v, 4 * g:4 * g + 4], page[:, 256 * g:256 * g + 256],
                                           start=(v == 0), stop=(v == NPG))
                        if v < NPG:
                            mm.then_inc(v_used[v % 4], 1)
                        else:
                            mm.then_inc(p_m, 1)

                    for v in range(4):
                        values(v)
                    def scores(t):
                        n = (t + 1) * P
                        for j in range(2):
                            pe.wait_ge(s_free[j], 1 + (12, 11)[j] * i + 3 + t)
                            for lo, hi in key_spans(t):
                                pe.matmul(S[j][:, lo:hi], qkT[64 * j:64 * j + 64, 0, t * P:n], qkT[64 * j:64 * j + 64, 1, lo:hi],
                                          start=True, stop=(hi < n))
                            pe.matmul(S[j][:, t * P:n], identb[:, :], causal[:, :], start=False, stop=True).then_inc(s_full[j], 1)

                    for j in range(2):
                        pe.wait_ge(s_free[j], 1 + (12, 11)[j] * i + 3)
                    scores(0)
                    for t in range(NT):
                        if t + 1 < NT:
                            for v in range(4 * t + 4, 4 * t + 8):
                                values(v)
                            scores(t + 1)
                        else:
                            values(NPG)
                        pe.wait_ge(d_p, NT * i + t + 1)
                        for f in range(F(t + 1) - F(t)):
                            pe.wait_ge(t_free, 1 + NF * i + F(t) + f)
                            for b in range(min(4, t + 1 - 4 * f)):
                                mm = pe.transpose(TB[:, b * P:(b + 1) * P], e12[:, 0, (4 * f + b) * P:(4 * f + b + 1) * P], ident[:, :])
                            mm.then_inc(t_full, 1)
                        pe.wait_ge(z_free[t % 2], 1 + 12 * i + 8 + t // 2)
                        pe.wait_ge(t_free, 1 + NF * i + F(t + 1))
                        for b in range(t + 1):
                            mm = pe.matmul(Z[t % 2][:, 0:HD], pT[:, b, :], v_sb[:, b, :], start=(b == 0), stop=(b == t))
                        mm.then_inc(z_full[t % 2], 1)
                    pe.wait_ge(d_od, i + 1)
                    for j in range(2):
                        mm = pe.matmul(DB[:, 408 + 4 * j:412 + 4 * j], od[:, j * P:(j + 1) * P], coef[:, j:HA:2], start=True, stop=True)
                    mm.then_inc(p_m, 1)
                    pe.wait_ge(d_og, 1 + i + 1)
                    pe.wait_ge(s_free[0], 1 + 12 * i + 11)
                    for t in range(NT):
                        mm = pe.transpose(S[0][:, t * P:(t + 1) * P], g_sb[:, t, :], ident[:, :])
                    mm.then_inc(s_full[0], 1)

        end_stage()

        NS = NPG + 1
        Wf = W[:, :, :, :].rearrange("p a b c -> p (a b c)")
        kg = Wf[:, 4096:8192].rearrange("p (b f c) -> p b f c", b=NB, f=2)
        vgt = Wf[:, 0:4096].rearrange("p (b f c) -> p b f c", b=NB, f=2)
        at = [0]

        def take_big(n, dt=F32):
            words = n if dt != BF16 else n // 2
            a = big[:, at[0]:at[0] + words]
            at[0] += words
            return a if dt == F32 else a.bitcast(dt)

        cmpm, eqm, rkm, pre, tot = (take_big(NB * NS) for _ in range(5))
        reset = take_big(NB * NS)
        below = take_big(P)
        iotaj = take_big(TOPK)
        oneh = take_big(4 * TOPK, BF16).rearrange("p (s j) -> p s j", s=4)
        ids = take_big(2 * NB * NPG, BF16).rearrange("p (n q) -> p n q", q=2)
        idi, idi2 = take_big(NB * NPG, I32), take_big(NB * NPG, I32)
        ab = take_big(TOPK)[0:2, :]
        idx = take_big(2 * NB, U32)
        idxf = take_big(2 * 2 * NB).rearrange("p (f b q) -> p f b q", f=2, b=NB)
        ssb = take_big(TOPK + 8)[0:64, :]
        ptb = take_big(2 * 64).rearrange("p (f n) -> p f n", f=2)
        st_sb = take_big(128)
        d64 = take_big(64)[0:64, :]
        pbc = take_big(64)
        sqa = take_big(64)
        ktb = e12[:, :, 0:512]
        kTb = big[:, 0:2048]
        rtmpk = [big[:, 2048:2560], big[:, 2560:3072]]
        ropb = big[:, 4608:5120].rearrange("p (t a r) -> p t a r", t=NT, a=2)
        vb = big[:, 5120:7168].rearrange("p (t c) -> p t c", c=2 * HD)
        kq = qkT[:, :, :].rearrange("p a (b c) -> p (a b) c", c=2 * HD)
        assert at[0] <= 4608 - 64
        three = lambda a: a.rearrange("p (b n) -> p b n", b=NB)
        s8 = lambda lo, n=NB, dt=F32: small[:, 192 + lo:192 + lo + n].bitcast(dt) if dt != F32 else small[:, 192 + lo:192 + lo + n]
        prefix, biti, mflip, thr, acci = s8(0, dt=I32), s8(8, dt=I32), s8(16, dt=I32), s8(24, dt=I32), s8(32, dt=I32)
        bitf, cnt, need, selx, gef = s8(40), s8(48), s8(56), s8(64), s8(72)
        rmax, rsm, own, pex, subc = small[0:64, 280:281], small[0:64, 281:282], small[0:64, 282:283], small[0:64, 283:284], small[:, 284:285]
        x64 = take_big(64)[0:1, :]
        snew_b_d = dram("snew_b_d", [NB, HB])
        ska, sva = (a.rearrange("l n p h d -> (l n p) (h d)") for a in (cache_sk, cache_sv))

        b_in = sem("b_in")
        b_st = sem("b_st")
        b_cst = sem("b_cst")
        b_ch = sem("b_ch")
        b_gch = sem("b_gch")
        b_cnt = sem("b_cnt")
        b_tot = sem("b_tot")
        b_eq = sem("b_eq")
        b_pre = sem("b_pre")
        b_oh = sem("b_oh")
        b_ohu = sem("b_ohu")
        b_ab = sem("b_ab")
        b_abc = sem("b_abc")
        b_abt = sem("b_abt")
        b_idx = sem("b_idx")
        b_k, b_v = [sem(f"b_k{j}") for j in range(NB)], [sem(f"b_v{j}") for j in range(NB)]
        b_kt = sem("b_kt")
        b_ktc = sem("b_ktc")
        b_s = sem("b_s")
        b_sc = sem("b_sc")
        b_s2 = sem("b_s2")
        b_e = sem("b_e")
        b_p = sem("b_p")
        b_pt = sem("b_pt")
        b_o = sem("b_o")
        c_in = sem("c_in")
        c_z = [sem("c_z0"), sem("c_z1")]
        c_zf = [sem("c_zf0"), sem("c_zf1")]
        c_rot = sem("c_rot")
        c_t = sem("c_t")
        c_tc = sem("c_tc")
        c_st = sem("c_st")
        g_w = sem("g_w")
        g_z = [sem("g_z0"), sem("g_z1")]
        g_zf = [sem("g_zf0"), sem("g_zf1")]
        g_w1 = sem("g_w1")
        GB = [Z[0], S[1]]
        b_q = sem("b_q")
        b_qs = sem("b_qs")

        with nc.Block() as block:
            @block.sync
            def _(sp):
                sp.dma_start(idi, page_table.rearrange("b n -> (b n)").partition_broadcast(P)).then_inc(b_in, 16)
                sp.dma_start(snew_b_d, snb).then_inc(b_st, 16)
                sp.wait_ge(b_st, 16)
                sp.dma_start(own, snew_b_d.rearrange("b h -> (b h)").unsqueeze(1), allow_slow_non_contiguous=True).then_inc(b_in, 16)
                sp.dma_start(ropb, rope_b.rearrange("(t p) a r -> p t a r", p=P)).then_inc(c_in, 16)

                def weights(u, signal):
                    for q, lo in enumerate((QS, GS)):
                        sp.dma_start(W[:, u, :, q * HD:(q + 1) * HD], win[:, :, u * HD + lo:u * HD + lo + HD]).then_inc(signal, 16)

                for s in range(2):
                    sp.wait_ge(c_z[s], NT // 2)
                weights(0, g_w)
                for s in range(2):
                    sp.wait_ge(c_zf[s], NT)
                sp.dma_start(sv_p.rearrange("l b (t p) h d -> p (l b t) (h d)", p=P), vb).then_inc(c_st, 16)
                sp.wait_ge(c_rot, 1)
                sp.dma_start(sk_p.rearrange("l b (t p) h d -> p (l b t) (h d)", p=P), kq).then_inc(c_st, 16)
                sp.wait_ge(b_kt, NB)
                weights(1, g_w1)
                sp.wait_ge(c_st, 32)
                sp.wait_ge(g_w1, 32)

            @block.gpsimd
            def _(pool):
                link = Chain(pool, b_gch)
                pool.iota(iotaj, pattern=[[1, TOPK]], base=0, channel_multiplier=0, allow_small_or_imprecise_dtypes=True)
                pool.iota(idi2, pattern=[[0, NB * NPG]], base=0, channel_multiplier=1)
                link(pool.memset(reset, 1.0))
                link(pool.memset(three(reset)[:, :, 0:1], 0.0))
                link(pool.memset(below, 1.0))
                pool.affine_select(out=below, in_=below, compare_op=ALU.is_gt, fill=0.0, base=0, pattern=[[1, P]],
                                   channel_multiplier=-1).then_inc(b_cst, 1)
                for b in range(NB):
                    if b == 0:
                        pool.wait_ge(b_idx, 1)
                        for s in range(2):
                            pool.wait_ge(c_z[s], NT)
                            pool.wait_ge(g_z[s], NT // 2)
                    for f in range(2):
                        on = bass.IndirectOffsetOnAxis(ap=idx[:, f * NB + b:f * NB + b + 1], axis=0)
                        pool.indirect_dma_start(out=kg[:, b, f, :], out_offset=None, in_=ska, in_offset=on,
                                                bounds_check=POOL * P - 1, oob_is_err=False).then_inc(b_k[b], 16)
                        pool.indirect_dma_start(out=vgt[:, b, f, :], out_offset=None, in_=sva, in_offset=on,
                                                bounds_check=POOL * P - 1, oob_is_err=False).then_inc(b_v[b], 16)

            @block.vector
            def _(dve):
                link = Chain(dve, b_ch)
                siv = si[:, :, :]
                dve.wait_ge(b_cst, 1)
                dve.wait_ge(b_in, 32)
                link(dve.tensor_scalar(idi, idi, P, None, ALU.mult))
                link(dve.tensor_tensor(idi2, idi, idi2, ALU.add))
                link(dve.tensor_scalar(idi, idi2, 255, None, ALU.bitwise_and))
                link(dve.tensor_scalar(idi2, idi2, 8, None, ALU.logical_shift_right))
                link(dve.tensor_copy(ids[:, :, 0], idi2))
                link(dve.tensor_copy(ids[:, :, 1], idi))

                def count(n, thr_ap, op):
                    link(dve.tensor_tensor(three(cmpm), siv, thr_ap, op))
                    dve.tensor_reduce(cnt, three(cmpm), AX.X, ALU.add).then_inc(b_cnt, 1)
                    dve.wait_ge(b_tot, n)

                link(dve.memset(thr, 0))
                wide = lambda a: spread(a, 2, NS)
                count(1, wide(thr.bitcast(F32)), ALU.is_ge)
                link(dve.tensor_scalar(mflip, TB[:, 0:NB], TOPK - 0.5, -1.0, ALU.is_lt, ALU.mult))
                link(dve.memset(prefix, 0))
                link(dve.memset(bitf, float(2 ** 30)))
                link(dve.tensor_copy(biti, bitf))
                with dve.Fori(0, 31) as r:
                    inner = Chain(dve, b_ch, clear=True)
                    inner(dve.tensor_tensor(thr, prefix, biti, ALU.bitwise_or))
                    inner(dve.tensor_tensor(thr, thr, mflip, ALU.bitwise_xor))
                    inner(dve.tensor_tensor(three(cmpm), siv, wide(thr.bitcast(F32)), ALU.is_ge))
                    dve.tensor_reduce(cnt, three(cmpm), AX.X, ALU.add).then_inc(b_cnt, 1)
                    dve.wait_ge(b_tot, r + 2)
                    inner(dve.scalar_tensor_tensor(out=acci, in0=TB[:, 0:NB], scalar=TOPK - 0.5, in1=bitf, op0=ALU.is_ge, op1=ALU.mult))
                    inner(dve.tensor_tensor(prefix, prefix, acci, ALU.bitwise_or))
                    inner(dve.tensor_scalar(bitf, bitf, 0.5, None, ALU.mult))
                    inner(dve.tensor_copy(biti, bitf))
                link = Chain(dve, b_ch, clear=True)
                link(dve.tensor_tensor(thr, prefix, mflip, ALU.bitwise_xor))
                tf = wide(thr.bitcast(F32))
                link(dve.tensor_tensor(three(eqm), siv, tf, ALU.is_equal))
                link(dve.tensor_tensor(three(cmpm), siv, tf, ALU.is_gt))
                dve.tensor_reduce(cnt, three(cmpm), AX.X, ALU.add).then_inc(b_cnt, 1)
                dve.wait_ge(b_tot, 33)
                link(dve.tensor_scalar(need, TB[:, 0:NB], -1.0, float(TOPK), ALU.mult, ALU.add))
                dve.nop().then_inc(b_eq, 1)

                def ranks(n, m):
                    dve.wait_ge(b_pre, n)
                    link(dve.tensor_copy(pre, S[0][:, 512:512 + NB * NS]))
                    link(dve.tensor_tensor_scan(out=tot, data0=reset, data1=pre, initial=0.0, op0=ALU.mult, op1=ALU.add))
                    link(dve.tensor_tensor(tot, tot, pre, ALU.subtract))
                    link(dve.tensor_tensor(pre, tot, S[0][:, 0:NB * NS], ALU.add))

                ranks(1, eqm)
                link(dve.tensor_tensor(three(rkm), three(pre), wide(need), ALU.is_lt))
                link(dve.tensor_tensor(eqm, eqm, rkm, ALU.mult))
                link(dve.tensor_tensor(eqm, eqm, cmpm, ALU.add))
                dve.nop().then_inc(b_eq, 1)
                link(dve.tensor_copy(x64.rearrange("p (b h) -> p b h", h=HB), spread(three(eqm)[0:1, :, NPG], 2, HB)))
                dve.nop().then_inc(b_eq, 1)
                ranks(2, eqm)
                link(dve.scalar_tensor_tensor(out=rkm, in0=pre, scalar=1.0, in1=eqm, op0=ALU.add, op1=ALU.mult))
                link(dve.tensor_scalar(rkm, rkm, -1.0, None, ALU.add))
                rk3 = three(rkm)
                for b in range(NB):
                    for n in range(NPG):
                        u = b * NPG + n
                        if u >= 4:
                            dve.wait_ge(b_ohu, u - 3)
                        dve.tensor_scalar(oneh[:, u % 4, :], iotaj, rk3[:, b, n:n + 1], None, ALU.is_equal).then_inc(b_oh, 1)
                dve.wait_ge(b_abt, NB)
                link(dve.tensor_copy(idxf.rearrange("p f b q -> p (f b q)"), TB[:, 0:32]))
                link(dve.scalar_tensor_tensor(out=idx.rearrange("p (f b) -> p f b", f=2), in0=idxf[:, :, :, 0], scalar=256.0,
                                              in1=idxf[:, :, :, 1], op0=ALU.mult, op1=ALU.add))
                dve.nop().then_inc(b_idx, 1)
                dve.wait_ge(c_in, 16)
                for s in range(2):
                    dve.wait_ge(c_zf[s], NT // 2)
                rope(link, kq.rearrange("p t (g d) -> p t g d", g=2), tuple(spread(ropb[:, :, a, :], 2, 2) for a in (0, 1)),
                     *[a.rearrange("p (t g r) -> p t g r", g=2, r=32) for a in rtmpk], 32)
                dve.nop().then_inc(c_rot, 1)
                dve.wait_ge(b_s, NB)
                dve.tensor_copy(st_sb, Z[0][:, 0:128]).then_inc(b_sc, 1)
                dve.wait_ge(b_s2, 1)
                link(dve.tensor_copy(ssb[:, 0:TOPK], Z[1][0:64, 0:TOPK]))
                link(dve.tensor_copy(pex, Z[1][0:64, 256:257]))
                link(dve.scalar_tensor_tensor(out=ssb[:, 255:256], in0=pex, scalar=NEG, in1=ssb[:, 255:256], op0=ALU.mult, op1=ALU.add))
                link(dve.tensor_scalar(rmax, pex, -NEG, NEG, ALU.mult, ALU.add))
                link(dve.tensor_tensor(ssb[:, 256:257], own, rmax, ALU.add))
                link(dve.tensor_reduce(rmax, ssb[:, 0:257], AX.X, ALU.max))
                link(dve.tensor_scalar(rmax, rmax, -SC_B, None, ALU.mult))
                dve.nop().then_inc(b_sc, 1)
                dve.wait_ge(b_e, 1)
                link(dve.reciprocal(rsm, rsm))
                link(dve.tensor_scalar(ssb[:, 0:257], ssb[:, 0:257], rsm, None, ALU.mult))
                link(dve.tensor_scalar(d64, ident[0:64, 0:64], ssb[:, 256:257], None, ALU.mult))
                dve.nop().then_inc(b_p, 1)
                dve.wait_ge(b_pt, 1)
                link(dve.tensor_copy(ptb.rearrange("p f n -> p (f n)"), TB[:, 0:128]))
                link(dve.tensor_copy(pbc, TB[:, 128:192]))
                dve.nop().then_inc(b_p, 1)
                dve.wait_ge(b_o, 1)
                for n in range(HKV):
                    ob = odec[:, HA + 4 * n:HA + 4 * n + 4, 0:NB].rearrange("p h b -> p b h")
                    pb = pbc.rearrange("p (b h) -> p b h", h=HB)[:, :, 4 * n:4 * n + 4]
                    link(dve.tensor_tensor(ob, pb, spread(gsT[:, 24 + n, :], 2, 4), ALU.mult))
                    link(dve.tensor_tensor(ob, ob, Z[0][:, 0:64].rearrange("p (b h) -> p b h", h=HB)[:, :, 4 * n:4 * n + 4], ALU.add))
                link(dve.tensor_tensor(odec[:, HA:16, 0:NB], odec[:, HA:16, 0:NB], gsT[:, HA:16, :], ALU.mult))
                oa = odec[:, 0:HA, 0:NB]
                sq3 = sqa.rearrange("p (h b) -> p h b", h=HA)
                link(dve.tensor_tensor(sq3, oa, oa, ALU.mult))
                dve.nop().then_inc(b_q, 1)
                dve.wait_ge(b_qs, 1)
                link(dve.tensor_copy(subc, TB[:, 300:301]))
                link(dve.reciprocal(sqa, sqa))
                link(dve.scalar_tensor_tensor(out=oa, in0=oa, scalar=subc, in1=sq3, op0=ALU.mult, op1=ALU.mult))
                link(dve.tensor_tensor(oa, oa, gsT[:, 0:HA, :], ALU.mult))

            @block.scalar
            def _(act):
                for c in range(2 * NT):
                    act.wait_ge(c_z[c % 2], c // 2 + 1)
                    dst = kq[:, c % NT, :] if c < NT else vb[:, c % NT, :]
                    act.activation(dst, Z[c % 2][:, 0:CW], ACT.Copy).then_inc(c_zf[c % 2], 1)
                for b in range(NB):
                    act.wait_ge(b_ab, b + 1)
                    act.activation(ab, DB[0:2, 0:TOPK] if b % 2 == 0 else Z[1][0:2, 0:TOPK], ACT.Copy).then_inc(b_abc, 1)
                    act.wait_ge(g_z[b % 2], b // 2 + 1)
                    act.activation(qk[:, b, 0:HD], GB[b % 2][:, 0:HD], ACT.Copy)
                    act.activation(vg[:, 0, b, :], GB[b % 2][:, HD:CW], ACT.Copy).then_inc(g_zf[b % 2], 1)
                    if b + 1 < NB:
                        act.wait_ge(b_abt, b + 1)
                for n in range(HKV):
                    act.wait_ge(c_t, n + 1)
                    act.activation(kTb[:, n * T:(n + 1) * T], S[n][:, :], ACT.Copy).then_inc(c_tc, 1)
                for b in range(NB):
                    act.wait_ge(b_kt, b + 1)
                    if b >= 2:
                        act.wait_ge(b_s, b - 1)
                    act.activation(ktb[:, b % 2, :], S[b % 2][:, 0:512], ACT.Copy).then_inc(b_ktc, 1)
                act.wait_ge(b_sc, 2)
                act.activation(ssb[:, 0:257], ssb[:, 0:257], ACT.Exp, scale=SC_B, bias=rmax, accum_out=rsm).then_inc(b_e, 1)
                act.wait_ge(b_o, 2)
                act.activation(sqa, TB[:, 192:256], ACT.Sqrt, scale=1.0 / HD, bias=eps).then_inc(b_qs, 1)

            @block.tensor
            def _(pe):
                def half_tile(c, f):
                    if f == 0 and c >= 2:
                        pe.wait_ge(c_zf[c % 2], c // 2)
                    for k in range(8 * f, 8 * f + 8):
                        mm = pe.matmul(Z[c % 2][:, 0:CW], hT[:, k, (c % NT) * P:(c % NT + 1) * P], W[:, c // NT, k, :],
                                       start=(k == 0), stop=(k == KT - 1))
                    if f:
                        mm.then_inc(c_z[c % 2], 1)

                for n in range(33):
                    pe.wait_ge(b_cnt, n + 1)
                    pe.matmul(TB[:, 0:NB], ones[:, :], cnt, start=True, stop=True).then_inc(b_tot, 1)
                    if n < 4 * NT:
                        half_tile(n // 2, n % 2)
                for n in range(2):
                    pe.wait_ge(b_eq, n + 1)
                    pe.matmul(S[0][:, 0:NB * NS], below, eqm, start=True, stop=True)
                    pe.matmul(S[0][:, 512:512 + NB * NS], ones[:, :], eqm, start=True, stop=True).then_inc(b_pre, 1)
                pe.wait_ge(g_w, 32)
                for s in range(2):
                    pe.wait_ge(c_zf[s], NT)
                for b in range(NB):
                    dst = DB if b % 2 == 0 else Z[1]
                    if b >= 2:
                        pe.wait_ge(g_zf[b % 2], b // 2)
                    for n in range(NPG):
                        u = b * NPG + n
                        pe.wait_ge(b_oh, u + 1)
                        mm = pe.matmul(dst[0:2, 0:TOPK], ids[:, u, :], oneh[:, u % 4, :], start=(n == 0), stop=(n == NPG - 1))
                        mm.then_inc(b_ohu, 1)
                        if n % 2 == 0:
                            k = n // 2
                            mm = pe.matmul(GB[b % 2][:, 0:CW], hT[:, k, b * P:(b + 1) * P], W[:, 0, k, :], start=(k == 0), stop=(k == KT - 1))
                            if k == KT - 1:
                                mm.then_inc(g_z[b % 2], 1)
                    pe.wait_ge(b_ohu, (b + 1) * NPG)
                    pe.nop().then_inc(b_ab, 1)
                    pe.wait_ge(b_abc, b + 1)
                    for f in range(2):
                        mm = pe.transpose(TB[:, 2 * (f * NB + b):2 * (f * NB + b) + 2], ab[:, f * P:(f + 1) * P], ident[0:2, 0:2])
                    mm.then_inc(b_abt, 1)

                def row_scores(b):
                    pe.wait_ge(b_ktc, b + 1)
                    for f in range(2):
                        for n in range(HKV):
                            mm = pe.matmul(Z[0][:, f * 64 + b * HB + 4 * n:f * 64 + b * HB + 4 * n + 4],
                                           ktb[:, b % 2, (2 * f + n) * P:(2 * f + n + 1) * P],
                                           gsT[:, 16 + 4 * n:20 + 4 * n, b], start=True, stop=True)
                    mm.then_inc(b_s, 1)

                pe.wait_ge(c_rot, 1)
                for s in range(2):
                    pe.wait_ge(g_zf[s], NT // 2)
                for n in range(HKV):
                    for t in range(NT):
                        mm = pe.transpose(S[n][:, t * P:(t + 1) * P], kq[:, t, n * HD:(n + 1) * HD], ident[:, :])
                    mm.then_inc(c_t, 1)
                for b in range(NB):
                    pe.wait_ge(b_k[b], 32)
                    if b < 2:
                        pe.wait_ge(c_tc, b + 1)
                    if b >= 2:
                        pe.wait_ge(b_ktc, b - 1)
                    for f in range(2):
                        for n in range(HKV):
                            mm = pe.transpose(S[b % 2][:, (2 * f + n) * P:(2 * f + n + 1) * P], kg[:, b, f, n * HD:(n + 1) * HD], ident[:, :])
                    mm.then_inc(b_kt, 1)
                    if b:
                        row_scores(b - 1)
                row_scores(NB - 1)
                pe.wait_ge(b_sc, 1)
                for f in range(2):
                    pe.transpose(Z[1][0:64, f * P:(f + 1) * P], st_sb[:, f * 64:(f + 1) * 64], ident[:, :])
                pe.wait_ge(b_eq, 3)
                pe.matmul(Z[1][0:64, 256:257], x64, ones[0:1, 0:1], start=True, stop=True).then_inc(b_s2, 1)
                pe.wait_ge(b_p, 1)
                for f in range(2):
                    pe.transpose(TB[:, f * 64:(f + 1) * 64], ssb[:, f * P:(f + 1) * P], ident[0:64, 0:64])
                pe.matmul(TB[:, 128:192], ones[0:64, :], d64, start=True, stop=True).then_inc(b_pt, 1)
                pe.wait_ge(b_p, 2)
                for b in range(NB):
                    pe.wait_ge(b_v[b], 32)
                    for n in range(HKV):
                        for f in range(2):
                            mm = pe.matmul(Z[0][:, b * HB + 4 * n:b * HB + 4 * n + 4], vgt[:, b, f, n * HD:(n + 1) * HD],
                                           ptb[:, f, b * HB + 4 * n:b * HB + 4 * n + 4], start=(f == 0), stop=(f == 1))
                mm.then_inc(b_o, 1)
                pe.wait_ge(b_q, 1)
                pe.transpose(TB[:, 300:428], subw[:, :], ident[:, :])
                pe.matmul(TB[:, 192:256], ones[:, :], sqa, start=True, stop=True).then_inc(b_o, 1)

        end_stage()

        sigb = big[:, 2048:3072].rearrange("p (t d) -> p t d", d=HD)
        rtmp = [big[:, 3072:3328], big[:, 3328:3584]]
        PB = [Z[0], DB]
        oTs = qb
        FB = F(NT) + 2
        h_w = [sem("h_w0"), sem("h_w1")]
        h_wu = [sem("h_wu0"), sem("h_wu1")]
        h_z = [sem("h_z0"), sem("h_z1")]
        h_zf = [sem("h_zf0"), sem("h_zf1")]
        h_rot = sem("h_rot")
        h_s = [sem("h_s0"), sem("h_s1")]
        h_sf = [sem("h_sf0"), sem("h_sf1")]
        h_t, h_tf = sem("h_t"), sem("h_tf")
        h_nm = sem("h_nm")
        h_x = sem("h_x")
        h_pv = sem("h_pv")
        h_o = sem("h_o")
        h_eg = sem("h_eg")
        h_sil = sem("h_sil")
        h_st = sem("h_st")
        h_ch = sem("h_ch")

        with nc.Block() as block:
            @block.sync
            def _(sp):
                for s in (*h_wu, *h_zf, *h_sf, h_t, h_tf, h_o, h_pv, h_sil, h_st):
                    sp.sem_inc(s, 1)
                for s in range(2):
                    sp.sem_inc(h_z[s], NT // 2)
                    sp.sem_inc(h_zf[s], NT // 2)
                    sp.sem_inc(h_w[s], 32)
                sp.sem_inc(h_wu[0], 1)
                def weights(m, u):
                    sp.wait_ge(h_wu[u], 1 + m)
                    for q, lo in enumerate((QS, GS)):
                        sp.dma_start(W[:, u, :, q * HD:(q + 1) * HD], win[:, :, ds(m * 2 * HD + u * HD + lo, HD)]).then_inc(h_w[u], 16)
                with sp.Fori(1, HB // 2) as m:
                    weights(m, 0)
                    weights(m, 1)

            @block.tensor
            def _(pe):
                def project(m, u, t):
                    H = 2 * m + u
                    if t == 0:
                        pe.wait_ge(h_w[u], 32 * m + 32)
                    pe.wait_ge(h_zf[t % 2], 1 + 4 * H + t // 2)
                    for k in range(KT):
                        mm = pe.matmul(PB[t % 2][:, 0:CW], hT[:, k, t * P:(t + 1) * P], W[:, u, k, :], start=(k == 0), stop=(k == KT - 1))
                    mm.then_inc(h_z[t % 2], 1)
                    if t == NT - 1:
                        pe.wait_ge(h_z[t % 2], 4 * H + 4)
                        pe.nop().then_inc(h_wu[u], 1)

                def queries(m, u):
                    H = 2 * m + u
                    pe.wait_ge(h_rot, H + 1)
                    pe.wait_ge(h_sf[1], 1 + 5 * H)
                    for t in range(NT):
                        mm = pe.transpose(S[1][:, t * P:(t + 1) * P], qk[:, t, u * HD:(u + 1) * HD], ident[:, :])
                    mm.then_inc(h_s[1], 1)

                def scores(m, u, t):
                    H, n = 2 * m + u, (t + 1) * P
                    j = t % 2
                    if t == 0:
                        pe.wait_ge(h_sf[1], 1 + 5 * H + 1)
                    pe.wait_ge(h_sf[j], 1 + (4 * H + t // 2 if j == 0 else 5 * H + 1 + t // 2))
                    for lo, hi in key_spans(t):
                        own = hi == n
                        pe.matmul(S[j][:, lo:hi], qkT[:, u, t * P:n], kTb[:, ds((m // 2) * T + lo, hi - lo)], start=True, stop=False)
                        mm = pe.matmul(S[j][:, lo:hi], identb[:, :], bias[:, t * BS + lo:t * BS + hi], start=False, stop=not own)
                        if own:
                            mm = pe.matmul(S[j][:, lo:hi], identb[:, :], causal[:, :], start=False, stop=True)
                    mm.then_inc(h_s[j], 1)

                def head(m, u, last):
                    H = 2 * m + u
                    m1, u1 = (m, 1) if u == 0 else (m + 1, 0)
                    for t in range(NT):
                        if not last:
                            project(m1, u1, t)
                        if t + 1 < NT:
                            scores(m, u, t + 1)
                        pe.wait_ge(h_x, NT * H + t + 1)
                        for f in range(F(t + 1) - F(t)):
                            pe.wait_ge(h_tf, 1 + FB * H + F(t) + f)
                            for b in range(min(4, t + 1 - 4 * f)):
                                mm = pe.transpose(TB[:, b * P:(b + 1) * P], e12[:, t % 2, (4 * f + b) * P:(4 * f + b + 1) * P], ident[:, :])
                            mm.then_inc(h_t, 1)
                        pe.wait_ge(h_tf, 1 + FB * H + F(t + 1))
                        pe.wait_ge(h_o, 1 + NT * H + t)
                        for b in range(t + 1):
                            mm = pe.matmul(Z[1][:, 0:HD], pT[:, b, :], vb[:, b, ds((m // 2) * HD, HD)], start=(b == 0), stop=(b == t))
                        mm.then_inc(h_pv, 1)
                    if not last:
                        queries(m1, u1)
                        scores(m1, u1, 0)
                    pe.wait_ge(h_o, 1 + NT * H + NT)
                    for f in range(2):
                        pe.wait_ge(h_tf, 1 + FB * H + F(NT) + f)
                        for b in range(4):
                            mm = pe.transpose(TB[:, b * P:(b + 1) * P], vg[:, u, 4 * f + b, :], ident[:, :])
                        mm.then_inc(h_t, 1)

                queries(0, 0)
                scores(0, 0, 0)
                with pe.Fori(0, HB // 2 - 1) as m:
                    head(m, 0, False)
                    head(m, 1, False)
                head(HB // 2 - 1, 0, False)
                head(HB // 2 - 1, 1, True)

            @block.scalar
            def _(act):
                def take(m, u, t):
                    act.wait_ge(h_z[t % 2], 4 * (2 * m + u) + t // 2 + 1)
                    act.activation(qk[:, t, u * HD:(u + 1) * HD], PB[t % 2][:, 0:HD], ACT.Copy)
                    act.activation(vg[:, u, t, :], PB[t % 2][:, HD:CW], ACT.Copy).then_inc(h_zf[t % 2], 1)

                def ready(m, u):
                    H = 2 * m + u
                    for b in range(2):
                        act.wait_ge(h_zf[b], 1 + 4 * H + 4)
                    act.wait_ge(h_sil, 1 + H)
                    act.activation(sigb, vg[:, u, :, :], ACT.Exp, scale=-1.0).then_inc(h_eg, 1)
                    act.wait_ge(h_s[1], 5 * H + 1)
                    act.activation(qkT[:, u, :], S[1][:, :], ACT.Copy).then_inc(h_sf[1], 1)

                def head(m, u, last):
                    H = 2 * m + u
                    m1, u1 = (m, 1) if u == 0 else (m + 1, 0)
                    for t in range(NT):
                        n, j = (t + 1) * P, t % 2
                        act.wait_ge(h_nm, NT * H + t + 1)
                        act.wait_ge(h_t, 1 + FB * H + (F(t - 1) if t else 0))
                        act.activation(e12[:, j, 0:n], S[j][:, 0:n], ACT.Exp, scale=SC_B, bias=nmx[:, t, 0:1],
                                       accum_out=rsum[:, t, 0:1]).then_inc(h_x, 1)
                        act.wait_ge(h_x, NT * H + t + 1)
                        act.nop().then_inc(h_sf[j], 1)
                        if not last:
                            take(m1, u1, t)
                        for f in range(F(t + 1) - F(t)):
                            act.wait_ge(h_t, 1 + FB * H + F(t) + f + 1)
                            if f == 0:
                                act.wait_ge(h_pv, 1 + NT * H + t)
                            nb = min(4, t + 1 - 4 * f)
                            act.activation(pTf[:, 512 * f:512 * f + nb * P], TB[:, 0:nb * P], ACT.Copy).then_inc(h_tf, 1)
                    if not last:
                        ready(m1, u1)
                    act.wait_ge(h_st, 1 + 16 * H)
                    for f in range(2):
                        act.wait_ge(h_t, 1 + FB * H + F(NT) + f + 1)
                        act.activation(oTs[:, 512 * f:512 * f + 512], TB[:, :], ACT.Copy).then_inc(h_tf, 1)
                    act.wait_ge(h_tf, 1 + FB * H + FB)
                    act.dma_start(oT_d[ds(H + HA, 1) if not isinstance(H, int) else slice(H + HA, H + HA + 1), :, :].rearrange("o p t -> (o p) t"),
                                  oTs[:, :]).then_inc(h_st, 16)

                ready(0, 0)
                with act.Fori(0, HB // 2 - 1) as m:
                    head(m, 0, False)
                    head(m, 1, False)
                head(HB // 2 - 1, 0, False)
                head(HB // 2 - 1, 1, True)
                act.wait_ge(h_st, 1 + 16 * HB)

            @block.vector
            def _(dve):
                def rotate(link, m, u):
                    H = 2 * m + u
                    for b in range(2):
                        dve.wait_ge(h_zf[b], 1 + 4 * H + 4)
                    rope(link, qk[:, :, u * HD:(u + 1) * HD], tuple(ropb[:, :, a, :] for a in (0, 1)),
                         *[a.rearrange("p (t r) -> p t r", r=32) for a in rtmp], 32)
                    dve.nop().then_inc(h_rot, 1)

                def maximum(link, m, u, t):
                    H, j = 2 * m + u, t % 2
                    dve.wait_ge(h_s[j], (4 * H + t // 2 + 1) if j == 0 else (5 * H + 2 + t // 2))
                    link(dve.tensor_reduce(mx[:, t, 0:1], S[j][:, 0:(t + 1) * P], AX.X, ALU.max))
                    dve.tensor_scalar(nmx[:, t, 0:1], mx[:, t, 0:1], -SC_B, None, ALU.mult).then_inc(h_nm, 1)

                def head(m, u, last):
                    H = 2 * m + u
                    m1, u1 = (m, 1) if u == 0 else (m + 1, 0)
                    link = Chain(dve, h_ch, clear=True)
                    g = vg[:, u, :, :]
                    dve.wait_ge(h_eg, H + 1)
                    link(dve.tensor_scalar(sigb, sigb, 1.0, None, ALU.add))
                    link(dve.reciprocal(sigb, sigb))
                    link(dve.tensor_tensor(g, g, sigb, ALU.mult))
                    dve.nop().then_inc(h_sil, 1)
                    maximum(link, m, u, 0)
                    for t in range(NT):
                        dve.wait_ge(h_x, NT * H + t + 1)
                        link(dve.reciprocal(rrec[:, t, 0:1], rsum[:, t, 0:1]))
                        if t + 1 < NT:
                            maximum(link, m, u, t + 1)
                        elif not last:
                            rotate(link, m1, u1)
                        dve.wait_ge(h_pv, 1 + NT * H + t + 1)
                        dve.scalar_tensor_tensor(out=g[:, t, :], in0=Z[1][:, 0:HD], scalar=rrec[:, t, 0:1], in1=g[:, t, :],
                                                 op0=ALU.mult, op1=ALU.mult).then_inc(h_o, 1)

                link = Chain(dve, h_ch)
                rotate(link, 0, 0)
                with dve.Fori(0, HB // 2 - 1) as m:
                    head(m, 0, False)
                    head(m, 1, False)
                head(HB // 2 - 1, 0, False)
                head(HB // 2 - 1, 1, True)

        end_stage()

        NCO = D // CW
        biasf = bias[:, :].bitcast(F32)
        bf, qkf, vgf = big, qk[:, :, :].rearrange("p a b -> p (a b)"), vg[:, :, :, :].rearrange("p a b c -> p (a b c)")
        qkTf, e12f = qkT[:, :, :].rearrange("p a b -> p (a b)"), e12[:, :, :].rearrange("p a b -> p (a b)")
        wide_t = [bf[:, 0:2048], bf[:, 2048:4096], bf[:, 4096:6144], qkf, vgf, qkTf, e12f, biasf[:, 0:2048]]
        rows = lambda t: P if t < NT else NB

        def ohalf(t, hh):
            if t < NT:
                return wide_t[t][:, 1024 * hh:1024 * hh + 1024]
            return (qb[0:NB, :], vnew[0:NB, :])[hh]

        ochunk = lambda t, c: ohalf(t, c // 4)[:, (c % 4) * CW:(c % 4) * CW + CW]
        vec = [bf[:, 6144:7168], biasf[:, 2048:3072]]
        xst = [pTf, kiT[:, :]]
        wpe = [sc[:, :, :].rearrange("p a b -> p (a b)")[:, 0:512].rearrange("p (k n) -> p k n", k=2),
               ex[:, :, :].rearrange("p a b -> p (a b)")[:, 0:512].rearrange("p (k n) -> p k n", k=2)]
        kibf = kib[:, :, :, :].rearrange("p a b c -> p (a b c)")
        sg = [kibf[:, 0:256], kibf[:, 256:512]]
        part = [qib[:, :, :].rearrange("p a b -> p (a b)"), qit[:, :, :].rearrange("p a b -> p (a b)")]
        pin2 = [biasf[:, 3072:3328], biasf[:, 3328:3584]]
        psT = small[:, 160:176].rearrange("p (k b) -> p k b", k=2)
        ss2 = small[:, 192:210].rearrange("p (t j) -> p t j", j=2)
        rs9 = small[:, 212:221]
        wo, wg, wp = (a.rearrange("l (k p) n -> p (l k) n", p=P) for a in (w_out, w_pg, w_pe))
        pp = p_prompt.rearrange("l b (t p) d -> p (l b t) d", p=P)
        ps = p_sample.rearrange("l b s d -> (l b s) d")
        yp = y_prompt.rearrange("b (t p) d -> p (b t) d", p=P)
        ys = y_sample.rearrange("b s d -> (b s) d")

        o_h = sem("o_h")
        o_w = [sem("o_w0"), sem("o_w1")]
        o_wu = [sem("o_wu0"), sem("o_wu1")]
        o_z = [sem("o_z0"), sem("o_z1")]
        o_zf = [sem("o_zf0"), sem("o_zf1")]
        o_pz, o_pc, o_ps, o_pf = sem("o_pz"), sem("o_pc"), sem("o_ps"), sem("o_pf")
        o_vec = sem("o_vec")
        o_vec2 = sem("o_vec2")
        o_x = [sem("o_x0"), sem("o_x1")]
        o_xu = [sem("o_xu0"), sem("o_xu1")]
        o_ch, o_ach = sem("o_ch"), sem("o_ach")
        o_rsq = sem("o_rsq")
        o_rs = sem("o_rs")
        o_xm = sem("o_xm")
        o_t, o_tf = sem("o_t"), sem("o_tf")
        o_p = sem("o_p")
        o_pt, o_ptf = sem("o_pt"), sem("o_ptf")
        e_w = [sem("e_w0"), sem("e_w1")]
        e_wu = [sem("e_wu0"), sem("e_wu1")]
        e_z = [sem("e_z0"), sem("e_z1")]
        e_a = sem("e_a")
        e_s = sem("e_s")
        e_f = [sem("e_f0"), sem("e_f1")]
        e_st = sem("e_st")

        with nc.Block() as block:
            @block.sync
            def _(sp):
                for s in (*o_zf, o_pc, o_pf, *e_wu, *e_f):
                    sp.sem_inc(s, 1)
                for c in range(2):
                    sp.dma_start(W[:, c, :, :], wo[:, :, c * CW:(c + 1) * CW]).then_inc(o_w[c], 16)
                    for k in range(8 * c, 8 * c + 8, 4):
                        sp.dma_start(hT[:, k:k + 4, :], oT_d[k:k + 4, :, :].rearrange("k p t -> p k t")).then_inc(o_h, 16)
                for hh in range(2):
                    sp.dma_start(vec[hh], post_w[0:1, 1024 * hh:1024 * hh + 1024].broadcast_to([P, 1024])).then_inc(o_vec, 16)
                with sp.Fori(1, NCO // 2) as i:
                    for s in range(2):
                        sp.wait_ge(o_wu[s], i)
                        sp.dma_start(W[:, s, :, :], wo[:, :, ds(i * 2 * CW + s * CW, CW)]).then_inc(o_w[s], 16)
                for t in range(NT + 1):
                    for hh in range(2):
                        if t:
                            sp.wait_ge(o_xu[hh], t)
                        src = xp[:, t, 1024 * hh:1024 * hh + 1024] if t < NT else xs[:, 1024 * hh:1024 * hh + 1024]
                        sp.dma_start(xst[hh][0:rows(t), :], src).then_inc(o_x[hh], 16)
                for hh in range(2):
                    sp.wait_ge(o_xu[hh], NT + 1)
                    sp.dma_start(vec[hh], b_pg[0:1, 1024 * hh:1024 * hh + 1024].broadcast_to([P, 1024])).then_inc(o_vec2, 16)
                with sp.Fori(0, NCO // 2) as i:
                    for s in range(2):
                        sp.wait_ge(e_wu[s], 1 + i)
                        sp.dma_start(W[:, s, :, :], wg[:, :, ds(i * 2 * CW + s * CW, CW)]).then_inc(e_w[s], 16)
                        sp.dma_start(wpe[s], wp[:, :, ds(i * 2 * CW + s * CW, CW)]).then_inc(e_w[s], 16)
                for t in range(NT + 1):
                    sp.wait_ge(e_f[(7 * 9 + t) % 2], 1 + (7 * 9 + t) // 2 + 1)
                    for hh in range(2):
                        dst = yp[:, t, 1024 * hh:1024 * hh + 1024] if t < NT else ys[:, 1024 * hh:1024 * hh + 1024]
                        sp.dma_start(dst, ohalf(t, hh)).then_inc(e_st, 16)
                sp.wait_ge(e_st, 32 * (NT + 1))

            @block.gpsimd
            def _(pool):
                for t in range(NT + 1):
                    if t >= 2:
                        pool.wait_ge(o_pt, t - 1)
                    pool.dma_start(pin2[t % 2][0:rows(t), :], pp[:, t, :] if t < NT else ps).then_inc(o_p, 16)
                    pool.wait_ge(o_p, 16 * t + 16)

            @block.tensor
            def _(pe):
                def chunk(i, s):
                    pe.wait_ge(o_w[s], 16 * i + 16)
                    for t in range(NT):
                        pe.wait_ge(o_zf[t % 2], 1 + 8 * i + 4 * s + t // 2)
                        for k in range(KT):
                            mm = pe.matmul(Z[t % 2][:, 0:CW], hT[:, k, t * P:(t + 1) * P], W[:, s, k, :], start=(k == 0), stop=(k == KT - 1))
                        mm.then_inc(o_z[t % 2], 1)
                    pe.wait_ge(o_pc, 1 + 2 * i + s)
                    for k in range(KT):
                        g = k % 4
                        mm = pe.matmul(TB[32 * g:32 * g + 32, 0:CW], odec[:, k, :], W[:, s, k, :], start=(k < 4), stop=(k >= KT - 4))
                    mm.then_inc(o_pz, 1)
                    pe.wait_ge(o_pz, 2 * i + s + 1)
                    pe.nop().then_inc(o_wu[s], 1)
                    pe.wait_ge(o_pc, 1 + 2 * i + s + 1)
                    pe.wait_ge(o_pf, 1 + 2 * i + s)
                    pe.matmul(DB[0:NB, 0:CW], sel, part[0], start=True, stop=True).then_inc(o_ps, 1)

                pe.wait_ge(o_h, 64)
                with pe.Fori(0, NCO // 2) as i:
                    chunk(i, 0)
                    chunk(i, 1)
                for t in range(NT + 1):
                    r = rows(t)
                    for hh in range(2):
                        pe.wait_ge(o_xm, 2 * t + hh + 1)
                        if t:
                            pe.wait_ge(o_tf, 2 * (t - 1) + hh + 1)
                        for k in range(8):
                            mm = pe.transpose(S[hh][:, k * P:k * P + r], ohalf(t, hh)[:, k * P:(k + 1) * P], ident[0:r, 0:r])
                        mm.then_inc(o_t, 1)
                for t in range(NT + 1):
                    r = rows(t)
                    pe.wait_ge(o_p, 16 * t + 16)
                    if t:
                        pe.wait_ge(o_ptf, t)
                    for k in range(2):
                        mm = pe.transpose(TB[:, k * P:k * P + r], pin2[t % 2][0:r, k * P:(k + 1) * P], ident[0:r, 0:r])
                    mm.then_inc(o_pt, 1)
                pe.wait_ge(o_tf, 2 * (NT + 1))
                pe.wait_ge(o_ptf, NT + 1)

                def gate(i, s):
                    pe.wait_ge(e_w[s], 32 * i + 32)
                    for t in range(NT + 1):
                        v = 9 * s + t
                        b = v % 2
                        pe.wait_ge(e_f[b], 1 + 9 * i + v // 2)
                        if t < NT:
                            for k in range(KT):
                                pe.matmul(Z[b][:, 0:CW], hT[:, k, t * P:(t + 1) * P], W[:, s, k, :], start=(k == 0), stop=(k == KT - 1))
                        else:
                            pe.wait_ge(o_pc, 1 + NCO + 2 * i + s)
                            for k in range(KT):
                                g = k % 4
                                mm = pe.matmul(S[0][32 * g:32 * g + 32, 0:CW], odec[:, k, :], W[:, s, k, :], start=(k < 4), stop=(k >= KT - 4))
                            mm.then_inc(o_pz, 1)
                            pe.wait_ge(o_pc, 1 + NCO + 2 * i + s + 1)
                            pe.matmul(Z[b][0:NB, 0:CW], sel, part[0], start=True, stop=True)
                        for k in range(2):
                            lhs = xst[k][:, t * P:(t + 1) * P] if t < NT else psT[:, k, :]
                            mm = pe.matmul((TB, DB)[b][0:rows(t), 0:CW], lhs, wpe[s][:, k, :], start=(k == 0), stop=(k == 1))
                        mm.then_inc(e_z[b], 1)
                    pe.wait_ge(e_z[b], 9 * i + (9 * s + NT) // 2 + 1)
                    pe.nop().then_inc(e_wu[s], 1)

                with pe.Fori(0, NCO // 2) as i:
                    gate(i, 0)
                    gate(i, 1)

            @block.scalar
            def _(act):
                def take(c):
                    for t in range(NT):
                        act.wait_ge(o_z[t % 2], 4 * c + t // 2 + 1)
                        act.activation(ochunk(t, c), Z[t % 2][:, 0:CW], ACT.Copy).then_inc(o_zf[t % 2], 1)
                    act.wait_ge(o_pz, c + 1)
                    if c:
                        act.wait_ge(o_ps, c)
                    act.activation(part[0], TB[:, 0:CW], ACT.Copy).then_inc(o_pc, 1)
                    act.wait_ge(o_ps, c + 1)
                    act.activation(ochunk(NT, c), DB[0:NB, 0:CW], ACT.Copy).then_inc(o_pf, 1)
                def turn(t):
                    for hh in range(2):
                        act.wait_ge(o_t, 2 * t + hh + 1)
                        src = S[hh][:, :].rearrange("p (k n) -> p k n", n=P)
                        if t < NT:
                            act.activation(hT[:, 8 * hh:8 * hh + 8, t * P:(t + 1) * P], src, ACT.Copy).then_inc(o_tf, 1)
                        else:
                            act.activation(odec[:, 8 * hh:8 * hh + 8, 0:NB], src[:, :, 0:NB], ACT.Copy).then_inc(o_tf, 1)

                for c in range(NCO):
                    take(c)
                for b in range(2):
                    act.wait_ge(o_zf[b], 1 + 4 * NCO)
                act.wait_ge(o_pf, 1 + NCO)
                for t in range(NT + 1):
                    r = rows(t)
                    for hh in range(2):
                        if t:
                            act.wait_ge(o_ach, 2 * t + hh - 1)
                        act.activation(S[hh][0:r, :], ohalf(t, hh), ACT.Square, accum_out=ss2[0:r, t, hh:hh + 1]).then_inc(o_ach, 1)
                for t in range(NT + 1):
                    r = rows(t)
                    act.wait_ge(o_rsq, t + 1)
                    act.activation(rs9[0:r, t:t + 1], rs9[0:r, t:t + 1], ACT.Sqrt, scale=1.0 / D, bias=eps[0:r, :]).then_inc(o_rs, 1)
                    if t:
                        turn(t - 1)
                turn(NT)
                for t in range(NT + 1):
                    act.wait_ge(o_pt, t + 1)
                    r = rows(t)
                    if t == 0:
                        for hh in range(2):
                            act.wait_ge(o_xu[hh], NT + 1)
                    if t < NT:
                        act.activation(xst[0][:, t * P:(t + 1) * P], TB[:, 0:P], ACT.Copy)
                        act.activation(xst[1][:, t * P:(t + 1) * P], TB[:, P:2 * P], ACT.Copy).then_inc(o_ptf, 1)
                    else:
                        act.activation(psT[:, :, :], TB[:, 0:2 * P].rearrange("p (k n) -> p k n", k=2)[:, :, 0:NB], ACT.Copy).then_inc(o_ptf, 1)
                with act.Fori(0, NCO // 2) as i:
                    for s in range(2):
                        for t in range(NT + 1):
                            v = 9 * s + t
                            if t == NT:
                                act.wait_ge(o_pz, NCO + 2 * i + s + 1)
                                act.activation(part[0], S[0][:, 0:CW], ACT.Copy).then_inc(o_pc, 1)
                            act.wait_ge(e_a, 18 * i + v + 1)
                            act.activation(sg[v % 2][0:rows(t), :], sg[v % 2][0:rows(t), :], ACT.Sigmoid).then_inc(e_s, 1)

            @block.vector
            def _(dve):
                link = Chain(dve, o_ch)
                dve.wait_ge(o_vec, 32)
                for t in range(NT + 1):
                    r = rows(t)
                    dve.wait_ge(o_ach, 2 * t + 2)
                    dve.tensor_tensor(rs9[0:r, t:t + 1], ss2[0:r, t, 0:1], ss2[0:r, t, 1:2], ALU.add).then_inc(o_rsq, 1)
                for t in range(NT + 1):
                    r = rows(t)
                    dve.wait_ge(o_rs, t + 1)
                    link(dve.reciprocal(rs9[0:r, t:t + 1], rs9[0:r, t:t + 1]))
                    for hh in range(2):
                        link(dve.scalar_tensor_tensor(out=ohalf(t, hh), in0=ohalf(t, hh), scalar=rs9[0:r, t:t + 1], in1=vec[hh][0:r, :],
                                                      op0=ALU.mult, op1=ALU.mult))
                        dve.wait_ge(o_x[hh], 16 * t + 16)
                        link(dve.tensor_tensor(ohalf(t, hh), ohalf(t, hh), xst[hh][0:r, :], ALU.add))
                        dve.nop().then_inc(o_xu[hh], 1)
                        dve.nop().then_inc(o_xm, 1)
                dve.wait_ge(o_vec2, 32)
                for c in range(NCO):
                    for t in range(NT + 1):
                        u, r = 9 * c + t, rows(t)
                        b = u % 2
                        dve.wait_ge(e_z[b], u // 2 + 1)
                        if u >= 2:
                            dve.wait_ge(e_f[b], 1 + u // 2)
                        dve.tensor_tensor(sg[b][0:r, :], Z[b][0:r, 0:CW], vec[c // 4][0:r, (c % 4) * CW:(c % 4) * CW + CW], ALU.add).then_inc(e_a, 1)
                        dve.wait_ge(e_s, u + 1)
                        link(dve.tensor_tensor(sg[b][0:r, :], sg[b][0:r, :], (TB, DB)[b][0:r, 0:CW], ALU.mult))
                        dve.tensor_tensor(ochunk(t, c), ochunk(t, c), sg[b][0:r, :], ALU.add).then_inc(e_f[b], 1)


_INS = ["x_prompt", "x_sample", "p_prompt", "p_sample", "cache_diff_k", "cache_diff_v", "cache_dsa_k", "cache_dsa_v",
        "cache_idx_k", "page_table", "pre_norm_w", "post_norm_w", "w_in", "lam_q1", "lam_k1", "lam_q2", "lam_k2",
        "diff_norm_w", "w_out", "w_ple_gate", "b_ple_gate", "w_ple_proj"]
_OUTS = [(1, 1024, 2048), (8, 1, 2048), (1, 1, 1024, 8, 128), (1, 1, 1024, 8, 128), (1, 1, 1024, 2, 128),
         (1, 1, 1024, 2, 128), (1, 1, 1024, 64), (1, 8, 1, 8, 128), (1, 8, 1, 8, 128), (1, 8, 1, 2, 128),
         (1, 8, 1, 2, 128), (1, 8, 1, 64)]


def rope_table(first, n, d):
    r = d // 4
    half = r // 2
    inv = (np.float32(500000.0) ** (np.float32(-2.0 / r) * np.arange(half, dtype=np.float32))).astype(np.float32)
    ang = (np.arange(first, first + n, dtype=np.float32)[:, None] * inv[None, :]).astype(np.float32)
    c, s = np.cos(ang), np.sin(ang)
    return np.ascontiguousarray(np.stack([np.concatenate([c, c], -1), np.concatenate([s, s], -1)], 1).astype(np.float32))


def kernel(**inputs):
    import numpy as _np
    import concourse.bacc as _bacc
    from concourse import mybir as _mybir
    from concourse.bass_utils import run_bass_kernel_spmd as _run

    nc = _bacc.Bacc("TRN2", target_bir_lowering=False, num_devices=1)
    arrays, args = {}, []

    def give(name, a):
        a = _np.ascontiguousarray(a)
        arrays[name] = a
        args.append(nc.dram_tensor(name, a.shape, _mybir.dt.from_np(a.dtype), kind="ExternalInput").ap())

    for name in _INS:
        give(f"in_{name}_dram", inputs[name])
    give("rope_a", rope_table(0, T, DI))
    give("rope_b", rope_table(0, T, HD))
    give("rope_new", _np.concatenate([rope_table(PAST, 1, DI), rope_table(PAST, 1, HD)], -1).reshape(2, 48))
    for i, shape in enumerate(_OUTS):
        args.append(nc.dram_tensor(f"out_{i}_dram", shape, _mybir.dt.float32, kind="ExternalOutput").ap())
    hymba_step(nc, *args)
    r = _run(nc, [arrays], core_ids=[0])
    return tuple(r.results[0][f"out_{i}_dram"] for i in range(len(_OUTS)))
```

```python
import math
import numpy as np
import concourse.bass as bass
from concourse import mybir
from contextlib import ExitStack

F32 = mybir.dt.float32
BF16 = mybir.dt.bfloat16
I32 = mybir.dt.int32
U32 = mybir.dt.uint32
ALU = mybir.AluOpType
ACT = mybir.ActivationFunctionType
AX = mybir.AxisListType
ds = bass.ds

P = 128
D = 2048
KT = D // P
T = 1024
NT = T // P
NB = 8
PAST = 4096
NPG = PAST // P
POOL = 320
HA, HB, HKV = 8, 8, 2
HD = 128
NI = 4
DI = 64
TOPK = 256
BS = T - P
CW = 256
ROWS = 32
QA, KA, VA, GA = 0, 1024, 2048, 3072
QS, KS, VS, GS = 4096, 5120, 5376, 5632
QI, KI, WI = 6656, 6912, 6976
NIN = 6980
NEG = -1.0e30
TAKEN = -3.0e38
EPS = 1e-6
LAM_INIT = 0.8 - 0.6 * math.exp(-0.3 * 0)
SC_A = 1.0 / math.sqrt(64.0)
SC_B = 1.0 / math.sqrt(128.0)


class Chain:

    def __init__(self, eng, sem, clear=False):
        self.eng, self.sem, self.n = eng, sem, 0
        if clear:
            eng.sem_clear(sem)

    def __call__(self, ins):
        self.n += 1
        ins.then_inc(self.sem, 1)
        self.eng.wait_ge(self.sem, self.n)


def rope(link, z, tab, t1, t2, r):
    h = r // 2
    nd = len(z.shape) - 1
    cut = lambda a, lo, hi: a[tuple([slice(None)] * nd + [slice(lo, hi)])]
    cos, sin = tab
    x = cut(z, 0, r)
    link(link.eng.tensor_tensor(t1, x, cos, ALU.mult))
    link(link.eng.tensor_tensor(t2, x, sin, ALU.mult))
    link(link.eng.tensor_tensor(cut(z, 0, h), cut(t1, 0, h), cut(t2, h, r), ALU.subtract))
    link(link.eng.tensor_tensor(cut(z, h, r), cut(t1, h, r), cut(t2, 0, h), ALU.add))



def spread(ap, axis, n):
    ap = ap.unsqueeze(axis)
    shape = list(ap.shape)
    shape[axis] = n
    return ap.broadcast_to(shape)


def hymba_step(nc, x_prompt, x_sample, p_prompt, p_sample, cache_dk, cache_dv, cache_sk, cache_sv, cache_ik,
               page_table, pre_w, post_w, w_in, lam_q1, lam_k1, lam_q2, lam_k2, sub_w, w_out, w_pg, b_pg, w_pe,
               rope_a, rope_b, rope_new,
               y_prompt, y_sample, dk_p, dv_p, sk_p, sv_p, ik_p, dk_s, dv_s, sk_s, sv_s, ik_s):
    def dram(name, shape, dt=F32):
        return nc.dram_tensor(name, shape, dt, kind="Internal").ap()

    zs_d = dram("zs_d", [NB, NIN])
    snew_a_d = dram("snew_a_d", [NB, 16])
    mask_d = dram("mask_d", [NT, P, T])
    qiT_d = dram("qiT_d", [2, P, T])
    oT_d = dram("oT_d", [HA + HB, P, T])

    xp = x_prompt.rearrange("b (t p) d -> p (b t) d", p=P)
    xs = x_sample.rearrange("b s d -> (b s) d")
    win = w_in.rearrange("l (k p) n -> p (l k) n", p=P)

    ctx = ExitStack()
    with ctx:
        def sb(name, shape, dt=F32):
            return ctx.enter_context(nc.sbuf_tensor(name, shape, dt))

        held = []

        def sem(name):
            held.append(nc.alloc_semaphore(name=name))
            return held[-1]

        def end_stage():
            nc.clear_and_free_semaphores(held)
            held.clear()
            nc.all_engine_barrier()

        hT = sb("hT", [P, KT, T])
        W = sb("W", [P, 2, KT, CW])
        big = sb("big", [P, 7 * 1024])
        qk = sb("qk", [P, NT, 2 * HD])
        vg = sb("vg", [P, 2, NT, HD])
        qkT = sb("qkT", [P, 2, T])
        e12 = sb("e12", [P, 2, T])
        pT = sb("pT", [P, NT, P])
        kiT = sb("kiT", [P, T])
        bias = sb("bias", [P, (NT - 1) * BS + T], BF16)
        qb = sb("qb", [P, 1024])
        ident = sb("ident", [P, P])
        ones = sb("ones", [P, P])
        identb = sb("identb", [P, P], BF16)
        causal = sb("causal", [P, P], BF16)
        ropa = sb("ropa", [P, NT, 2, 16])
        gsT = sb("gsT", [P, 26, NB])
        si = sb("si", [P, NB, NPG + 1])
        wall = sb("wall", [P, NT, NI])
        odec = sb("odec", [P, 16, ROWS])
        lam = sb("lam", [P, 4])
        coefm = sb("coefm", [P, HA])
        small = sb("small", [P, 320])
        ptab = sb("ptab", [1, NB * NPG], I32)

        Z = [ctx.enter_context(nc.psum_tensor(f"Z{i}", [P, 512], F32)) for i in range(2)]
        S = [ctx.enter_context(nc.psum_tensor(f"S{i}", [P, T], F32)) for i in range(2)]
        TB = ctx.enter_context(nc.psum_tensor("TB", [P, 512], F32))
        DB = ctx.enter_context(nc.psum_tensor("DB", [P, 512], F32))

        hTs = pT[:, 0:4, :].rearrange("p a b -> p (a b)").rearrange("p (k r) -> p k r", r=ROWS)
        zs = big[0:NB, 0:NIN]
        xbuf = [vg[:, :, :, :].rearrange("p a b c -> p (a b c)"), qkT[:, :, :].rearrange("p a b -> p (a b)"),
                big[:, 2560:4608], big[:, 4608:6656]]
        junk = bias[:, :].bitcast(F32)[:, 0:2048]
        wqi = [a.rearrange("p (k c) -> p k c", c=CW) for a in xbuf[0:2]]
        wki = bias[:, :].bitcast(F32)[:, 0:KT * (NIN - KI)].rearrange("p (k c) -> p k c", k=KT)
        kid = bias[:, :].bitcast(F32)[:, 1152:1152 + NT * P].rearrange("p (t c) -> p t c", c=P)
        order = [NT] + list(range(NT))
        prew = qk[:, :, :].rearrange("p a b -> p (a b)")
        lamin = kiT[:, 0:256].rearrange("p (a d) -> p a d", a=4)
        maskt = qb
        ss, rs = small[:, 0:9], small[:, 16:25]
        sel = small[:, 32:40]
        eps = small[:, 48:49]
        tmp = e12[:, 0, 0:512].rearrange("p (s n) -> p s n", s=2)
        INDEX_FROM = NT + 2
        NCH = (NIN + CW - 1) // CW
        width = lambda c: min(CW, NIN - c * CW)
        rows = lambda t: P if t < NT else NB

        s_const = sem("u_const")
        s_mask = sem("u_mask")
        s_maskout = sem("u_maskout")
        s_in = sem("u_in")
        s_x = [sem(f"u_x{i}") for i in range(4)]
        s_ss = sem("u_ss")
        s_rs = sem("u_rs")
        s_h = sem("u_h")
        s_ht = sem("u_ht")
        s_hc = sem("u_hc")
        s_pool = sem("u_pool")
        s_act = sem("u_act")
        s_lam = sem("u_lam")
        s_w = [sem(f"u_w{i}") for i in range(2)]
        s_pz = sem("u_pz")
        s_evz = sem("u_evz")
        s_ps = sem("u_ps")
        s_evs = sem("u_evs")
        s_dve = sem("u_dve")
        s_wi = sem("u_wi")
        s_iz = [sem("u_iz0"), sem("u_iz1")]
        s_izf = [sem("u_izf0"), sem("u_izf1")]

        with nc.Block() as block:
            @block.sync
            def _(sp):
                sp.dma_start(prew, pre_w.partition_broadcast(P).rearrange("q l d -> q (l d)")).then_inc(s_in, 16)

                def load_x(n):
                    t = order[n]
                    if n >= 4:
                        sp.wait_ge(s_ht, 2 * (n - 3))
                        sp.wait_ge(s_ss, n - 3)
                    sp.dma_start(xbuf[n % 4][0:rows(t), :], xp[:, t, :] if t < NT else xs).then_inc(s_x[n % 4], 16)

                def load_w(c):
                    if c >= 2:
                        sp.wait_ge(s_pz, c - 1)
                    sp.dma_start(W[:, c % 2, :, :], win[:, :, c * CW:(c + 1) * CW]).then_inc(s_w[c % 2], 16)

                load_x(0)
                load_x(1)
                load_w(0)
                load_x(2)
                load_w(1)
                load_x(3)
                for n in range(1, NT + 1):
                    if n + 3 <= NT:
                        load_x(n + 3)
                    load_w(n + 1)
                sp.wait_ge(s_ht, 2 * (NT + 1))
                for j in range(2):
                    sp.dma_start(wqi[j], win[:, 8 * j:8 * j + 8, QI:KI]).then_inc(s_wi, 16)
                sp.wait_ge(s_ss, NT + 1)
                sp.dma_start(wki, win[:, :, KI:NIN]).then_inc(s_wi, 16)
                with sp.Fori(NT // 2 + 1, 13) as i:
                    for s in range(2):
                        sp.wait_ge(s_pz, 2 * i + s - 1)
                        sp.dma_start(W[:, s, :, :], win[:, :, ds(2 * i * CW + s * CW, CW)]).then_inc(s_w[s], 16)
                for c in range(26, NCH):
                    sp.wait_ge(s_pz, c - 1)
                    sp.dma_start(W[:, c % 2, :, 0:width(c)], win[:, :, c * CW:c * CW + width(c)]).then_inc(s_w[c % 2], 16)

            @block.gpsimd
            def _(pool):
                link = Chain(pool, s_pool)
                pool.memset(odec[:, :, :], 0.0)
                pool.memset(hTs, 0.0)
                pool.memset(ones[:, :], 1.0)
                for a, v in ((ident, 0.0), (identb, 0.0), (causal, 0.0)):
                    pool.memset(a[:, :], v)
                pool.memset(coefm[:, :], 0.0)
                pool.memset(small[:, 40:48], 0.0)
                pool.memset(eps, EPS)
                link(pool.memset(sel, 0.0))
                for a in (ident, identb):
                    pool.affine_select(out=a[:, :], in_=a[:, :], compare_op=ALU.not_equal, fill=1.0, base=0,
                                       pattern=[[-1, P]], channel_multiplier=1)
                pool.affine_select(out=causal[:, :], in_=causal[:, :], compare_op=ALU.is_ge, fill=NEG, base=0,
                                   pattern=[[-1, P]], channel_multiplier=1)
                for g in range(4):
                    link(pool.affine_select(out=sel, in_=sel, compare_op=ALU.not_equal, fill=1.0, base=-32 * g,
                                            pattern=[[-1, NB]], channel_multiplier=1))
                for s, a in ((0, coefm[:, :]), (1, small[:, 40:48])):
                    v = a.rearrange("p (g j) -> p g j", j=2)
                    link(pool.affine_select(out=v, in_=v, compare_op=ALU.not_equal, fill=1.0, base=-s,
                                            pattern=[[-32, 4], [-2, 2]], channel_multiplier=1))
                pool.nop().then_inc(s_const, 1)
                for t in range(NT):
                    if t:
                        pool.wait_ge(s_maskout, 16 * t)
                    link(pool.memset(maskt[:, :], 0.0))
                    pool.affine_select(out=maskt[:, :], in_=maskt[:, :], compare_op=ALU.is_ge, fill=NEG, base=P * t,
                                       pattern=[[-1, T]], channel_multiplier=1).then_inc(s_mask, 1)
                    pool.wait_ge(s_mask, t + 1)
                    pool.dma_start(mask_d[t, :, :], maskt[:, :]).then_inc(s_maskout, 16)
                pool.wait_ge(s_maskout, 16 * NT)

            @block.scalar
            def _(act):
                for i, v in enumerate((lam_q1, lam_k1, lam_q2, lam_k2)):
                    act.dma_start(lamin[:, i, :], v.partition_broadcast(P).rearrange("q l d -> q (l d)")).then_inc(s_in, 16)
                act.dma_start(ptab[:, :], page_table.rearrange("b n -> (b n)").unsqueeze(0)).then_inc(s_in, 16)
                act.dma_start(ropa[:, :, :, :], rope_a.rearrange("(t p) a r -> p t a r", p=P)).then_inc(s_in, 16)

                def root(n):
                    act.wait_ge(s_x[n % 4], 16 * (n // 4 + 1))
                    r = rows(order[n])
                    if n:
                        act.wait_ge(s_ss, n)
                    act.activation(junk[0:r, :], xbuf[n % 4][0:r, :], ACT.Square, accum_out=ss[0:r, n:n + 1]).then_inc(s_ss, 1)
                    act.wait_ge(s_ss, n + 1)
                    act.wait_ge(s_const, 1)
                    act.activation(rs[0:r, n:n + 1], ss[0:r, n:n + 1], ACT.Sqrt, scale=1.0 / D, bias=eps[0:r, :]).then_inc(s_rs, 1)

                def copy_partial(c, cc, w):
                    act.wait_ge(s_pz, cc + 1)
                    if c >= 2:
                        act.wait_ge(s_ps, cc - 1)
                    act.activation(tmp[:, c % 2, 0:w], Z[c % 2][:, 0:w], ACT.Copy).then_inc(s_evz, 1)

                root(0)
                for n, t in enumerate(order):
                    if n < NT:
                        root(n + 1)
                    for j in range(2):
                        act.wait_ge(s_ht, 2 * n + j + 1)
                        if t < NT:
                            act.activation(hT[:, 8 * j:8 * j + 8, t * P:(t + 1) * P],
                                           S[j][:, :].rearrange("p (k n) -> p k n", n=P), ACT.Copy).then_inc(s_hc, 1)
                        else:
                            act.activation(hTs[:, 8 * j:8 * j + 8, 0:NB],
                                           S[j][:, :].rearrange("p (k n) -> p k n", n=P)[:, :, 0:NB], ACT.Copy).then_inc(s_hc, 1)
                    if n:
                        copy_partial(n - 1, n - 1, CW)
                act.wait_ge(s_lam, 1)
                act.activation(lam[:, 2:4], lam[:, 2:4], ACT.Exp).then_inc(s_act, 1)
                act.wait_ge(s_h, NT + 1)
                for c in range(NT, NCH):
                    copy_partial(c, c, width(c))
                    m = c - INDEX_FROM
                    if 0 <= m < 2 * NT:
                        t = m % NT
                        act.wait_ge(s_iz[m % 2], m // 2 + 1)
                        if m < NT:
                            act.activation(qk[:, t, :], S[m % 2][:, 0:CW], ACT.Copy).then_inc(s_izf[m % 2], 1)
                        else:
                            act.activation(kid[:, t, 0:DI], S[m % 2][:, 0:DI], ACT.Copy)
                            act.activation(wall[:, t, :], S[m % 2][:, DI:DI + NI], ACT.Copy).then_inc(s_izf[m % 2], 1)

            @block.vector
            def _(dve):
                link = Chain(dve, s_dve)
                dve.wait_ge(s_in, 16 * 7)
                link(dve.tensor_tensor(lamin[:, 0:4:2, :], lamin[:, 0:4:2, :], lamin[:, 1:4:2, :], ALU.mult))
                link(dve.tensor_reduce(lam[:, 2:4], lamin[:, 0:4:2, :], AX.X, ALU.add))
                dve.nop().then_inc(s_lam, 1)

                def take(c, cc, w):
                    dve.wait_ge(s_ps, cc + 1)
                    src = (TB, DB)[c % 2]
                    dst = zs[:, cc * CW:cc * CW + w] if isinstance(cc, int) else big[0:NB, ds(cc * CW, w)]
                    dve.tensor_copy(dst, src[0:NB, 0:w]).then_inc(s_evs, 1)

                for n, t in enumerate(order):
                    dve.wait_ge(s_rs, n + 1)
                    r = rows(t)
                    link(dve.reciprocal(rs[0:r, n:n + 1], rs[0:r, n:n + 1]))
                    dve.scalar_tensor_tensor(out=xbuf[n % 4][0:r, :], in0=xbuf[n % 4][0:r, :], scalar=rs[0:r, n:n + 1],
                                             in1=prew[0:r, :], op0=ALU.mult, op1=ALU.mult).then_inc(s_h, 1)
                    if n >= 3:
                        take(n - 3, n - 3, CW)
                for c in (NT - 2, NT - 1):
                    take(c, c, CW)
                dve.wait_ge(s_act, 1)
                link(dve.tensor_tensor(lam[:, 1:2], lam[:, 3:4], lam[:, 2:3], ALU.subtract))
                link(dve.tensor_scalar(lam[:, 0:1], lam[:, 1:2], -LAM_INIT, None, ALU.add))
                dve.wait_ge(s_const, 1)
                link(dve.scalar_tensor_tensor(out=coefm[:, :], in0=small[:, 40:48], scalar=lam[:, 0:1], in1=coefm[:, :],
                                              op0=ALU.mult, op1=ALU.add))

                with dve.Fori(NT // 2, 13) as i:
                    for s in range(2):
                        take(2 + s, 2 * i + s, CW)
                for c in range(26, NCH):
                    take(c, c, width(c))

            @block.tensor
            def _(pe):
                pe.wait_ge(s_const, 1)

                def turn(n):
                    pe.wait_ge(s_h, n + 1)
                    r = rows(order[n])
                    for j in range(2):
                        if n:
                            pe.wait_ge(s_hc, 2 * (n - 1) + j + 1)
                        for k in range(8):
                            kk = 8 * j + k
                            mm = pe.transpose(S[j][:, k * P:k * P + r], xbuf[n % 4][0:r, kk * P:(kk + 1) * P], ident[0:r, 0:r])
                        mm.then_inc(s_ht, 1)

                def add(c, cc, w):
                    pe.wait_ge(s_evz, cc + 1)
                    if c >= 2:
                        pe.wait_ge(s_evs, cc - 1)
                    pe.matmul((TB, DB)[c % 2][0:NB, 0:w], sel, tmp[:, c % 2, 0:w], start=True, stop=True).then_inc(s_ps, 1)

                def project(c, cc, w):
                    pe.wait_ge(s_w[c % 2], cc * 8 - (c % 2) * 8 + 16)
                    if c >= 2:
                        pe.wait_ge(s_evz, cc - 1)
                    for k in range(KT):
                        g = k % 4
                        mm = pe.matmul(Z[c % 2][32 * g:32 * g + 32, 0:w], hTs[:, k, :], W[:, c % 2, k, 0:w],
                                       start=(k < 4), stop=(k >= KT - 4))
                    mm.then_inc(s_pz, 1)
                turn(0)
                for n in range(1, NT + 1):
                    turn(n)
                    if n == 1:
                        pe.wait_ge(s_hc, 2)
                    project(n - 1, n - 1, CW)
                    if n >= 2:
                        add(n - 2, n - 2, CW)

                def index_tile(m):
                    t = m % NT
                    if m == 0:
                        pe.wait_ge(s_wi, 48)
                        pe.wait_ge(s_hc, 2 * (NT + 1))
                    if m >= 2:
                        pe.wait_ge(s_izf[m % 2], m // 2)
                    for k in range(KT):
                        rhs = wqi[k // 8][:, k % 8, :] if m < NT else wki[:, k, :]
                        mm = pe.matmul(S[m % 2][:, 0:rhs.shape[-1]], hT[:, k, t * P:(t + 1) * P], rhs, start=(k == 0), stop=(k == KT - 1))
                    mm.then_inc(s_iz[m % 2], 1)

                for c in range(NT, NCH):
                    project(c, c, width(c))
                    add(c - 1, c - 1, CW)
                    if 0 <= c - INDEX_FROM < 2 * NT:
                        index_tile(c - INDEX_FROM)
                add(NCH - 1, NCH - 1, width(NCH - 1))

        end_stage()

        zg = lambda lo, n, d: zs[:, lo:lo + n * d].rearrange("p (g d) -> p g d", d=d)
        rnew = small[0:NB, 64:160].rearrange("p (a r) -> p a r", a=2)
        sna, snb, sni, rel4 = small[0:NB, 160:176], small[0:NB, 176:184], small[0:NB, 184:185], small[0:NB, 188:192]
        snew_i_d = dram("snew_i_d", [NB, 1])
        flat8 = lambda a: a[0:NB, :, :].rearrange("p a b -> p (a b)")
        gates = flat8(e12)
        prod8 = flat8(pT)
        qi4 = qk[:, :, :].rearrange("p t (g d) -> p t g d", d=DI)

        v_in = sem("v_in")
        v_dve = sem("v_dve")
        v_rot = sem("v_rot")
        v_out = sem("v_out")
        v_eg = sem("v_eg")
        v_tr = sem("v_tr")
        v_ki = sem("v_ki")
        v_qt = sem("v_qt")
        v_qc = sem("v_qc")
        v_st = sem("v_st")

        with nc.Block() as block:
            @block.sync
            def _(sp):
                sp.dma_start(rnew, rope_new.unsqueeze(0).broadcast_to([NB, 2, 48])).then_inc(v_in, 16)
                sp.wait_ge(v_rot, 1)
                sp.dma_start(zs_d, zs).then_inc(v_out, 16)
                for dst, lo, n in ((dk_s, KA, 1024), (dv_s, VA, 1024), (sk_s, KS, 256), (sv_s, VS, 256)):
                    sp.dma_start(dst.rearrange("l b s h d -> (l b s) (h d)"), zs[:, lo:lo + n]).then_inc(v_out, 16)
                sp.dma_start(ik_s.rearrange("l b s d -> (l b s) d"), zs[:, KI:KI + DI]).then_inc(v_out, 16)
                sp.wait_ge(v_rot, 2)
                sp.dma_start(snew_a_d, sna).then_inc(v_out, 16)
                sp.wait_ge(v_rot, 3)
                sp.dma_start(snew_i_d, sni).then_inc(v_out, 16)
                sp.wait_ge(v_qc, 2)
                sp.dma_start(qiT_d.rearrange("j p t -> p j t"), qkT[:, :, :]).then_inc(v_st, 16)
                sp.wait_ge(v_ki, 2)
                sp.dma_start(ik_p.rearrange("l b (t p) d -> p (l b t) d", p=P), kid[:, :, 0:DI]).then_inc(v_st, 16)
                sp.wait_ge(v_out, 16 * 8)
                sp.dma_start(si[0:1, :, NPG:NPG + 1], snew_i_d.unsqueeze(0),
                             allow_slow_non_contiguous=True).then_inc(v_st, 16)
                sp.wait_ge(v_st, 48)

            @block.vector
            def _(dve):
                link = Chain(dve, v_dve)
                dve.wait_ge(v_in, 16)
                tab = lambda n, lo, r: tuple(spread(rnew[:, a, lo:lo + r], 1, n) for a in (0, 1))
                for lo, n, d, c0 in ((QA, 32, DI, 0), (QS, 10, HD, 16), (QI, 5, DI, 0)):
                    r = d // 4
                    tt = [prod8[:, a * 512:a * 512 + n * r].rearrange("p (g r) -> p g r", r=r) for a in (0, 1)]
                    rope(link, zg(lo, n, d), tab(n, c0, r), tt[0], tt[1], r)
                link(dve.memset(si[:, :, NPG:NPG + 1], NEG))
                dve.nop().then_inc(v_rot, 1)
                pr = prod8[:, 0:1024]
                link(dve.tensor_tensor(pr, zs[:, QA:QA + 1024], zs[:, KA:KA + 1024], ALU.mult))
                link(dve.tensor_reduce(sna, pr.rearrange("p (g d) -> p g d", d=64), AX.X, ALU.add))
                dve.nop().then_inc(v_rot, 1)
                link(dve.tensor_tensor(pr.rearrange("p (n j d) -> p n j d", n=2, d=HD),
                                       zs[:, QS:QS + 1024].rearrange("p (n j d) -> p n j d", n=2, d=HD),
                                       spread(zg(KS, 2, HD), 2, 4), ALU.mult))
                link(dve.tensor_reduce(snb, pr.rearrange("p (g d) -> p g d", d=HD), AX.X, ALU.add))
                link(dve.tensor_tensor(pr[:, 0:256].rearrange("p (g d) -> p g d", d=DI), zg(QI, 4, DI),
                                       spread(zs[:, KI:KI + DI], 1, NI), ALU.mult))
                link(dve.tensor_reduce(rel4, pr[:, 0:256].rearrange("p (g d) -> p g d", d=DI), AX.X, ALU.add))
                link(dve.scalar_tensor_tensor(out=rel4, in0=rel4, scalar=0.0, in1=zs[:, WI:WI + NI], op0=ALU.max, op1=ALU.mult))
                link(dve.tensor_reduce(sni, rel4, AX.X, ALU.add))
                dve.nop().then_inc(v_rot, 1)
                dve.wait_ge(v_eg, 1)
                link(dve.tensor_tensor(gates[:, 0:1024], gates[:, 0:1024], zs[:, GA:GA + 1024], ALU.mult))
                link(dve.tensor_tensor(gates[:, 1024:2048], gates[:, 1024:2048], zs[:, GS:GS + 1024], ALU.mult))
                dve.nop().then_inc(v_rot, 1)
                dve.wait_ge(v_tr, 1)
                link(dve.tensor_copy(gsT[:, :, :].rearrange("p a b -> p (a b)"), TB[:, 0:26 * NB]))
                t4 = lambda a, g: prompt_tmp[:, a * 512:a * 512 + NT * g * 16].rearrange("p (t g r) -> p t g r", g=g, r=16)
                prompt_tmp = pT[:, :, :].rearrange("p a b -> p (a b)")
                ptab4 = lambda g: tuple(spread(ropa[:, :, a, :], 2, g) for a in (0, 1))
                rope(link, qi4, ptab4(4), t4(0, 4), t4(1, 4), 16)
                dve.nop().then_inc(v_ki, 1)
                rope(link, kid[:, :, 0:DI], tuple(ropa[:, :, a, :] for a in (0, 1)),
                     prompt_tmp[:, 0:128].rearrange("p (t r) -> p t r", r=16),
                     prompt_tmp[:, 512:640].rearrange("p (t r) -> p t r", r=16), 16)
                link(dve.tensor_copy(kid[:, :, DI:2 * DI], kid[:, :, 0:DI]))
                dve.nop().then_inc(v_ki, 1)

            @block.scalar
            def _(act):
                act.activation(gates[:, 0:1024], zs[:, GA:GA + 1024], ACT.Sigmoid)
                act.activation(gates[:, 1024:2048], zs[:, GS:GS + 1024], ACT.Sigmoid).then_inc(v_eg, 1)
                for j in range(2):
                    act.wait_ge(v_qt, j + 1)
                    act.activation(qkT[:, j, :], S[j][:, :], ACT.Copy).then_inc(v_qc, 1)
                act.wait_ge(v_qt, 3)
                act.activation(kiT[:, :], S[0][:, :], ACT.Copy).then_inc(v_qc, 1)

            @block.tensor
            def _(pe):
                pe.wait_ge(v_rot, 4)
                for j in range(26):
                    src = gates[:, j * P:(j + 1) * P] if j < 16 else (
                        zs[:, QS + (j - 16) * P:QS + (j - 15) * P] if j < 24 else zs[:, VS + (j - 24) * P:VS + (j - 23) * P])
                    mm = pe.transpose(TB[:, j * NB:(j + 1) * NB], src, ident[0:NB, 0:NB])
                mm.then_inc(v_tr, 1)
                pe.wait_ge(v_ki, 1)
                for j in range(2):
                    for t in range(NT):
                        mm = pe.transpose(S[j][:, t * P:(t + 1) * P], qk[:, t, j * P:(j + 1) * P], ident[:, :])
                    mm.then_inc(v_qt, 1)
                pe.wait_ge(v_ki, 2)
                pe.wait_ge(v_qc, 1)
                for t in range(NT):
                    mm = pe.transpose(S[0][:, t * P:(t + 1) * P], kid[:, t, :], ident[:, :])
                mm.then_inc(v_qt, 1)

        end_stage()

        ring_k = [big[:, s * 1024:(s + 1) * 1024] for s in range(4)]
        ring_v = [big[:, (4 + s) * 1024:(5 + s) * 1024] for s in range(2)] + ring_k[2:4]
        work = big[:, 6 * 1024:7 * 1024]
        pTf = pT[:, :, :].rearrange("p a b -> p (a b)")
        prods = [work, pTf]
        kib = sb("kib", [P, 2, 4, DI])
        kprod = sb("kprod", [P, 2, 4, DI])
        qib = sb("qib", [P, NI, DI])
        sc = sb("sc", [P, NPG + 1, 16])
        ex = sb("ex", [P, NPG + 1, 16])
        vnew = sb("vnew", [P, 1024])
        qit = sb("qit", [P, 2, P])
        subw = sb("subw", [P, HD])
        srel = sb("srel", [P, NPG, NI])
        mx, nmx = small[:, 192:208].rearrange("p (t j) -> p t j", j=2), small[:, 208:224].rearrange("p (t j) -> p t j", j=2)
        rsum, rrec = small[:, 224:240].rearrange("p (t j) -> p t j", j=2), small[:, 240:256].rearrange("p (t j) -> p t j", j=2)
        cc, ss8, top8, m16, es16 = small[:, 256:264], small[:, 264:272], small[:, 272:280], small[:, 288:304], small[:, 304:320]
        mm1, den, coef, dg16 = small[0:16, 64:65], small[:, 65:66], small[:, 72:80], small[0:16, 80:96]
        zero = small[:, 104:105]
        wib, wic = small[:, 96:100], small[:, 100:104]
        od = e12[:, 1, 0:256]
        z4 = qk[:, :, :].rearrange("p t (g d) -> p t g d", d=DI)
        onat = qk[:, :, 0:HD]
        v_sb, g_sb = vg[:, 0, :, :], vg[:, 1, :, :]
        sqs = kprod[:, 0, 0:2, :].rearrange("p a d -> p (a d)")
        sig = qk[:, :, HD:2 * HD]
        INDEX_AT = (11, 11, 12, 12)
        ROUNDS = (14, 3, 3, 2, 2, 2, 2, 2, 2)
        SOFTMAX_AT = (12, 13)
        TURN_AT = 10
        ROPE_AT = 22
        assert sum(ROUNDS) == TOPK // 8
        SPANS = ((0, NT // 2, T // 2), (NT // 2, NT, T))
        F = lambda t: t if t < 4 else 2 * t - 4
        NF = F(NT)
        key_spans = lambda t: [(lo, min(lo + 512, t * P)) for lo in range(0, t * P, 512)] + [(t * P, t * P + P)]
        dkv = lambda a: a.rearrange("l n p h d -> (l n) p (h d)")
        ck, cv, ci = dkv(cache_dk), dkv(cache_dv), cache_ik.rearrange("l n p d -> (l n) p d")

        w_rdy = [sem("a_w0"), sem("a_w1")]
        w_used = [sem("a_wu0"), sem("a_wu1")]
        k_rdy = [sem(f"a_k{s}") for s in range(4)]
        k_used = [sem(f"a_ku{s}") for s in range(4)]
        v_rdy = [sem(f"a_v{s}") for s in range(4)]
        v_used = [sem(f"a_vu{s}") for s in range(4)]
        i_rdy = [sem("a_i0"), sem("a_i1")]
        i_used = [sem("a_iu0"), sem("a_iu1")]
        q_rdy = [sem("a_q0"), sem("a_q1")]
        q_free = [sem("a_qf0"), sem("a_qf1")]
        b_in = sem("a_bin")
        vn_in = sem("a_vnin")
        c_in = sem("a_cin")
        t_in = sem("a_tin")
        qt_in = sem("a_qtin")
        g_si = sem("a_gsi")
        g_ch = sem("a_gch")
        z_full = [sem("a_z0"), sem("a_z1")]
        z_free = [sem("a_zf0"), sem("a_zf1")]
        s_full = [sem("a_s0"), sem("a_s1")]
        s_free = [sem("a_sf0"), sem("a_sf1")]
        t_full, t_free = sem("a_t"), sem("a_tf")
        d_ch, a_ch = sem("a_dch"), sem("a_ach")
        d_ps = sem("a_dps")
        d_red = sem("a_dred")
        d_rot = sem("a_drot")
        d_m = sem("a_dm")
        p_m = sem("a_pm")
        d_sub = sem("a_dsub")
        a_e = sem("a_ae")
        d_es = sem("a_des")
        d_od = sem("a_dod")
        a_eg = sem("a_aeg")
        d_nm = sem("a_dnm")
        a_x = sem("a_ax")
        d_p = sem("a_dp")
        a_ss = sem("a_ass")
        a_sq = sem("a_asq")
        d_og = sem("a_dog")
        a_rl = sem("a_arl")
        p_idx = sem("a_pidx")
        d_top = sem("a_dtop")
        st_k, st_v, st_o = sem("a_stk"), sem("a_stv"), sem("a_sto")
        x_in = sem("a_xin")

        with nc.Block() as block:
            @block.sync
            def _(sp):
                for s in (*w_used, *k_used, *v_used, *i_used, *q_free, *z_free, *s_free, d_sub, p_m, g_si, p_idx, t_free, t_full,
                          st_k, st_v, st_o, d_og, a_sq):
                    sp.sem_inc(s, 1)
                sp.dma_start(subw[:, :], sub_w.partition_broadcast(P).rearrange("q l d -> q (l d)")).then_inc(x_in, 16)
                for first, end, width in SPANS:
                    with sp.Fori(first, end) as i:
                        sp.wait_ge(w_used[0], 1 + i)
                        for j, lo in enumerate((QA, KA)):
                            sp.dma_start(W[:, 0, :, j * HD:(j + 1) * HD], win[:, :, ds(i * HD + lo, HD)]).then_inc(w_rdy[0], 16)
                        sp.wait_ge(k_used[3], 1 + 8 * i)
                        sp.dma_start(qb[:, :], zs_d[ds(i, 1), QA:QA + 1024].broadcast_to([P, 1024])).then_inc(b_in, 16)
                        sp.wait_ge(d_sub, 1 + i)
                        sp.wait_ge(x_in, 17)
                        sp.dma_start(sc[0:1, NPG, :], snew_a_d[ds(i, 1), :]).then_inc(b_in, 16)
                        sp.wait_ge(g_si, 1 + i)
                        sp.dma_start(qib[:, :, :].rearrange("p h d -> p (h d)"),
                                     zs_d[ds(i, 1), QI:QI + 256].broadcast_to([P, 256])).then_inc(c_in, 16)
                        sp.dma_start(wib, zs_d[ds(i, 1), WI:WI + NI].broadcast_to([P, NI])).then_inc(c_in, 16)
                        for j in range(8):
                            if j == 4:
                                sp.wait_ge(w_used[1], 1 + i)
                                for q, lo in enumerate((VA, GA)):
                                    sp.dma_start(W[:, 1, :, q * HD:(q + 1) * HD], win[:, :, ds(i * HD + lo, HD)]).then_inc(w_rdy[1], 16)
                            sp.wait_ge(i_used[j % 2], 1 + 4 * i + j // 2)
                            for s in range(4):
                                page = sp.value_load(ptab[0:1, ds(i * NPG + 4 * j + s, 1)], min_val=0, max_val=POOL - 1)
                                sp.dma_start(kib[:, j % 2, s, :], ci[ds(page, 1), :, :].rearrange("o p d -> (o p) d")).then_inc(i_rdy[j % 2], 16)
                                sp.wait_ge(k_used[s], 1 + 8 * i + j)
                                if j == 0 and s >= 2:
                                    sp.wait_ge(v_used[s], 1 + 8 * i)
                                sp.dma_start(ring_k[s], ck[ds(page, 1), :, :].rearrange("o p d -> (o p) d")).then_inc(k_rdy[s], 16)
                        sp.wait_ge(p_m, 1 + 5 * i)
                        sp.dma_start(vnew[0:1, :], zs_d[ds(i, 1), VA:VA + 1024]).then_inc(vn_in, 16)
                        sp.wait_ge(p_idx, 1 + i)
                        sp.dma_start(qit[:, :, :], qiT_d[:, :, ds(i * P, P)].rearrange("j p t -> p j t")).then_inc(qt_in, 16)
                        sp.wait_ge(d_ps, (NPG - 1) * (i + 1))
                        sp.dma_start(work[:, 0:width], mask_d[ds(i, 1), :, 0:width].rearrange("o p t -> (o p) t")).then_inc(t_in, 16)
                        sp.wait_ge(d_rot, i + 1)
                        sp.dma_start(dk_p.rearrange("l b (t p) h d -> p (l b t) h d", p=P)[:, :, ds(i, 1), :].rearrange("p t o d -> p t (o d)"),
                                     qk[:, :, HD:2 * HD]).then_inc(st_k, 16)
                        for b in range(2):
                            sp.wait_ge(z_free[b], 1 + 12 * i + 8)
                        sp.dma_start(dv_p.rearrange("l b (t p) h d -> p (l b t) h d", p=P)[:, :, ds(i, 1), :].rearrange("p t o d -> p t (o d)"),
                                     v_sb).then_inc(st_v, 16)
                for s, lo in enumerate((KS, VS)):
                    sp.wait_ge(w_used[s], 1 + HA)
                    sp.dma_start(W[:, s, :, :], win[:, :, lo:lo + CW]).then_inc(w_rdy[s], 16)
                    sp.wait_ge(w_rdy[s], 32 * HA + 16)
                sp.wait_ge(st_k, 1 + 16 * HA)
                sp.wait_ge(st_v, 1 + 16 * HA)

            @block.gpsimd
            def _(pool):
                pool.memset(sc[:, NPG, :], NEG)
                pool.memset(den, 1.0)
                pool.memset(zero, 0.0)
                pool.memset(vnew[:, :], 0.0).then_inc(x_in, 1)
                for first, end, width in SPANS:
                    with pool.Fori(first, end) as i:
                        link = Chain(pool, g_ch, clear=True)
                        pool.wait_ge(c_in, 32 * i + 32)
                        pool.wait_ge(a_sq, 1 + i)
                        for u in range(8 * NI):
                            j, h = u // NI, u % NI
                            if h == 0:
                                pool.wait_ge(i_rdy[j % 2], 64 * (4 * i + j // 2 + 1))
                            pool.wait_ge(q_free[u % 2], 1 + 16 * i + u // 2)
                            mul = pool.tensor_tensor(kprod[:, u % 2, :, :], kib[:, j % 2, :, :], spread(qib[:, h, :], 1, 4), ALU.mult)
                            mul.then_inc(q_rdy[u % 2], 1)
                            if (u + 1) % 4 == 3:
                                pool.wait_ge(k_rdy[3], 16 * (8 * i + (u + 1) // 4 + 1))
                                pool.wait_ge(d_ps, (NPG - 1) * i + u)
                                pool.tensor_tensor(prods[1], ring_k[3], qb[:, :], ALU.mult).then_inc(k_used[3], 1)
                            if h == NI - 1:
                                pool.wait_ge(q_rdy[u % 2], 16 * i + u // 2 + 1)
                                pool.nop().then_inc(i_used[j % 2], 1)
                        for b in range(2):
                            pool.wait_ge(q_free[b], 1 + 16 * i + 16)
                        link(pool.tensor_tensor(zero, zero, zero, ALU.mult))
                        link(pool.tensor_scalar(srel[:, :, :], srel[:, :, :], 0.0, None, ALU.max))
                        link(pool.tensor_tensor(srel[:, :, :], srel[:, :, :], spread(wib, 1, NPG), ALU.mult))
                        for h in range(1, NI):
                            link(pool.tensor_tensor(srel[:, :, 0], srel[:, :, 0], srel[:, :, h], ALU.add))
                        pool.tensor_copy(si[:, ds(i, 1), 0:NPG].rearrange("p o n -> p (o n)"), srel[:, :, 0]).then_inc(g_si, 1)
                        pool.wait_ge(g_si, 1 + i + 1)
                        for v in range(NPG):
                            page = pool.value_load(ptab[0:1, ds(i * NPG + v, 1)], min_val=0, max_val=POOL - 1)
                            pool.wait_ge(v_used[v % 4], 1 + 8 * i + v // 4)
                            if v in (2, 3):
                                pool.wait_ge(k_used[v], 1 + 8 * i + 8)
                            pool.dma_start(ring_v[v % 4], cv[ds(page, 1), :, :].rearrange("o p d -> (o p) d")).then_inc(v_rdy[v % 4], 16)

            @block.scalar
            def _(act):
                for first, end, width in SPANS:
                    with act.Fori(first, end) as i:
                        act.wait_ge(st_k, 1 + 16 * i)
                        act.wait_ge(d_og, 1 + i)
                        for c in range(2 * NT):
                            t = c % NT
                            act.wait_ge(z_full[c % 2], 12 * i + c // 2 + 1)
                            if c == NT:
                                act.wait_ge(st_v, 1 + 16 * i)
                            if c < NT:
                                act.activation(qk[:, t, :], Z[c % 2][:, 0:CW], ACT.Copy).then_inc(z_free[c % 2], 1)
                            else:
                                act.activation(vg[:, :, t, :], Z[c % 2][:, 0:CW].rearrange("p (a d) -> p a d", d=HD), ACT.Copy).then_inc(z_free[c % 2], 1)
                            if c + 1 == TURN_AT:
                                act.wait_ge(st_o, 1 + 16 * i)
                                for j in range(2):
                                    act.wait_ge(s_full[j], (12, 11)[j] * i + 1)
                                    act.activation(qkT[:, j, :], S[j][:, :], ACT.Copy).then_inc(s_free[j], 1)
                            if c == SOFTMAX_AT[1] + 1:
                                act.wait_ge(d_sub, 1 + i + 1)
                                act.activation(ex[:, :, :], ex[:, :, :], ACT.Exp, scale=SC_A).then_inc(a_e, 1)
                            for h in range(NI):
                                if INDEX_AT[h] == c + 1:
                                    act.wait_ge(s_full[h % 2], (12, 11)[h % 2] * i + h // 2 + 2)
                                    act.activation(S[h % 2][:, 0:width], S[h % 2][:, 0:width], ACT.Relu).then_inc(a_rl, 1)

                        def squares(t):
                            act.wait_ge(z_free[t % 2], 1 + 12 * i + 8 + t // 2 + 1)
                            if t:
                                act.wait_ge(a_ss, NT * i + t)
                            act.activation(sqs, onat[:, t, :], ACT.Square, accum_out=ss8[:, t:t + 1]).then_inc(a_ss, 1)

                        for t in range(NT):
                            n = (t + 1) * P
                            act.wait_ge(d_nm, NT * i + t + 1)
                            act.wait_ge(t_full, 1 + NF * i + F(t))
                            for j in range(2):
                                x = act.activation(e12[:, j, 0:n], S[j][:, 0:n], ACT.Exp, scale=SC_A, bias=nmx[:, t, j:j + 1],
                                                   accum_out=rsum[:, t, j:j + 1])
                                x.then_inc(s_free[j], 1)
                            act.wait_ge(s_free[1], 1 + 11 * i + 4 + t)
                            act.nop().then_inc(a_x, 1)
                            if t == 0:
                                for b in range(2):
                                    act.wait_ge(z_free[b], 1 + 12 * i + 8)
                                act.wait_ge(st_k, 1 + 16 * i + 16)
                                act.activation(sig, g_sb, ACT.Sigmoid).then_inc(a_eg, 1)
                            for f in range(F(t + 1) - F(t)):
                                act.wait_ge(t_full, 1 + NF * i + F(t) + f + 1)
                                if f == 0:
                                    if t:
                                        act.wait_ge(z_full[(t - 1) % 2], 12 * i + 8 + (t - 1) // 2 + 1)
                                nb = min(4, t + 1 - 4 * f)
                                act.activation(pTf[:, 512 * f:512 * f + nb * P], TB[:, 0:nb * P], ACT.Copy).then_inc(t_free, 1)
                            if t:
                                squares(t - 1)
                        squares(NT - 1)
                        act.wait_ge(a_ss, NT * i + NT)
                        act.activation(ss8, ss8, ACT.Sqrt, scale=1.0 / HD, bias=eps).then_inc(a_sq, 1)
                        act.wait_ge(s_full[0], 12 * i + 12)
                        act.activation(qkT[:, 0, :], S[0][:, :], ACT.Copy).then_inc(s_free[0], 1)
                        act.wait_ge(s_free[0], 1 + 12 * i + 12)
                        act.dma_start(oT_d[ds(i, 1), :, :].rearrange("o p t -> (o p) t"), qkT[:, 0, :]).then_inc(st_o, 16)
                act.wait_ge(st_o, 1 + 16 * HA)

            @block.vector
            def _(dve):
                dve.wait_ge(x_in, 17)
                dve.tensor_scalar(subw[:, :], subw[:, :], 1.0 - LAM_INIT, None, ALU.mult).then_inc(x_in, 1)
                dve.wait_ge(x_in, 18)
                for first, end, width in SPANS:
                    with dve.Fori(first, end) as i:
                        link = Chain(dve, d_ch, clear=True)
                        seen = work[:, 0:width]
                        dve.wait_ge(b_in, 32 * i + 32)
                        dve.wait_ge(g_si, 1 + i)

                        def page_sum(p):
                            dve.wait_ge(k_used[p % 4], 1 + 8 * i + p // 4 + 1)
                            return dve.tensor_reduce(sc[:, p, :], prods[p % 2].rearrange("p (g d) -> p g d", d=64), AX.X, ALU.add)

                        def index_sum(u):
                            j, h = u // NI, u % NI
                            dve.wait_ge(q_rdy[u % 2], 16 * i + u // 2 + 1)
                            dve.tensor_reduce(srel[:, 4 * j:4 * j + 4, h], kprod[:, u % 2, :, :], AX.X, ALU.add).then_inc(q_free[u % 2], 1)

                        for p in range(NPG):
                            dve.wait_ge(k_rdy[p % 4], 16 * (8 * i + p // 4 + 1))
                            if p >= 2:
                                dve.wait_ge(d_ps, (NPG - 1) * i + p - 1)
                            if p % 4 != 3:
                                dve.tensor_tensor(prods[p % 2], ring_k[p % 4], qb[:, :], ALU.mult).then_inc(k_used[p % 4], 1)
                            if p:
                                page_sum(p - 1).then_inc(d_ps, 1)
                                index_sum(p - 1)
                            if p == ROPE_AT:
                                for b in range(2):
                                    dve.wait_ge(z_free[b], 1 + 12 * i + 4)
                                rope(link, z4, tuple(spread(ropa[:, :, a, :], 2, 4) for a in (0, 1)),
                                     *[e12[:, 1, a * 512:(a + 1) * 512].rearrange("p (t g r) -> p t g r", g=4, r=16) for a in (0, 1)], 16)
                                dve.nop().then_inc(d_rot, 1)
                        index_sum(NPG - 1)
                        page_sum(NPG - 1).then_inc(d_red, 1)
                        dve.wait_ge(d_red, i + 1)
                        link(dve.tensor_reduce(m16, sc[:, :, :].rearrange("p n h -> p h n"), AX.X, ALU.max))
                        dve.nop().then_inc(d_m, 1)
                        link(dve.tensor_copy(wic, wall[:, ds(i, 1), :].rearrange("p o h -> p (o h)")))
                        dve.wait_ge(t_in, 16 * i + 16)
                        for h in range(NI):
                            dve.wait_ge(a_rl, NI * i + h + 1)
                            dve.scalar_tensor_tensor(out=seen, in0=S[h % 2][:, 0:width], scalar=wic[:, h:h + 1], in1=seen,
                                                     op0=ALU.mult, op1=ALU.add).then_inc(s_free[h % 2], 1)
                            dve.wait_ge(s_free[h % 2], 1 + (12, 11)[h % 2] * i + h // 2 + 2)
                        link(dve.memset(top8, 0.0))

                        def take(rounds):
                            for r in range(rounds):
                                link(dve.max(top8, seen))
                                link(dve.match_replace(out=seen, in_to_replace=top8, in_values=seen, imm_value=TAKEN))

                        dve.wait_ge(p_m, 1 + 5 * i + 1)
                        link(dve.tensor_reduce(mm1, DB[0:16, 256:384], AX.X, ALU.max))
                        link(dve.tensor_scalar(dg16, ident[0:16, 0:16], mm1, None, ALU.mult))
                        dve.nop().then_inc(d_m, 1)
                        take(3)
                        dve.wait_ge(p_m, 1 + 5 * i + 2)
                        dve.tensor_tensor(ex[:, :, :], sc[:, :, :], spread(DB[:, 384:400], 1, NPG + 1), ALU.subtract).then_inc(d_sub, 1)
                        take(3)
                        dve.wait_ge(a_e, i + 1)
                        dve.tensor_reduce(es16, ex[:, :, :].rearrange("p n h -> p h n"), AX.X, ALU.add).then_inc(d_es, 1)
                        take(ROUNDS[0] - 6)
                        def maxima(t):
                            n = (t + 1) * P
                            for j in range(2):
                                dve.wait_ge(s_full[j], (12, 11)[j] * i + 4 + t)
                                last = dve.tensor_reduce(mx[:, t, j:j + 1], S[j][:, 0:n], AX.X, ALU.max)
                            link(last)
                            dve.tensor_scalar(nmx[:, t, :], mx[:, t, :], -SC_A, None, ALU.mult).then_inc(d_nm, 1)

                        def natural(t):
                            dve.wait_ge(z_full[t % 2], 12 * i + 8 + t // 2 + 1)
                            dve.tensor_scalar(onat[:, t, :], Z[t % 2][:, 0:HD], rrec[:, t, 0:1], None, ALU.mult).then_inc(z_free[t % 2], 1)

                        def sample_products():
                            dve.wait_ge(d_p, NT * i + NT)
                            link(dve.memset(od, 0.0))
                            dve.wait_ge(p_m, 1 + 5 * i + 4)
                            for g in range(4):
                                last = dve.tensor_copy(od[32 * g:32 * g + 4, :], DB[32 * g:32 * g + 4, 0:256])
                            last.then_inc(d_od, 1)

                        maxima(0)
                        dve.wait_ge(p_m, 1 + 5 * i + 3)
                        for g in range(4):
                            last = dve.tensor_copy(den[32 * g:32 * g + 4, :], TB[32 * g:32 * g + 4, 0:1])
                        link(last)
                        link(dve.reciprocal(cc[:, 0:1], den))
                        link(dve.tensor_scalar(coef, coefm[:, :], cc[:, 0:1], None, ALU.mult))
                        for t in range(NT):
                            n = (t + 1) * P
                            dve.wait_ge(a_x, NT * i + t + 1)
                            link(dve.reciprocal(rrec[:, t, :], rsum[:, t, :]))
                            link(dve.scalar_tensor_tensor(out=cc[:, t:t + 1], in0=rsum[:, t, 0:1], scalar=rrec[:, t, 1:2],
                                                          in1=lam[:, 0:1], op0=ALU.mult, op1=ALU.mult))
                            dve.scalar_tensor_tensor(out=e12[:, 0, 0:n], in0=e12[:, 1, 0:n], scalar=cc[:, t:t + 1],
                                                     in1=e12[:, 0, 0:n], op0=ALU.mult, op1=ALU.add).then_inc(d_p, 1)
                            if t:
                                natural(t - 1)
                            if t == 1:
                                dve.wait_ge(a_eg, i + 1)
                                link(dve.tensor_tensor(g_sb, g_sb, sig, ALU.mult))
                            if t == 2:
                                link(dve.tensor_tensor(g_sb, g_sb, spread(subw[:, :], 1, NT), ALU.mult))
                            if t + 1 < NT:
                                take(1)
                                maxima(t + 1)
                                take(ROUNDS[t + 1] - 1)
                            else:
                                sample_products()
                                take(ROUNDS[NT])
                        natural(NT - 1)
                        for b in range(2):
                            dve.wait_ge(z_free[b], 1 + 12 * i + 12)
                        link(dve.tensor_tensor(g_sb, g_sb, onat, ALU.mult))
                        dve.wait_ge(a_sq, 1 + i + 1)
                        link(dve.reciprocal(ss8, ss8))
                        dve.tensor_tensor(g_sb, g_sb, spread(ss8, 2, HD), ALU.mult).then_inc(d_og, 1)
                        dve.wait_ge(p_m, 1 + 5 * i + 5)
                        for j in range(2):
                            last = dve.tensor_copy(odec[:, j:HA:2, ds(i, 1)].rearrange("p h o -> p (h o)"), DB[:, 408 + 4 * j:412 + 4 * j])
                        link(last)
                        dve.tensor_scalar(bias[:, ds(i * BS, width)], seen, TAKEN / 2, NEG,
                                          ALU.is_gt, ALU.mult).then_inc(d_top, 1)
                        dve.wait_ge(d_top, i + 1)

            @block.tensor
            def _(pe):
                for first, end, width in SPANS:
                    with pe.Fori(first, end) as i:
                        def project(c):
                            s, t = c // NT, c % NT
                            if t == 0:
                                pe.wait_ge(w_rdy[s], 32 * i + 32)
                            pe.wait_ge(z_free[c % 2], 1 + 12 * i + c // 2)
                            for k in range(KT):
                                mm = pe.matmul(Z[c % 2][:, 0:CW], hT[:, k, t * P:(t + 1) * P], W[:, s, k, :],
                                               start=(k == 0), stop=(k == KT - 1))
                            mm.then_inc(z_full[c % 2], 1)
                            if t == NT - 1:
                                pe.wait_ge(z_full[c % 2], 12 * i + c // 2 + 1)
                                pe.nop().then_inc(w_used[s], 1)

                        def index(h):
                            j, r = h % 2, 64 * (h % 2)
                            if h == 0:
                                pe.wait_ge(qt_in, 16 * i + 16)
                            pe.wait_ge(s_free[j], 1 + (12, 11)[j] * i + 1 + h // 2)
                            for lo in range(0, width, 512):
                                mm = pe.matmul(S[j][:, lo:lo + 512], qit[r:r + 64, h // 2, :], kiT[r:r + 64, lo:lo + 512], start=True, stop=True)
                            mm.then_inc(s_full[j], 1)

                        for c in range(2 * NT):
                            if c == TURN_AT:
                                pe.wait_ge(d_rot, i + 1)
                                for j in range(2):
                                    pe.wait_ge(s_free[j], 1 + (12, 11)[j] * i)
                                    for t in range(NT):
                                        mm = pe.transpose(S[j][:, t * P:(t + 1) * P], qk[:, t, j * HD:(j + 1) * HD], ident[:, :])
                                    mm.then_inc(s_full[j], 1)
                            for h in range(NI):
                                if INDEX_AT[h] == c:
                                    index(h)
                            if c == SOFTMAX_AT[0]:
                                pe.wait_ge(d_m, 2 * i + 1)
                                pe.transpose(DB[0:16, 256:384], m16, ident[:, :]).then_inc(p_m, 1)
                            if c == SOFTMAX_AT[1]:
                                pe.wait_ge(d_m, 2 * i + 2)
                                pe.matmul(DB[:, 384:400], ones[0:16, :], dg16, start=True, stop=True).then_inc(p_m, 1)
                            project(c)
                        for j in range(2):
                            pe.wait_ge(s_full[j], (12, 11)[j] * i + 3)
                        pe.nop().then_inc(p_idx, 1)

                        def values(v):
                            if v < NPG:
                                pe.wait_ge(v_rdy[v % 4], 16 * (8 * i + v // 4 + 1))
                            else:
                                pe.wait_ge(vn_in, 16 * i + 16)
                            page = ring_v[v % 4] if v < NPG else vnew[:, :]
                            for g in range(4):
                                mm = pe.matmul(DB[32 * g:32 * g + 4, 0:256], ex[:, v, 4 * g:4 * g + 4], page[:, 256 * g:256 * g + 256],
                                               start=(v == 0), stop=(v == NPG))
                            if v < NPG:
                                mm.then_inc(v_used[v % 4], 1)
                            else:
                                mm.then_inc(p_m, 1)

                        def scores(t):
                            n = (t + 1) * P
                            for j in range(2):
                                pe.wait_ge(s_free[j], 1 + (12, 11)[j] * i + 3 + t)
                                for lo, hi in key_spans(t):
                                    pe.matmul(S[j][:, lo:hi], qkT[64 * j:64 * j + 64, 0, t * P:n], qkT[64 * j:64 * j + 64, 1, lo:hi],
                                              start=True, stop=(hi < n))
                                pe.matmul(S[j][:, t * P:n], identb[:, :], causal[:, :], start=False, stop=True).then_inc(s_full[j], 1)

                        for j in range(2):
                            pe.wait_ge(s_free[j], 1 + (12, 11)[j] * i + 3)
                        scores(0)
                        pe.wait_ge(d_es, i + 1)
                        for g in range(4):
                            mm = pe.matmul(TB[32 * g:32 * g + 4, 0:1], es16[:, 4 * g:4 * g + 4], ones[:, 0:1], start=True, stop=True)
                        mm.then_inc(p_m, 1)
                        for v in range(4):
                            values(v)
                        for t in range(NT):
                            if t + 1 < NT:
                                for v in range(4 * t + 4, 4 * t + 8):
                                    values(v)
                                scores(t + 1)
                            else:
                                values(NPG)
                            pe.wait_ge(d_p, NT * i + t + 1)
                            for f in range(F(t + 1) - F(t)):
                                pe.wait_ge(t_free, 1 + NF * i + F(t) + f)
                                for b in range(min(4, t + 1 - 4 * f)):
                                    mm = pe.transpose(TB[:, b * P:(b + 1) * P], e12[:, 0, (4 * f + b) * P:(4 * f + b + 1) * P], ident[:, :])
                                mm.then_inc(t_full, 1)
                            pe.wait_ge(z_free[t % 2], 1 + 12 * i + 8 + t // 2)
                            pe.wait_ge(t_free, 1 + NF * i + F(t + 1))
                            for b in range(t + 1):
                                mm = pe.matmul(Z[t % 2][:, 0:HD], pT[:, b, :], v_sb[:, b, :], start=(b == 0), stop=(b == t))
                            mm.then_inc(z_full[t % 2], 1)
                        pe.wait_ge(d_od, i + 1)
                        for j in range(2):
                            mm = pe.matmul(DB[:, 408 + 4 * j:412 + 4 * j], od[:, j * P:(j + 1) * P], coef[:, j:HA:2], start=True, stop=True)
                        mm.then_inc(p_m, 1)
                        pe.wait_ge(d_og, 1 + i + 1)
                        pe.wait_ge(s_free[0], 1 + 12 * i + 11)
                        for t in range(NT):
                            mm = pe.transpose(S[0][:, t * P:(t + 1) * P], g_sb[:, t, :], ident[:, :])
                        mm.then_inc(s_full[0], 1)

        end_stage()

        NS = NPG + 1
        Wf = W[:, :, :, :].rearrange("p a b c -> p (a b c)")
        kg = Wf[:, 4096:8192].rearrange("p (b f c) -> p b f c", b=NB, f=2)
        vgt = Wf[:, 0:4096].rearrange("p (b f c) -> p b f c", b=NB, f=2)
        at = [0]

        def take_big(n, dt=F32):
            words = n if dt != BF16 else n // 2
            a = big[:, at[0]:at[0] + words]
            at[0] += words
            return a if dt == F32 else a.bitcast(dt)

        cmpm, eqm, rkm, pre, tot = (take_big(NB * NS) for _ in range(5))
        reset = take_big(NB * NS)
        below = take_big(P)
        iotaj = take_big(TOPK)
        oneh = take_big(4 * TOPK, BF16).rearrange("p (s j) -> p s j", s=4)
        ids = take_big(2 * NB * NPG, BF16).rearrange("p (n q) -> p n q", q=2)
        idi, idi2 = take_big(NB * NPG, I32), take_big(NB * NPG, I32)
        ab = take_big(TOPK)[0:2, :]
        idx = take_big(2 * NB, U32)
        idxf = take_big(2 * 2 * NB).rearrange("p (f b q) -> p f b q", f=2, b=NB)
        ssb = take_big(TOPK + 8)[0:64, :]
        ptb = take_big(2 * 64).rearrange("p (f n) -> p f n", f=2)
        st_sb = take_big(128)
        d64 = take_big(64)[0:64, :]
        pbc = take_big(64)
        sqa = take_big(64)
        ktb = e12[:, :, 0:512]
        kTb = big[:, 0:2048]
        rtmpk = [big[:, 2048:2560], big[:, 2560:3072]]
        ropb = big[:, 4608:5120].rearrange("p (t a r) -> p t a r", t=NT, a=2)
        vb = big[:, 5120:7168].rearrange("p (t c) -> p t c", c=2 * HD)
        kq = qkT[:, :, :].rearrange("p a (b c) -> p (a b) c", c=2 * HD)
        assert at[0] <= 4608 - 64
        three = lambda a: a.rearrange("p (b n) -> p b n", b=NB)
        s8 = lambda lo, n=NB, dt=F32: small[:, 192 + lo:192 + lo + n].bitcast(dt) if dt != F32 else small[:, 192 + lo:192 + lo + n]
        prefix, biti, mflip, thr, acci = s8(0, dt=I32), s8(8, dt=I32), s8(16, dt=I32), s8(24, dt=I32), s8(32, dt=I32)
        bitf, cnt, need, selx, gef = s8(40), s8(48), s8(56), s8(64), s8(72)
        rmax, rsm, own, pex, subc = small[0:64, 280:281], small[0:64, 281:282], small[0:64, 282:283], small[0:64, 283:284], small[:, 284:285]
        x64 = take_big(64)[0:1, :]
        snew_b_d = dram("snew_b_d", [NB, HB])
        ska, sva = (a.rearrange("l n p h d -> (l n p) (h d)") for a in (cache_sk, cache_sv))

        b_in = sem("b_in")
        b_st = sem("b_st")
        b_cst = sem("b_cst")
        b_ch = sem("b_ch")
        b_gch = sem("b_gch")
        b_cnt = sem("b_cnt")
        b_tot = sem("b_tot")
        b_eq = sem("b_eq")
        b_pre = sem("b_pre")
        b_oh = sem("b_oh")
        b_ohu = sem("b_ohu")
        b_ab = sem("b_ab")
        b_abc = sem("b_abc")
        b_abt = sem("b_abt")
        b_idx = sem("b_idx")
        b_k, b_v = [sem(f"b_k{j}") for j in range(NB)], [sem(f"b_v{j}") for j in range(NB)]
        b_kt = sem("b_kt")
        b_ktc = sem("b_ktc")
        b_s = sem("b_s")
        b_sc = sem("b_sc")
        b_s2 = sem("b_s2")
        b_e = sem("b_e")
        b_p = sem("b_p")
        b_pt = sem("b_pt")
        b_o = sem("b_o")
        c_in = sem("c_in")
        c_z = [sem("c_z0"), sem("c_z1")]
        c_zf = [sem("c_zf0"), sem("c_zf1")]
        c_rot = sem("c_rot")
        c_t = sem("c_t")
        c_tc = sem("c_tc")
        c_st = sem("c_st")
        g_w = sem("g_w")
        g_z = [sem("g_z0"), sem("g_z1")]
        g_zf = [sem("g_zf0"), sem("g_zf1")]
        g_w1 = sem("g_w1")
        GB = [Z[0], S[1]]
        b_q = sem("b_q")
        b_qs = sem("b_qs")

        with nc.Block() as block:
            @block.sync
            def _(sp):
                sp.dma_start(idi, page_table.rearrange("b n -> (b n)").partition_broadcast(P)).then_inc(b_in, 16)
                sp.dma_start(snew_b_d, snb).then_inc(b_st, 16)
                sp.wait_ge(b_st, 16)
                sp.dma_start(own, snew_b_d.rearrange("b h -> (b h)").unsqueeze(1), allow_slow_non_contiguous=True).then_inc(b_in, 16)
                sp.dma_start(ropb, rope_b.rearrange("(t p) a r -> p t a r", p=P)).then_inc(c_in, 16)

                def weights(u, signal):
                    for q, lo in enumerate((QS, GS)):
                        sp.dma_start(W[:, u, :, q * HD:(q + 1) * HD], win[:, :, u * HD + lo:u * HD + lo + HD]).then_inc(signal, 16)

                for s in range(2):
                    sp.wait_ge(c_z[s], NT // 2)
                weights(0, g_w)
                for s in range(2):
                    sp.wait_ge(c_zf[s], NT)
                sp.dma_start(sv_p.rearrange("l b (t p) h d -> p (l b t) (h d)", p=P), vb).then_inc(c_st, 16)
                sp.wait_ge(c_rot, 1)
                sp.dma_start(sk_p.rearrange("l b (t p) h d -> p (l b t) (h d)", p=P), kq).then_inc(c_st, 16)
                sp.wait_ge(b_kt, NB)
                weights(1, g_w1)
                sp.wait_ge(c_st, 32)
                sp.wait_ge(g_w1, 32)

            @block.gpsimd
            def _(pool):
                link = Chain(pool, b_gch)
                pool.iota(iotaj, pattern=[[1, TOPK]], base=0, channel_multiplier=0, allow_small_or_imprecise_dtypes=True)
                pool.iota(idi2, pattern=[[0, NB * NPG]], base=0, channel_multiplier=1)
                link(pool.memset(reset, 1.0))
                link(pool.memset(three(reset)[:, :, 0:1], 0.0))
                link(pool.memset(below, 1.0))
                pool.affine_select(out=below, in_=below, compare_op=ALU.is_gt, fill=0.0, base=0, pattern=[[1, P]],
                                   channel_multiplier=-1).then_inc(b_cst, 1)
                for b in range(NB):
                    if b == 0:
                        pool.wait_ge(b_idx, 1)
                        for s in range(2):
                            pool.wait_ge(c_z[s], NT)
                            pool.wait_ge(g_z[s], NT // 2)
                    for f in range(2):
                        on = bass.IndirectOffsetOnAxis(ap=idx[:, f * NB + b:f * NB + b + 1], axis=0)
                        pool.indirect_dma_start(out=kg[:, b, f, :], out_offset=None, in_=ska, in_offset=on,
                                                bounds_check=POOL * P - 1, oob_is_err=False).then_inc(b_k[b], 16)
                        pool.indirect_dma_start(out=vgt[:, b, f, :], out_offset=None, in_=sva, in_offset=on,
                                                bounds_check=POOL * P - 1, oob_is_err=False).then_inc(b_v[b], 16)

            @block.vector
            def _(dve):
                link = Chain(dve, b_ch)
                siv = si[:, :, :]
                dve.wait_ge(b_cst, 1)
                dve.wait_ge(b_in, 32)
                link(dve.tensor_scalar(idi, idi, P, None, ALU.mult))
                link(dve.tensor_tensor(idi2, idi, idi2, ALU.add))
                link(dve.tensor_scalar(idi, idi2, 255, None, ALU.bitwise_and))
                link(dve.tensor_scalar(idi2, idi2, 8, None, ALU.logical_shift_right))
                link(dve.tensor_copy(ids[:, :, 0], idi2))
                link(dve.tensor_copy(ids[:, :, 1], idi))

                def count(n, thr_ap, op):
                    link(dve.tensor_tensor(three(cmpm), siv, thr_ap, op))
                    dve.tensor_reduce(cnt, three(cmpm), AX.X, ALU.add).then_inc(b_cnt, 1)
                    dve.wait_ge(b_tot, n)

                link(dve.memset(thr, 0))
                wide = lambda a: spread(a, 2, NS)
                count(1, wide(thr.bitcast(F32)), ALU.is_ge)
                link(dve.tensor_scalar(mflip, TB[:, 0:NB], TOPK - 0.5, -1.0, ALU.is_lt, ALU.mult))
                link(dve.memset(prefix, 0))
                link(dve.memset(bitf, float(2 ** 30)))
                link(dve.tensor_copy(biti, bitf))
                with dve.Fori(0, 31) as r:
                    inner = Chain(dve, b_ch, clear=True)
                    inner(dve.tensor_tensor(thr, prefix, biti, ALU.bitwise_or))
                    inner(dve.tensor_tensor(thr, thr, mflip, ALU.bitwise_xor))
                    inner(dve.tensor_tensor(three(cmpm), siv, wide(thr.bitcast(F32)), ALU.is_ge))
                    dve.tensor_reduce(cnt, three(cmpm), AX.X, ALU.add).then_inc(b_cnt, 1)
                    dve.wait_ge(b_tot, r + 2)
                    inner(dve.scalar_tensor_tensor(out=acci, in0=TB[:, 0:NB], scalar=TOPK - 0.5, in1=bitf, op0=ALU.is_ge, op1=ALU.mult))
                    inner(dve.tensor_tensor(prefix, prefix, acci, ALU.bitwise_or))
                    inner(dve.tensor_scalar(bitf, bitf, 0.5, None, ALU.mult))
                    inner(dve.tensor_copy(biti, bitf))
                link = Chain(dve, b_ch, clear=True)
                link(dve.tensor_tensor(thr, prefix, mflip, ALU.bitwise_xor))
                tf = wide(thr.bitcast(F32))
                link(dve.tensor_tensor(three(eqm), siv, tf, ALU.is_equal))
                link(dve.tensor_tensor(three(cmpm), siv, tf, ALU.is_gt))
                dve.tensor_reduce(cnt, three(cmpm), AX.X, ALU.add).then_inc(b_cnt, 1)
                dve.wait_ge(b_tot, 33)
                link(dve.tensor_scalar(need, TB[:, 0:NB], -1.0, float(TOPK), ALU.mult, ALU.add))
                dve.nop().then_inc(b_eq, 1)

                def ranks(n, m):
                    dve.wait_ge(b_pre, n)
                    link(dve.tensor_copy(pre, S[0][:, 512:512 + NB * NS]))
                    link(dve.tensor_tensor_scan(out=tot, data0=reset, data1=pre, initial=0.0, op0=ALU.mult, op1=ALU.add))
                    link(dve.tensor_tensor(tot, tot, pre, ALU.subtract))
                    link(dve.tensor_tensor(pre, tot, S[0][:, 0:NB * NS], ALU.add))

                ranks(1, eqm)
                link(dve.tensor_tensor(three(rkm), three(pre), wide(need), ALU.is_lt))
                link(dve.tensor_tensor(eqm, eqm, rkm, ALU.mult))
                link(dve.tensor_tensor(eqm, eqm, cmpm, ALU.add))
                dve.nop().then_inc(b_eq, 1)
                link(dve.tensor_copy(x64.rearrange("p (b h) -> p b h", h=HB), spread(three(eqm)[0:1, :, NPG], 2, HB)))
                dve.nop().then_inc(b_eq, 1)
                ranks(2, eqm)
                link(dve.scalar_tensor_tensor(out=rkm, in0=pre, scalar=1.0, in1=eqm, op0=ALU.add, op1=ALU.mult))
                link(dve.tensor_scalar(rkm, rkm, -1.0, None, ALU.add))
                rk3 = three(rkm)
                for b in range(NB):
                    for n in range(NPG):
                        u = b * NPG + n
                        if u >= 4:
                            dve.wait_ge(b_ohu, u - 3)
                        dve.tensor_scalar(oneh[:, u % 4, :], iotaj, rk3[:, b, n:n + 1], None, ALU.is_equal).then_inc(b_oh, 1)
                dve.wait_ge(b_abt, NB)
                link(dve.tensor_copy(idxf.rearrange("p f b q -> p (f b q)"), TB[:, 0:32]))
                link(dve.scalar_tensor_tensor(out=idx.rearrange("p (f b) -> p f b", f=2), in0=idxf[:, :, :, 0], scalar=256.0,
                                              in1=idxf[:, :, :, 1], op0=ALU.mult, op1=ALU.add))
                dve.nop().then_inc(b_idx, 1)
                dve.wait_ge(c_in, 16)
                for s in range(2):
                    dve.wait_ge(c_zf[s], NT // 2)
                rope(link, kq.rearrange("p t (g d) -> p t g d", g=2), tuple(spread(ropb[:, :, a, :], 2, 2) for a in (0, 1)),
                     *[a.rearrange("p (t g r) -> p t g r", g=2, r=32) for a in rtmpk], 32)
                dve.nop().then_inc(c_rot, 1)
                dve.wait_ge(b_s, NB)
                dve.tensor_copy(st_sb, Z[0][:, 0:128]).then_inc(b_sc, 1)
                dve.wait_ge(b_s2, 1)
                link(dve.tensor_copy(ssb[:, 0:TOPK], Z[1][0:64, 0:TOPK]))
                link(dve.tensor_copy(pex, Z[1][0:64, 256:257]))
                link(dve.scalar_tensor_tensor(out=ssb[:, 255:256], in0=pex, scalar=NEG, in1=ssb[:, 255:256], op0=ALU.mult, op1=ALU.add))
                link(dve.tensor_scalar(rmax, pex, -NEG, NEG, ALU.mult, ALU.add))
                link(dve.tensor_tensor(ssb[:, 256:257], own, rmax, ALU.add))
                link(dve.tensor_reduce(rmax, ssb[:, 0:257], AX.X, ALU.max))
                link(dve.tensor_scalar(rmax, rmax, -SC_B, None, ALU.mult))
                dve.nop().then_inc(b_sc, 1)
                dve.wait_ge(b_e, 1)
                link(dve.reciprocal(rsm, rsm))
                link(dve.tensor_scalar(ssb[:, 0:257], ssb[:, 0:257], rsm, None, ALU.mult))
                link(dve.tensor_scalar(d64, ident[0:64, 0:64], ssb[:, 256:257], None, ALU.mult))
                dve.nop().then_inc(b_p, 1)
                dve.wait_ge(b_pt, 1)
                link(dve.tensor_copy(ptb.rearrange("p f n -> p (f n)"), TB[:, 0:128]))
                link(dve.tensor_copy(pbc, TB[:, 128:192]))
                dve.nop().then_inc(b_p, 1)
                dve.wait_ge(b_o, 1)
                for n in range(HKV):
                    ob = odec[:, HA + 4 * n:HA + 4 * n + 4, 0:NB].rearrange("p h b -> p b h")
                    pb = pbc.rearrange("p (b h) -> p b h", h=HB)[:, :, 4 * n:4 * n + 4]
                    link(dve.tensor_tensor(ob, pb, spread(gsT[:, 24 + n, :], 2, 4), ALU.mult))
                    link(dve.tensor_tensor(ob, ob, Z[0][:, 0:64].rearrange("p (b h) -> p b h", h=HB)[:, :, 4 * n:4 * n + 4], ALU.add))
                link(dve.tensor_tensor(odec[:, HA:16, 0:NB], odec[:, HA:16, 0:NB], gsT[:, HA:16, :], ALU.mult))
                oa = odec[:, 0:HA, 0:NB]
                sq3 = sqa.rearrange("p (h b) -> p h b", h=HA)
                link(dve.tensor_tensor(sq3, oa, oa, ALU.mult))
                dve.nop().then_inc(b_q, 1)
                dve.wait_ge(b_qs, 1)
                link(dve.tensor_copy(subc, TB[:, 300:301]))
                link(dve.reciprocal(sqa, sqa))
                link(dve.scalar_tensor_tensor(out=oa, in0=oa, scalar=subc, in1=sq3, op0=ALU.mult, op1=ALU.mult))
                link(dve.tensor_tensor(oa, oa, gsT[:, 0:HA, :], ALU.mult))

            @block.scalar
            def _(act):
                for c in range(2 * NT):
                    act.wait_ge(c_z[c % 2], c // 2 + 1)
                    dst = kq[:, c % NT, :] if c < NT else vb[:, c % NT, :]
                    act.activation(dst, Z[c % 2][:, 0:CW], ACT.Copy).then_inc(c_zf[c % 2], 1)
                for b in range(NB):
                    act.wait_ge(b_ab, b + 1)
                    act.activation(ab, DB[0:2, 0:TOPK] if b % 2 == 0 else Z[1][0:2, 0:TOPK], ACT.Copy).then_inc(b_abc, 1)
                    act.wait_ge(g_z[b % 2], b // 2 + 1)
                    act.activation(qk[:, b, 0:HD], GB[b % 2][:, 0:HD], ACT.Copy)
                    act.activation(vg[:, 0, b, :], GB[b % 2][:, HD:CW], ACT.Copy).then_inc(g_zf[b % 2], 1)
                    if b + 1 < NB:
                        act.wait_ge(b_abt, b + 1)
                for n in range(HKV):
                    act.wait_ge(c_t, n + 1)
                    act.activation(kTb[:, n * T:(n + 1) * T], S[n][:, :], ACT.Copy).then_inc(c_tc, 1)
                for b in range(NB):
                    act.wait_ge(b_kt, b + 1)
                    if b >= 2:
                        act.wait_ge(b_s, b - 1)
                    act.activation(ktb[:, b % 2, :], S[b % 2][:, 0:512], ACT.Copy).then_inc(b_ktc, 1)
                act.wait_ge(b_sc, 2)
                act.activation(ssb[:, 0:257], ssb[:, 0:257], ACT.Exp, scale=SC_B, bias=rmax, accum_out=rsm).then_inc(b_e, 1)
                act.wait_ge(b_o, 2)
                act.activation(sqa, TB[:, 192:256], ACT.Sqrt, scale=1.0 / HD, bias=eps).then_inc(b_qs, 1)

            @block.tensor
            def _(pe):
                def half_tile(c, f):
                    if f == 0 and c >= 2:
                        pe.wait_ge(c_zf[c % 2], c // 2)
                    for k in range(8 * f, 8 * f + 8):
                        mm = pe.matmul(Z[c % 2][:, 0:CW], hT[:, k, (c % NT) * P:(c % NT + 1) * P], W[:, c // NT, k, :],
                                       start=(k == 0), stop=(k == KT - 1))
                    if f:
                        mm.then_inc(c_z[c % 2], 1)

                for n in range(33):
                    pe.wait_ge(b_cnt, n + 1)
                    pe.matmul(TB[:, 0:NB], ones[:, :], cnt, start=True, stop=True).then_inc(b_tot, 1)
                    if n < 4 * NT:
                        half_tile(n // 2, n % 2)
                for n in range(2):
                    pe.wait_ge(b_eq, n + 1)
                    pe.matmul(S[0][:, 0:NB * NS], below, eqm, start=True, stop=True)
                    pe.matmul(S[0][:, 512:512 + NB * NS], ones[:, :], eqm, start=True, stop=True).then_inc(b_pre, 1)
                pe.wait_ge(g_w, 32)
                for s in range(2):
                    pe.wait_ge(c_zf[s], NT)
                for b in range(NB):
                    dst = DB if b % 2 == 0 else Z[1]
                    if b >= 2:
                        pe.wait_ge(g_zf[b % 2], b // 2)
                    for n in range(NPG):
                        u = b * NPG + n
                        pe.wait_ge(b_oh, u + 1)
                        mm = pe.matmul(dst[0:2, 0:TOPK], ids[:, u, :], oneh[:, u % 4, :], start=(n == 0), stop=(n == NPG - 1))
                        mm.then_inc(b_ohu, 1)
                        if n % 2 == 0:
                            k = n // 2
                            mm = pe.matmul(GB[b % 2][:, 0:CW], hT[:, k, b * P:(b + 1) * P], W[:, 0, k, :], start=(k == 0), stop=(k == KT - 1))
                            if k == KT - 1:
                                mm.then_inc(g_z[b % 2], 1)
                    pe.wait_ge(b_ohu, (b + 1) * NPG)
                    pe.nop().then_inc(b_ab, 1)
                    pe.wait_ge(b_abc, b + 1)
                    for f in range(2):
                        mm = pe.transpose(TB[:, 2 * (f * NB + b):2 * (f * NB + b) + 2], ab[:, f * P:(f + 1) * P], ident[0:2, 0:2])
                    mm.then_inc(b_abt, 1)

                def row_scores(b):
                    pe.wait_ge(b_ktc, b + 1)
                    for f in range(2):
                        for n in range(HKV):
                            mm = pe.matmul(Z[0][:, f * 64 + b * HB + 4 * n:f * 64 + b * HB + 4 * n + 4],
                                           ktb[:, b % 2, (2 * f + n) * P:(2 * f + n + 1) * P],
                                           gsT[:, 16 + 4 * n:20 + 4 * n, b], start=True, stop=True)
                    mm.then_inc(b_s, 1)

                pe.wait_ge(c_rot, 1)
                for s in range(2):
                    pe.wait_ge(g_zf[s], NT // 2)
                for n in range(HKV):
                    for t in range(NT):
                        mm = pe.transpose(S[n][:, t * P:(t + 1) * P], kq[:, t, n * HD:(n + 1) * HD], ident[:, :])
                    mm.then_inc(c_t, 1)
                for b in range(NB):
                    pe.wait_ge(b_k[b], 32)
                    if b < 2:
                        pe.wait_ge(c_tc, b + 1)
                    if b >= 2:
                        pe.wait_ge(b_ktc, b - 1)
                    for f in range(2):
                        for n in range(HKV):
                            mm = pe.transpose(S[b % 2][:, (2 * f + n) * P:(2 * f + n + 1) * P], kg[:, b, f, n * HD:(n + 1) * HD], ident[:, :])
                    mm.then_inc(b_kt, 1)
                    if b:
                        row_scores(b - 1)
                row_scores(NB - 1)
                pe.wait_ge(b_sc, 1)
                for f in range(2):
                    pe.transpose(Z[1][0:64, f * P:(f + 1) * P], st_sb[:, f * 64:(f + 1) * 64], ident[:, :])
                pe.wait_ge(b_eq, 3)
                pe.matmul(Z[1][0:64, 256:257], x64, ones[0:1, 0:1], start=True, stop=True).then_inc(b_s2, 1)
                pe.wait_ge(b_p, 1)
                for f in range(2):
                    pe.transpose(TB[:, f * 64:(f + 1) * 64], ssb[:, f * P:(f + 1) * P], ident[0:64, 0:64])
                pe.matmul(TB[:, 128:192], ones[0:64, :], d64, start=True, stop=True).then_inc(b_pt, 1)
                pe.wait_ge(b_p, 2)
                for b in range(NB):
                    pe.wait_ge(b_v[b], 32)
                    for n in range(HKV):
                        for f in range(2):
                            mm = pe.matmul(Z[0][:, b * HB + 4 * n:b * HB + 4 * n + 4], vgt[:, b, f, n * HD:(n + 1) * HD],
                                           ptb[:, f, b * HB + 4 * n:b * HB + 4 * n + 4], start=(f == 0), stop=(f == 1))
                mm.then_inc(b_o, 1)
                pe.wait_ge(b_q, 1)
                pe.transpose(TB[:, 300:428], subw[:, :], ident[:, :])
                pe.matmul(TB[:, 192:256], ones[:, :], sqa, start=True, stop=True).then_inc(b_o, 1)

        end_stage()

        sigb = big[:, 2048:3072].rearrange("p (t d) -> p t d", d=HD)
        rtmp = [big[:, 3072:3328], big[:, 3328:3584]]
        PB = [Z[0], DB]
        oTs = qb
        FB = F(NT) + 2
        h_w = [sem("h_w0"), sem("h_w1")]
        h_wu = [sem("h_wu0"), sem("h_wu1")]
        h_z = [sem("h_z0"), sem("h_z1")]
        h_zf = [sem("h_zf0"), sem("h_zf1")]
        h_rot = sem("h_rot")
        h_s = [sem("h_s0"), sem("h_s1")]
        h_sf = [sem("h_sf0"), sem("h_sf1")]
        h_t, h_tf = sem("h_t"), sem("h_tf")
        h_nm = sem("h_nm")
        h_x = sem("h_x")
        h_pv = sem("h_pv")
        h_o = sem("h_o")
        h_eg = sem("h_eg")
        h_sil = sem("h_sil")
        h_st = sem("h_st")
        h_ch = sem("h_ch")
        h_next = sem("h_next")
        wo = w_out.rearrange("l (k p) n -> p (l k) n", p=P)

        with nc.Block() as block:
            @block.sync
            def _(sp):
                for s in (*h_wu, *h_zf, *h_sf, h_t, h_tf, h_o, h_pv, h_sil, h_st):
                    sp.sem_inc(s, 1)
                for s in range(2):
                    sp.sem_inc(h_z[s], NT // 2)
                    sp.sem_inc(h_zf[s], NT // 2)
                    sp.sem_inc(h_w[s], 32)
                sp.sem_inc(h_wu[0], 1)
                def weights(m, u):
                    sp.wait_ge(h_wu[u], 1 + m)
                    for q, lo in enumerate((QS, GS)):
                        sp.dma_start(W[:, u, :, q * HD:(q + 1) * HD], win[:, :, ds(m * 2 * HD + u * HD + lo, HD)]).then_inc(h_w[u], 16)
                with sp.Fori(1, HB // 2) as m:
                    weights(m, 0)
                    weights(m, 1)
                for u in range(2):
                    sp.wait_ge(h_wu[u], 1 + HB // 2)
                for c in range(2):
                    sp.dma_start(W[:, c, :, :], wo[:, :, c * CW:(c + 1) * CW]).then_inc(h_next, 16)
                for lo, hi in ((0, 4), (4, 8), (8, 12), (12, HA + HB - 1)):
                    if hi > HA:
                        sp.wait_ge(h_st, 1 + 16 * (hi - HA))
                    sp.dma_start(hT[:, lo:hi, :], oT_d[lo:hi, :, :].rearrange("k p t -> p k t")).then_inc(h_next, 16)
                sp.wait_ge(h_next, 16 * 6)

            @block.tensor
            def _(pe):
                def project(m, u, t):
                    H = 2 * m + u
                    if t == 0:
                        pe.wait_ge(h_w[u], 32 * m + 32)
                    pe.wait_ge(h_zf[t % 2], 1 + 4 * H + t // 2)
                    for k in range(KT):
                        mm = pe.matmul(PB[t % 2][:, 0:CW], hT[:, k, t * P:(t + 1) * P], W[:, u, k, :], start=(k == 0), stop=(k == KT - 1))
                    mm.then_inc(h_z[t % 2], 1)
                    if t == NT - 1:
                        pe.wait_ge(h_z[t % 2], 4 * H + 4)
                        pe.nop().then_inc(h_wu[u], 1)

                def queries(m, u):
                    H = 2 * m + u
                    pe.wait_ge(h_rot, H + 1)
                    pe.wait_ge(h_sf[1], 1 + 5 * H)
                    for t in range(NT):
                        mm = pe.transpose(S[1][:, t * P:(t + 1) * P], qk[:, t, u * HD:(u + 1) * HD], ident[:, :])
                    mm.then_inc(h_s[1], 1)

                def scores(m, u, t):
                    H, n = 2 * m + u, (t + 1) * P
                    j = t % 2
                    if t == 0:
                        pe.wait_ge(h_sf[1], 1 + 5 * H + 1)
                    pe.wait_ge(h_sf[j], 1 + (4 * H + t // 2 if j == 0 else 5 * H + 1 + t // 2))
                    for lo, hi in key_spans(t):
                        own = hi == n
                        pe.matmul(S[j][:, lo:hi], qkT[:, u, t * P:n], kTb[:, ds((m // 2) * T + lo, hi - lo)], start=True, stop=False)
                        mm = pe.matmul(S[j][:, lo:hi], identb[:, :], bias[:, t * BS + lo:t * BS + hi], start=False, stop=not own)
                        if own:
                            mm = pe.matmul(S[j][:, lo:hi], identb[:, :], causal[:, :], start=False, stop=True)
                    mm.then_inc(h_s[j], 1)

                def head(m, u, last):
                    H = 2 * m + u
                    m1, u1 = (m, 1) if u == 0 else (m + 1, 0)

                    def turned(src, f, n):
                        for b in range(n):
                            mm = pe.transpose(TB[:, b * P:(b + 1) * P], src(4 * f + b), ident[:, :])
                        mm.then_inc(h_t, 1)

                    for t in range(NT):
                        pe.wait_ge(h_x, NT * H + t + 1)
                        for f in range(F(t + 1) - F(t)):
                            pe.wait_ge(h_tf, 1 + FB * H + F(t) + f)
                            turned(lambda b: e12[:, t % 2, b * P:(b + 1) * P], f, min(4, t + 1 - 4 * f))
                            if f == 0 and t + 1 < NT:
                                scores(m, u, t + 1)
                        if not last:
                            project(m1, u1, t)
                        pe.wait_ge(h_tf, 1 + FB * H + F(t + 1))
                        pe.wait_ge(h_o, 1 + NT * H + t)
                        for b in range(t + 1):
                            mm = pe.matmul(Z[1][:, 0:HD], pT[:, b, :], vb[:, b, ds((m // 2) * HD, HD)], start=(b == 0), stop=(b == t))
                        mm.then_inc(h_pv, 1)
                    pe.wait_ge(h_o, 1 + NT * H + NT)
                    turned(lambda b: vg[:, u, b, :], 0, 4)
                    if not last:
                        queries(m1, u1)
                    pe.wait_ge(h_tf, 1 + FB * H + F(NT) + 1)
                    turned(lambda b: vg[:, u, b, :], 1, 4)
                    if not last:
                        scores(m1, u1, 0)

                queries(0, 0)
                scores(0, 0, 0)
                with pe.Fori(0, HB // 2 - 1) as m:
                    head(m, 0, False)
                    head(m, 1, False)
                head(HB // 2 - 1, 0, False)
                head(HB // 2 - 1, 1, True)

            @block.scalar
            def _(act):
                def take(m, u, t):
                    act.wait_ge(h_z[t % 2], 4 * (2 * m + u) + t // 2 + 1)
                    act.activation(qk[:, t, u * HD:(u + 1) * HD], PB[t % 2][:, 0:HD], ACT.Copy)
                    act.activation(vg[:, u, t, :], PB[t % 2][:, HD:CW], ACT.Copy).then_inc(h_zf[t % 2], 1)

                def ready(m, u):
                    H = 2 * m + u
                    for b in range(2):
                        act.wait_ge(h_zf[b], 1 + 4 * H + 4)
                    act.wait_ge(h_sil, 1 + H)
                    act.activation(sigb, vg[:, u, :, :], ACT.Sigmoid).then_inc(h_eg, 1)
                    act.wait_ge(h_s[1], 5 * H + 1)
                    act.activation(qkT[:, u, :], S[1][:, :], ACT.Copy).then_inc(h_sf[1], 1)

                def exps(H, t):
                    n, j = (t + 1) * P, t % 2
                    act.wait_ge(h_nm, NT * H + t + 1)
                    act.wait_ge(h_t, 1 + FB * H + (F(t - 1) if t else 0))
                    act.activation(e12[:, j, 0:n], S[j][:, 0:n], ACT.Exp, scale=SC_B, bias=nmx[:, t, 0:1],
                                   accum_out=rsum[:, t, 0:1]).then_inc(h_x, 1)
                    act.wait_ge(h_x, NT * H + t + 1)
                    act.nop().then_inc(h_sf[j], 1)

                def head(m, u, last):
                    H = 2 * m + u
                    m1, u1 = (m, 1) if u == 0 else (m + 1, 0)
                    for t in range(NT):
                        for f in range(F(t + 1) - F(t)):
                            act.wait_ge(h_t, 1 + FB * H + F(t) + f + 1)
                            if f == 0:
                                act.wait_ge(h_pv, 1 + NT * H + t)
                            nb = min(4, t + 1 - 4 * f)
                            act.activation(pTf[:, 512 * f:512 * f + nb * P], TB[:, 0:nb * P], ACT.Copy).then_inc(h_tf, 1)
                        if t + 1 < NT:
                            exps(H, t + 1)
                        if not last:
                            take(m1, u1, t)
                    act.wait_ge(h_st, 1 + 16 * H)
                    act.wait_ge(h_t, 1 + FB * H + F(NT) + 1)
                    act.activation(oTs[:, 0:512], TB[:, :], ACT.Copy).then_inc(h_tf, 1)
                    if not last:
                        ready(m1, u1)
                    act.wait_ge(h_t, 1 + FB * H + F(NT) + 2)
                    act.activation(oTs[:, 512:1024], TB[:, :], ACT.Copy).then_inc(h_tf, 1)
                    if not last:
                        exps(H + 1, 0)
                    act.wait_ge(h_tf, 1 + FB * H + FB)
                    act.dma_start(oT_d[ds(H + HA, 1) if not isinstance(H, int) else slice(H + HA, H + HA + 1), :, :].rearrange("o p t -> (o p) t"),
                                  oTs[:, :]).then_inc(h_st, 16)

                ready(0, 0)
                exps(0, 0)
                with act.Fori(0, HB // 2 - 1) as m:
                    head(m, 0, False)
                    head(m, 1, False)
                head(HB // 2 - 1, 0, False)
                head(HB // 2 - 1, 1, True)
                act.wait_ge(h_st, 1 + 16 * HB)

            @block.vector
            def _(dve):
                def rotate(link, m, u):
                    H = 2 * m + u
                    for b in range(2):
                        dve.wait_ge(h_zf[b], 1 + 4 * H + 4)
                    rope(link, qk[:, :, u * HD:(u + 1) * HD], tuple(ropb[:, :, a, :] for a in (0, 1)),
                         *[a.rearrange("p (t r) -> p t r", r=32) for a in rtmp], 32)
                    dve.nop().then_inc(h_rot, 1)

                def maximum(link, m, u, t):
                    H, j = 2 * m + u, t % 2
                    dve.wait_ge(h_s[j], (4 * H + t // 2 + 1) if j == 0 else (5 * H + 2 + t // 2))
                    link(dve.tensor_reduce(mx[:, t, 0:1], S[j][:, 0:(t + 1) * P], AX.X, ALU.max))
                    dve.tensor_scalar(nmx[:, t, 0:1], mx[:, t, 0:1], -SC_B, None, ALU.mult).then_inc(h_nm, 1)

                def head(m, u, last):
                    H = 2 * m + u
                    m1, u1 = (m, 1) if u == 0 else (m + 1, 0)
                    link = Chain(dve, h_ch, clear=True)
                    g = vg[:, u, :, :]
                    maximum(link, m, u, 0)
                    dve.wait_ge(h_eg, H + 1)
                    link(dve.tensor_tensor(g, g, sigb, ALU.mult))
                    dve.nop().then_inc(h_sil, 1)
                    for t in range(NT):
                        dve.wait_ge(h_x, NT * H + t + 1)
                        link(dve.reciprocal(rrec[:, t, 0:1], rsum[:, t, 0:1]))
                        if t + 1 < NT:
                            maximum(link, m, u, t + 1)
                        elif not last:
                            rotate(link, m1, u1)
                        dve.wait_ge(h_pv, 1 + NT * H + t + 1)
                        dve.scalar_tensor_tensor(out=g[:, t, :], in0=Z[1][:, 0:HD], scalar=rrec[:, t, 0:1], in1=g[:, t, :],
                                                 op0=ALU.mult, op1=ALU.mult).then_inc(h_o, 1)

                link = Chain(dve, h_ch)
                rotate(link, 0, 0)
                with dve.Fori(0, HB // 2 - 1) as m:
                    head(m, 0, False)
                    head(m, 1, False)
                head(HB // 2 - 1, 0, False)
                head(HB // 2 - 1, 1, True)

        end_stage()

        NCO = D // CW
        biasf = bias[:, :].bitcast(F32)
        bf, qkf, vgf = big, qk[:, :, :].rearrange("p a b -> p (a b)"), vg[:, :, :, :].rearrange("p a b c -> p (a b c)")
        qkTf, e12f = qkT[:, :, :].rearrange("p a b -> p (a b)"), e12[:, :, :].rearrange("p a b -> p (a b)")
        wide_t = [bf[:, 0:2048], bf[:, 2048:4096], bf[:, 4096:6144], qkf, vgf, qkTf, e12f, biasf[:, 0:2048]]
        rows = lambda t: P if t < NT else NB

        def ohalf(t, hh):
            if t < NT:
                return wide_t[t][:, 1024 * hh:1024 * hh + 1024]
            return (qb[0:NB, :], vnew[0:NB, :])[hh]

        ochunk = lambda t, c: ohalf(t, c // 4)[:, (c % 4) * CW:(c % 4) * CW + CW]
        vec = [bf[:, 6144:7168], biasf[:, 2048:3072]]
        xst = [pTf, kiT[:, :]]
        wpe = [sc[:, :, :].rearrange("p a b -> p (a b)")[:, 0:512].rearrange("p (k n) -> p k n", k=2),
               ex[:, :, :].rearrange("p a b -> p (a b)")[:, 0:512].rearrange("p (k n) -> p k n", k=2)]
        kibf = kib[:, :, :, :].rearrange("p a b c -> p (a b c)")
        sg = [kibf[:, 0:256], kibf[:, 256:512]]
        part = [qib[:, :, :].rearrange("p a b -> p (a b)"), qit[:, :, :].rearrange("p a b -> p (a b)")]
        pin = wide_t[NT - 1].rearrange("p (t c) -> p t c", c=2 * P)
        pins = biasf[0:NB, 3072:3328]
        xin = [Wf[:, 1024 * q:1024 * q + 1024] for q in range(4)]
        psT = small[:, 160:176].rearrange("p (k b) -> p k b", k=2)
        ss4 = small[:, 224:260].rearrange("p (t j) -> p t j", j=4)
        rs9 = small[:, 212:221]
        wg, wp = (a.rearrange("l (k p) n -> p (l k) n", p=P) for a in (w_pg, w_pe))
        pp = p_prompt.rearrange("l b (t p) d -> p (l b t) d", p=P)
        ps = p_sample.rearrange("l b s d -> (l b s) d")
        yp = y_prompt.rearrange("b (t p) d -> p (b t) d", p=P)
        ys = y_sample.rearrange("b s d -> (b s) d")

        o_h = sem("o_h")
        o_w = [sem("o_w0"), sem("o_w1")]
        o_wu = [sem("o_wu0"), sem("o_wu1")]
        o_z = [sem("o_z0"), sem("o_z1")]
        o_zf = [sem("o_zf0"), sem("o_zf1")]
        o_pz, o_pc, o_ps, o_pf = sem("o_pz"), sem("o_pc"), sem("o_ps"), sem("o_pf")
        o_vec = sem("o_vec")
        o_vec2 = sem("o_vec2")
        o_x = [sem(f"o_x{q}") for q in range(4)]
        o_xu = [sem("o_xu0"), sem("o_xu1")]
        o_ch, o_ach = sem("o_ch"), sem("o_ach")
        o_rsq = sem("o_rsq")
        o_rs = sem("o_rs")
        o_xm = sem("o_xm")
        o_t, o_tf = sem("o_t"), sem("o_tf")
        o_p = sem("o_p")
        o_pt, o_ptf = sem("o_pt"), sem("o_ptf")
        e_w = [sem("e_w0"), sem("e_w1")]
        e_wu = [sem("e_wu0"), sem("e_wu1")]
        e_z = [sem("e_z0"), sem("e_z1")]
        e_a = sem("e_a")
        e_s = sem("e_s")
        e_f = [sem("e_f0"), sem("e_f1")]
        e_st = sem("e_st")

        with nc.Block() as block:
            @block.sync
            def _(sp):
                for s in (*o_zf, o_pc, o_pf, *e_wu, *e_f):
                    sp.sem_inc(s, 1)
                sp.dma_start(hT[:, HA + HB - 1, :], oT_d[HA + HB - 1, :, :]).then_inc(o_h, 16)
                sp.dma_start(pin, pp).then_inc(o_p, 16)
                sp.dma_start(pins, ps).then_inc(o_p, 16)
                for c in range(2):
                    sp.sem_inc(o_w[c], 16)
                for hh in range(2):
                    sp.dma_start(vec[hh], post_w[0:1, 1024 * hh:1024 * hh + 1024].broadcast_to([P, 1024])).then_inc(o_vec, 16)
                with sp.Fori(1, NCO // 2) as i:
                    for s in range(2):
                        sp.wait_ge(o_wu[s], i)
                        sp.dma_start(W[:, s, :, :], wo[:, :, ds(i * 2 * CW + s * CW, CW)]).then_inc(o_w[s], 16)
                sp.wait_ge(o_wu[0], NCO // 2)
                for t in range(NT + 1):
                    for hh in range(2):
                        if t >= 2:
                            sp.wait_ge(o_xu[hh], t - 1)
                        src = xp[:, t, 1024 * hh:1024 * hh + 1024] if t < NT else xs[:, 1024 * hh:1024 * hh + 1024]
                        sp.dma_start(xin[2 * (t % 2) + hh][0:rows(t), :], src).then_inc(o_x[2 * (t % 2) + hh], 16)

                def gate_weights(i, s):
                    sp.dma_start(W[:, 1 - s, :, :], wg[:, :, ds(i * 2 * CW + s * CW, CW)]).then_inc(e_w[s], 16)
                    sp.dma_start(wpe[s], wp[:, :, ds(i * 2 * CW + s * CW, CW)]).then_inc(e_w[s], 16)

                sp.wait_ge(o_wu[1], NCO // 2)
                gate_weights(0, 0)
                for hh in range(2):
                    sp.wait_ge(o_xu[hh], NT + 1)
                    sp.dma_start(vec[hh], b_pg[0:1, 1024 * hh:1024 * hh + 1024].broadcast_to([P, 1024])).then_inc(o_vec2, 16)
                gate_weights(0, 1)
                with sp.Fori(1, NCO // 2) as i:
                    for s in range(2):
                        sp.wait_ge(e_wu[s], 1 + i)
                        gate_weights(i, s)
                for t in range(NT + 1):
                    sp.wait_ge(e_f[(7 * 9 + t) % 2], 1 + (7 * 9 + t) // 2 + 1)
                    for hh in range(2):
                        dst = yp[:, t, 1024 * hh:1024 * hh + 1024] if t < NT else ys[:, 1024 * hh:1024 * hh + 1024]
                        sp.dma_start(dst, ohalf(t, hh)).then_inc(e_st, 16)
                sp.wait_ge(e_st, 32 * (NT + 1))

            @block.tensor
            def _(pe):
                def tile(i, s, t):
                    pe.wait_ge(o_zf[t % 2], 1 + 8 * i + 4 * s + t // 2)
                    for k in range(KT):
                        mm = pe.matmul(Z[t % 2][:, 0:CW], hT[:, k, t * P:(t + 1) * P], W[:, s, k, :], start=(k == 0), stop=(k == KT - 1))
                    mm.then_inc(o_z[t % 2], 1)

                def sample(i, s):
                    pe.wait_ge(o_pc, 1 + 2 * i + s)
                    for k in range(KT):
                        g = k % 4
                        mm = pe.matmul(TB[32 * g:32 * g + 32, 0:CW], odec[:, k, :], W[:, s, k, :], start=(k < 4), stop=(k >= KT - 4))
                    mm.then_inc(o_pz, 1)
                    pe.wait_ge(o_pz, 2 * i + s + 1)
                    pe.nop().then_inc(o_wu[s], 1)
                    pe.wait_ge(o_pc, 1 + 2 * i + s + 1)
                    pe.wait_ge(o_pf, 1 + 2 * i + s)
                    pe.matmul(DB[0:NB, 0:CW], sel, part[0], start=True, stop=True).then_inc(o_ps, 1)

                def chunk(i, s):
                    pe.wait_ge(o_w[s], 16 * i + 16)
                    for t in range(NT):
                        tile(i, s, t)
                    sample(i, s)

                def turn(t):
                    r = rows(t)
                    for hh in range(2):
                        pe.wait_ge(o_xm, 2 * t + hh + 1)
                        if t:
                            pe.wait_ge(o_tf, 2 * (t - 1) + hh + 1)
                        for k in range(8):
                            mm = pe.transpose(S[hh][:, k * P:k * P + r], ohalf(t, hh)[:, k * P:(k + 1) * P], ident[0:r, 0:r])
                        mm.then_inc(o_t, 1)

                pe.wait_ge(o_p, 32)
                for k in range(2):
                    for t in range(NT):
                        mm = pe.transpose(S[k][:, t * P:(t + 1) * P], pin[:, t, k * P:(k + 1) * P], ident[:, :])
                    mm.then_inc(o_pt, 1)
                for k in range(2):
                    mm = pe.transpose(TB[:, k * P:k * P + NB], pins[:, k * P:(k + 1) * P], ident[0:NB, 0:NB])
                mm.then_inc(o_pt, 1)
                pe.wait_ge(o_h, 16)
                pe.wait_ge(o_ptf, 3)
                with pe.Fori(0, NCO // 2 - 1) as i:
                    chunk(i, 0)
                    chunk(i, 1)
                chunk(NCO // 2 - 1, 0)
                pe.wait_ge(o_w[1], 16 * (NCO // 2))
                for t in range(NT):
                    tile(NCO // 2 - 1, 1, t)
                    if t >= 2:
                        turn(t - 2)
                sample(NCO // 2 - 1, 1)
                for t in range(NT - 2, NT + 1):
                    turn(t)
                pe.wait_ge(o_tf, 2 * (NT + 1))

                def gate(i, s):
                    pe.wait_ge(e_w[s], 32 * i + 32)
                    for t in range(NT + 1):
                        v = 9 * s + t
                        b = v % 2
                        pe.wait_ge(e_f[b], 1 + 9 * i + v // 2)
                        if t < NT:
                            for k in range(KT):
                                pe.matmul(Z[b][:, 0:CW], hT[:, k, t * P:(t + 1) * P], W[:, 1 - s, k, :], start=(k == 0), stop=(k == KT - 1))
                        else:
                            pe.wait_ge(o_pc, 1 + NCO + 2 * i + s)
                            for k in range(KT):
                                g = k % 4
                                mm = pe.matmul(S[0][32 * g:32 * g + 32, 0:CW], odec[:, k, :], W[:, 1 - s, k, :], start=(k < 4), stop=(k >= KT - 4))
                            mm.then_inc(o_pz, 1)
                            pe.wait_ge(o_pc, 1 + NCO + 2 * i + s + 1)
                            pe.matmul(Z[b][0:NB, 0:CW], sel, part[0], start=True, stop=True)
                        for k in range(2):
                            lhs = xst[k][:, t * P:(t + 1) * P] if t < NT else psT[:, k, :]
                            mm = pe.matmul((TB, DB)[b][0:rows(t), 0:CW], lhs, wpe[s][:, k, :], start=(k == 0), stop=(k == 1))
                        mm.then_inc(e_z[b], 1)
                    pe.wait_ge(e_z[b], 9 * i + (9 * s + NT) // 2 + 1)
                    pe.nop().then_inc(e_wu[s], 1)

                with pe.Fori(0, NCO // 2) as i:
                    gate(i, 0)
                    gate(i, 1)

            @block.scalar
            def _(act):
                def take(t, c):
                    act.wait_ge(o_z[t % 2], 4 * c + t // 2 + 1)
                    act.activation(ochunk(t, c), Z[t % 2][:, 0:CW], ACT.Copy).then_inc(o_zf[t % 2], 1)

                def sample(c):
                    act.wait_ge(o_pz, c + 1)
                    if c:
                        act.wait_ge(o_ps, c)
                    act.activation(part[0], TB[:, 0:CW], ACT.Copy).then_inc(o_pc, 1)
                    act.wait_ge(o_ps, c + 1)
                    act.activation(ochunk(NT, c), DB[0:NB, 0:CW], ACT.Copy).then_inc(o_pf, 1)

                def squares(t):
                    r = rows(t)
                    for q in range(4):
                        if t or q:
                            act.wait_ge(o_ach, 4 * t + q)
                        act.activation(kibf[0:r, :], ohalf(t, q // 2)[:, (q % 2) * 512:(q % 2) * 512 + 512], ACT.Square,
                                       accum_out=ss4[0:r, t, q:q + 1]).then_inc(o_ach, 1)

                def root(t):
                    r = rows(t)
                    act.wait_ge(o_rsq, t + 1)
                    act.activation(rs9[0:r, t:t + 1], rs9[0:r, t:t + 1], ACT.Sqrt, scale=1.0 / D, bias=eps[0:r, :]).then_inc(o_rs, 1)

                def turn(t):
                    for hh in range(2):
                        act.wait_ge(o_t, 2 * t + hh + 1)
                        src = S[hh][:, :].rearrange("p (k n) -> p k n", n=P)
                        if t < NT:
                            act.activation(hT[:, 8 * hh:8 * hh + 8, t * P:(t + 1) * P], src, ACT.Copy).then_inc(o_tf, 1)
                        else:
                            act.activation(odec[:, 8 * hh:8 * hh + 8, 0:NB], src[:, :, 0:NB], ACT.Copy).then_inc(o_tf, 1)

                for k in range(2):
                    act.wait_ge(o_pt, k + 1)
                    act.activation(xst[k], S[k][:, :], ACT.Copy).then_inc(o_ptf, 1)
                act.wait_ge(o_pt, 3)
                act.activation(psT[:, :, :], TB[:, 0:2 * P].rearrange("p (k n) -> p k n", k=2)[:, :, 0:NB], ACT.Copy).then_inc(o_ptf, 1)
                for c in range(NCO - 1):
                    for t in range(NT):
                        take(t, c)
                    sample(c)
                for t in range(NT):
                    take(t, NCO - 1)
                    if t:
                        root(t - 1)
                    act.wait_ge(o_zf[t % 2], 1 + 4 * (NCO - 1) + t // 2 + 1)
                    squares(t)
                    if t >= 2:
                        turn(t - 2)
                root(NT - 1)
                sample(NCO - 1)
                act.wait_ge(o_pf, 1 + NCO)
                squares(NT)
                turn(NT - 2)
                root(NT)
                turn(NT - 1)
                turn(NT)
                with act.Fori(0, NCO // 2) as i:
                    for s in range(2):
                        for t in range(NT + 1):
                            v = 9 * s + t
                            if t == NT:
                                act.wait_ge(o_pz, NCO + 2 * i + s + 1)
                                act.activation(part[0], S[0][:, 0:CW], ACT.Copy).then_inc(o_pc, 1)
                            act.wait_ge(e_a, 18 * i + v + 1)
                            act.activation(sg[v % 2][0:rows(t), :], sg[v % 2][0:rows(t), :], ACT.Sigmoid).then_inc(e_s, 1)

            @block.vector
            def _(dve):
                link = Chain(dve, o_ch)
                dve.wait_ge(o_vec, 32)
                for t in range(NT + 1):
                    r = rows(t)
                    dve.wait_ge(o_ach, 4 * t + 4)
                    dve.tensor_reduce(rs9[0:r, t:t + 1], ss4[0:r, t, :], AX.X, ALU.add).then_inc(o_rsq, 1)
                    dve.wait_ge(o_rs, t + 1)
                    link(dve.reciprocal(rs9[0:r, t:t + 1], rs9[0:r, t:t + 1]))
                    for hh in range(2):
                        link(dve.scalar_tensor_tensor(out=ohalf(t, hh), in0=ohalf(t, hh), scalar=rs9[0:r, t:t + 1], in1=vec[hh][0:r, :],
                                                      op0=ALU.mult, op1=ALU.mult))
                        dve.wait_ge(o_x[2 * (t % 2) + hh], 16 * (t // 2 + 1))
                        link(dve.tensor_tensor(ohalf(t, hh), ohalf(t, hh), xin[2 * (t % 2) + hh][0:r, :], ALU.add))
                        dve.nop().then_inc(o_xu[hh], 1)
                        dve.nop().then_inc(o_xm, 1)
                dve.wait_ge(o_vec2, 32)
                for c in range(NCO):
                    for t in range(NT + 1):
                        u, r = 9 * c + t, rows(t)
                        b = u % 2
                        dve.wait_ge(e_z[b], u // 2 + 1)
                        if u >= 2:
                            dve.wait_ge(e_f[b], 1 + u // 2)
                        dve.tensor_tensor(sg[b][0:r, :], Z[b][0:r, 0:CW], vec[c // 4][0:r, (c % 4) * CW:(c % 4) * CW + CW], ALU.add).then_inc(e_a, 1)
                        dve.wait_ge(e_s, u + 1)
                        link(dve.tensor_tensor(sg[b][0:r, :], sg[b][0:r, :], (TB, DB)[b][0:r, 0:CW], ALU.mult))
                        dve.tensor_tensor(ochunk(t, c), ochunk(t, c), sg[b][0:r, :], ALU.add).then_inc(e_f[b], 1)


_INS = ["x_prompt", "x_sample", "p_prompt", "p_sample", "cache_diff_k", "cache_diff_v", "cache_dsa_k", "cache_dsa_v",
        "cache_idx_k", "page_table", "pre_norm_w", "post_norm_w", "w_in", "lam_q1", "lam_k1", "lam_q2", "lam_k2",
        "diff_norm_w", "w_out", "w_ple_gate", "b_ple_gate", "w_ple_proj"]
_OUTS = [(1, 1024, 2048), (8, 1, 2048), (1, 1, 1024, 8, 128), (1, 1, 1024, 8, 128), (1, 1, 1024, 2, 128),
         (1, 1, 1024, 2, 128), (1, 1, 1024, 64), (1, 8, 1, 8, 128), (1, 8, 1, 8, 128), (1, 8, 1, 2, 128),
         (1, 8, 1, 2, 128), (1, 8, 1, 64)]


def rope_table(first, n, d):
    r = d // 4
    half = r // 2
    inv = (np.float32(500000.0) ** (np.float32(-2.0 / r) * np.arange(half, dtype=np.float32))).astype(np.float32)
    ang = (np.arange(first, first + n, dtype=np.float32)[:, None] * inv[None, :]).astype(np.float32)
    c, s = np.cos(ang), np.sin(ang)
    return np.ascontiguousarray(np.stack([np.concatenate([c, c], -1), np.concatenate([s, s], -1)], 1).astype(np.float32))


def kernel(**inputs):
    import numpy as _np
    import concourse.bacc as _bacc
    from concourse import mybir as _mybir
    from concourse.bass_utils import run_bass_kernel_spmd as _run

    nc = _bacc.Bacc("TRN2", target_bir_lowering=False, num_devices=1)
    arrays, args = {}, []

    def give(name, a):
        a = _np.ascontiguousarray(a)
        arrays[name] = a
        args.append(nc.dram_tensor(name, a.shape, _mybir.dt.from_np(a.dtype), kind="ExternalInput").ap())

    for name in _INS:
        give(f"in_{name}_dram", inputs[name])
    give("rope_a", rope_table(0, T, DI))
    give("rope_b", rope_table(0, T, HD))
    give("rope_new", _np.concatenate([rope_table(PAST, 1, DI), rope_table(PAST, 1, HD)], -1).reshape(2, 48))
    for i, shape in enumerate(_OUTS):
        args.append(nc.dram_tensor(f"out_{i}_dram", shape, _mybir.dt.float32, kind="ExternalOutput").ap())
    hymba_step(nc, *args)
    r = _run(nc, [arrays], core_ids=[0])
    return tuple(r.results[0][f"out_{i}_dram"] for i in range(len(_OUTS)))
```
